# Optimizing a Trainium2 kernel written in Bass

```python
import math
import jax, jax.numpy as jnp
from jax import lax
import numpy as np

D_MODEL = 1024
BATCH = 1
SEQ = 256
DEPTH = 2

GRID_W = 64
CTX_LEN = 256
N_GROUPS = 4
GROUP_W = D_MODEL // N_GROUPS
HEADS = 4
HEAD_DIM = GROUP_W // HEADS
CHUNK = 128
DIFF_QK = HEAD_DIM // 2
ROT_HALF = DIFF_QK // 2
ROPE_THETA = 10000.0
Q_BLOCK = 128
D_FF = 2816
EPS = 1e-6
G_AU, G_AV, G_BX, G_BB, G_BC, G_CF, G_DQ, G_DK, G_DV = range(9)
IN_COLS = 9 * GROUP_W
KV_COL0 = G_DK * GROUP_W


def rmsnorm(x, g=None):
    xf = x.astype(jnp.float32)
    y = xf * lax.rsqrt(jnp.mean(xf * xf, axis=-1, keepdims=True) + EPS)
    if g is not None:
        y = y * g.astype(jnp.float32)
    return y.astype(x.dtype)

def adaln_params(cvec, w_ada, b_ada):
    m = jax.nn.silu(cvec) @ w_ada + b_ada
    return jnp.split(m, 6, axis=-1)

def modulate(h, shift, scale):
    return h * (1 + scale) + shift

def group(z, i):
    return z[..., i * GROUP_W:(i + 1) * GROUP_W]

def dwconv3(x, w):
    xp = jnp.pad(x, ((0, 0), (1, 1), (0, 0)))
    return xp[:, :-2] * w[0] + xp[:, 1:-1] * w[1] + xp[:, 2:] * w[2]

def mixer_a(z, ws, bs):
    B, N, _ = z.shape
    u = jax.nn.gelu(group(z, G_AU))
    v = rmsnorm(jax.nn.gelu(group(z, G_AV)).reshape(B, N, HEADS, HEAD_DIM))
    v = v.reshape(B, N // CHUNK, CHUNK, HEADS, HEAD_DIM)
    mixed = jnp.einsum('hpq,bcqhd->bcphd', ws, v) + bs.T[:, :, None]
    return u * mixed.reshape(B, N, GROUP_W)

def mixer_b(z, w):
    return group(z, G_BB) * dwconv3(group(z, G_BC) * group(z, G_BX), w)

def mixer_c(z):
    B, N, _ = z.shape
    f = group(z, G_CF).reshape(B, N, HEADS, HEAD_DIM).astype(jnp.float32)
    F = jnp.fft.fft2(f, axes=(1, 3), norm='ortho').real
    return F.astype(z.dtype).reshape(B, N, GROUP_W)

def apply_rope_2d(t, ang_r, ang_c):
    def rot(u, ang):
        cos = jnp.cos(ang)[None, :, None, None, :].astype(u.dtype)
        sin = jnp.sin(ang)[None, :, None, None, :].astype(u.dtype)
        u1, u2 = u[..., :ROT_HALF // 2], u[..., ROT_HALF // 2:]
        return jnp.concatenate([u1 * cos - u2 * sin, u2 * cos + u1 * sin], axis=-1)
    return jnp.concatenate([rot(t[..., :ROT_HALF], ang_r), rot(t[..., ROT_HALF:], ang_c)], axis=-1)

def diff_attend(q, k, v, lam):
    s = jnp.einsum('bqhmd,bkhmd->bhmqk', q, k).astype(jnp.float32) * (DIFF_QK ** -0.5)
    p = jax.nn.softmax(s, axis=-1)
    a = p[:, :, 0] - lam * p[:, :, 1]
    return jnp.einsum('bhqk,bkhd->bqhd', a.astype(v.dtype), v)

def diff_out(o, g, lam_init):
    B, N = o.shape[0], o.shape[1]
    return (rmsnorm(o, g) * (1 - lam_init)).reshape(B, N, GROUP_W)

def conv_ffn(h, w_up, conv_w, w_down):
    up = h @ w_up
    a, b = up[..., :D_FF], up[..., D_FF:]
    return (jax.nn.silu(dwconv3(a, conv_w)) * b) @ w_down

def trunk_layer(x, xc, c, c_ctx, ang_r, ang_c, layer_idx, ctx_out,
                w_ada, b_ada, g1, g2, w_in, gm_ws, gm_bs, sc_w,
                lq1, lk1, lq2, lk2, subln_g, w_out, w_up, ffn_conv, w_down):
    B, N, _ = x.shape
    L = xc.shape[1]
    sh1, sc1, gt1, sh2, sc2, gt2 = [m[:, None, :] for m in adaln_params(c, w_ada, b_ada)]
    shc1, scc1, gtc1, shc2, scc2, gtc2 = adaln_params(c_ctx, w_ada, b_ada)
    lam_init = 0.8 - 0.6 * math.exp(-0.3 * layer_idx)
    f32 = jnp.float32
    lam = (jnp.exp(jnp.sum(lq1.astype(f32) * lk1.astype(f32)))
           - jnp.exp(jnp.sum(lq2.astype(f32) * lk2.astype(f32))) + lam_init)

    h = modulate(rmsnorm(x, g1), sh1, sc1)
    hc = modulate(rmsnorm(xc, g1), shc1, scc1)
    z = h @ w_in
    zc_kv = hc @ w_in[:, KV_COL0:]
    kc = zc_kv[..., :GROUP_W].reshape(B, L, HEADS, 2, DIFF_QK)
    vc = zc_kv[..., GROUP_W:].reshape(B, L, HEADS, HEAD_DIM)

    q = apply_rope_2d(group(z, G_DQ).reshape(B, N, HEADS, 2, DIFF_QK), ang_r, ang_c)
    k = apply_rope_2d(group(z, G_DK).reshape(B, N, HEADS, 2, DIFF_QK), ang_r, ang_c)
    v = group(z, G_DV).reshape(B, N, HEADS, HEAD_DIM)
    k_all = jnp.concatenate([kc, k], axis=1)
    v_all = jnp.concatenate([vc, v], axis=1)
    qb = q.reshape(B, N // Q_BLOCK, Q_BLOCK, HEADS, 2, DIFF_QK).swapaxes(0, 1)
    o = lax.map(lambda qi: diff_attend(qi, k_all, v_all, lam), qb)
    o = o.swapaxes(0, 1).reshape(B, N, HEADS, HEAD_DIM)

    mix = jnp.concatenate([mixer_a(z, gm_ws, gm_bs), mixer_b(z, sc_w), mixer_c(z),
                           diff_out(o, subln_g, lam_init)], axis=-1)
    x = x + gt1 * (mix @ w_out)
    x = x + gt2 * conv_ffn(modulate(rmsnorm(x, g2), sh2, sc2), w_up, ffn_conv, w_down)
    if not ctx_out:
        return x, None

    zc = hc @ w_in[:, :KV_COL0]
    qc = group(zc, G_DQ).reshape(B, L, HEADS, 2, DIFF_QK)
    oc = diff_attend(qc, kc, vc, lam)
    mixc = jnp.concatenate([mixer_a(zc, gm_ws, gm_bs), mixer_b(zc, sc_w), mixer_c(zc),
                            diff_out(oc, subln_g, lam_init)], axis=-1)
    xc = xc + gtc1 * (mixc @ w_out)
    xc = xc + gtc2 * conv_ffn(modulate(rmsnorm(xc, g2), shc2, scc2), w_up, ffn_conv, w_down)
    return x, xc

def first_inputs(seed: int = 0) -> dict:
    key = jax.random.key(seed)
    ks = jax.random.split(key, 24)
    D = D_MODEL

    def nrm(k, shape, scale):
        return jax.random.normal(k, shape, jnp.float32) * scale

    return {
        'x': nrm(ks[0], (BATCH, SEQ, D), 1.0),
        'c': nrm(ks[1], (BATCH, D), 1.0),
        'ctx': nrm(ks[2], (BATCH, CTX_LEN, D), 1.0),
        'c_ctx': nrm(ks[3], (D,), 1.0),
        'w_ada': nrm(ks[4], (DEPTH, D, 6 * D), 0.5 * D ** -0.5),
        'b_ada': nrm(ks[5], (DEPTH, 6 * D), 0.02),
        'norm1_g': 1.0 + nrm(ks[6], (DEPTH, D), 0.02),
        'norm2_g': 1.0 + nrm(ks[7], (DEPTH, D), 0.02),
        'w_in': nrm(ks[8], (DEPTH, D, IN_COLS), D ** -0.5),
        'gmlp_ws': nrm(ks[9], (DEPTH, HEADS, CHUNK, CHUNK), CHUNK ** -0.5),
        'gmlp_bs': 1.0 + nrm(ks[10], (DEPTH, HEADS, CHUNK), 0.02),
        'sconv_w': nrm(ks[11], (DEPTH, 3, GROUP_W), 3 ** -0.5),
        'lambda_q1': nrm(ks[12], (DEPTH, DIFF_QK), 0.1),
        'lambda_k1': nrm(ks[13], (DEPTH, DIFF_QK), 0.1),
        'lambda_q2': nrm(ks[14], (DEPTH, DIFF_QK), 0.1),
        'lambda_k2': nrm(ks[15], (DEPTH, DIFF_QK), 0.1),
        'subln_g': 1.0 + nrm(ks[16], (DEPTH, HEAD_DIM), 0.02),
        'w_out': nrm(ks[17], (DEPTH, D, D), D ** -0.5),
        'ffn_w_up': nrm(ks[18], (DEPTH, D, 2 * D_FF), D ** -0.5),
        'ffn_conv_w': nrm(ks[19], (DEPTH, 3, D_FF), 3 ** -0.5),
        'ffn_w_down': nrm(ks[20], (DEPTH, D_FF, D), D_FF ** -0.5),
        'final_g': 1.0 + nrm(ks[21], (D,), 0.02),
    }

def first_block(x, c, ctx, c_ctx, w_ada, b_ada, norm1_g, norm2_g, w_in, gmlp_ws, gmlp_bs,
              sconv_w, lambda_q1, lambda_k1, lambda_q2, lambda_k2, subln_g, w_out,
              ffn_w_up, ffn_conv_w, ffn_w_down, final_g):
    N = x.shape[1]
    ROWS = N // GRID_W
    row = jnp.broadcast_to(jnp.arange(ROWS, dtype=jnp.float32)[:, None], (ROWS, GRID_W)).reshape(-1)
    col = jnp.broadcast_to(jnp.arange(GRID_W, dtype=jnp.float32)[None, :], (ROWS, GRID_W)).reshape(-1)
    inv_freq = ROPE_THETA ** (-jnp.arange(0, ROT_HALF, 2, dtype=jnp.float32) / ROT_HALF)
    ang_r = row[:, None] * inv_freq
    ang_c = col[:, None] * inv_freq
    xc = ctx
    for l in range(DEPTH):
        x, xc = trunk_layer(
            x, xc, c, c_ctx, ang_r, ang_c, l, l < DEPTH - 1,
            w_ada[l], b_ada[l], norm1_g[l], norm2_g[l], w_in[l], gmlp_ws[l], gmlp_bs[l],
            sconv_w[l], lambda_q1[l], lambda_k1[l], lambda_q2[l], lambda_k2[l], subln_g[l],
            w_out[l], ffn_w_up[l], ffn_conv_w[l], ffn_w_down[l])
    return rmsnorm(x, final_g)


DEPTH_2 = 1


MLSTM_HEADS = 4
MLSTM_DH = 128
MLSTM_W = MLSTM_HEADS * MLSTM_DH
MLSTM_GATES = 2 * 2 * MLSTM_HEADS
MLSTM_CHUNK = 128

ATTN_Q_HEADS = 8
ATTN_KV_HEADS = 2
ATTN_GROUP = ATTN_Q_HEADS // ATTN_KV_HEADS
ATTN_DH = 64
ATTN_Q_W = ATTN_Q_HEADS * ATTN_DH
ATTN_KV_W = ATTN_KV_HEADS * ATTN_DH
WINDOW = 128
ATTN_BLOCK = 128
ROPE_BASE = 10000.0
ROPE_AXIS_FREQS = ATTN_DH // 4

N_BRANCH = 2
IN_SIZES = (MLSTM_W, MLSTM_W, MLSTM_W, MLSTM_W, MLSTM_GATES,
            ATTN_Q_W, ATTN_KV_W, ATTN_KV_W, N_BRANCH * D_MODEL)
D_IN = 4 * MLSTM_W + MLSTM_GATES + ATTN_Q_W + 2 * ATTN_KV_W + N_BRANCH * D_MODEL

PEER_HEADS = 8
PEER_N_KEYS = 128
PEER_N_EXPERTS = PEER_N_KEYS * PEER_N_KEYS
PEER_KEY_DIM = 256
PEER_HALF = PEER_KEY_DIM // 2
PEER_TOPK = 16
PEER_BLOCK = 128


def _rms(x, g):
    xf = x.astype(jnp.float32)
    y = xf * lax.rsqrt(jnp.mean(xf * xf, axis=-1, keepdims=True) + EPS)
    return y.astype(x.dtype) * g

def _modulate(x, g, shift, scale):
    return _rms(x, g) * (1 + scale) + shift

def _adaln(cond, w, b):
    mod = jax.nn.silu(cond) @ w + b
    return tuple(m[:, None, :] for m in jnp.split(mod, 6, axis=-1))

def _split_in(p):
    idx = []
    acc = 0
    for s in IN_SIZES[:-1]:
        acc += s
        idx.append(acc)
    return jnp.split(p, idx, axis=-1)

def _axial_rope(T):
    rows = T // GRID_W
    row = jnp.broadcast_to(jnp.arange(rows)[:, None], (rows, GRID_W)).reshape(T)
    col = jnp.broadcast_to(jnp.arange(GRID_W)[None, :], (rows, GRID_W)).reshape(T)
    inv = ROPE_BASE ** (-jnp.arange(ROPE_AXIS_FREQS, dtype=jnp.float32) / ROPE_AXIS_FREQS)
    ang = jnp.concatenate([row[:, None].astype(jnp.float32) * inv,
                           col[:, None].astype(jnp.float32) * inv], axis=-1)
    return jnp.cos(ang), jnp.sin(ang)

def _rope(t, cos, sin):
    t1, t2 = jnp.split(t, 2, axis=-1)
    c = cos[None, :, None, :]
    s = sin[None, :, None, :]
    return jnp.concatenate([t1 * c - t2 * s, t2 * c + t1 * s], axis=-1).astype(t.dtype)

def _chunk_seq(t, reverse):
    if reverse:
        t = jnp.flip(t, axis=1)
    B, T = t.shape[:2]
    t = jnp.moveaxis(t, 2, 1)
    return t.reshape((B, t.shape[1], T // MLSTM_CHUNK, MLSTM_CHUNK) + t.shape[3:])

def _unchunk(h, reverse):
    B, H = h.shape[:2]
    h = jnp.moveaxis(h.reshape(B, H, -1, h.shape[-1]), 1, 2)
    return jnp.flip(h, axis=1) if reverse else h

def _mlstm_summaries(k, v, li, lf):
    b = jnp.cumsum(lf, axis=-1)
    a = b[..., -1]
    w_log = a[..., None] - b + li
    m_loc = jnp.max(w_log, axis=-1)
    w = jnp.exp(w_log - m_loc[..., None])
    C_loc = jnp.einsum('bhcs,bhcsk,bhcsv->bhckv', w, k, v)
    n_loc = jnp.einsum('bhcs,bhcsk->bhck', w, k)
    return b, a, m_loc, C_loc, n_loc

def _mlstm_scan(a, m_loc, C_loc, n_loc, state0):
    def step(carry, inp):
        C, n, m = carry
        a_c, m_c, C_c, n_c = inp
        m_new = jnp.maximum(a_c + m, m_c)
        d_old = jnp.exp(a_c + m - m_new)
        d_new = jnp.exp(m_c - m_new)
        C_new = d_old[..., None, None] * C + d_new[..., None, None] * C_c
        n_new = d_old[..., None] * n + d_new[..., None] * n_c
        return (C_new, n_new, m_new), (C, n, m)
    xs = tuple(jnp.moveaxis(t, 2, 0) for t in (a, m_loc, C_loc, n_loc))
    final, starts = lax.scan(step, state0, xs)
    starts = tuple(jnp.moveaxis(t, 0, 2) for t in starts)
    return starts, final

def _mlstm_outputs(q, k, v, li, b, starts):
    C_s, n_s, m_s = starts
    L = q.shape[-2]
    log_inter = b + m_s[..., None]
    log_d = b[..., :, None] - b[..., None, :] + li[..., None, :]
    seen = jnp.tril(jnp.ones((L, L), dtype=bool))
    log_d = jnp.where(seen, log_d, -jnp.inf)
    m_t = jnp.maximum(log_inter, jnp.max(log_d, axis=-1))
    s = jnp.einsum('bhctk,bhcsk->bhcts', q, k) * jnp.exp(log_d - m_t[..., None])
    inter = jnp.exp(log_inter - m_t)
    num = (jnp.einsum('bhcts,bhcsv->bhctv', s, v)
           + inter[..., None] * jnp.einsum('bhctk,bhckv->bhctv', q, C_s))
    den = jnp.sum(s, axis=-1) + inter * jnp.einsum('bhctk,bhck->bhct', q, n_s)
    return num / jnp.maximum(jnp.abs(den), jnp.exp(-m_t))[..., None]

def _mlstm_direction(ctx_in, lat_in, reverse, with_ctx_out):
    qc, kc, vc, ic, fc = (_chunk_seq(t, reverse) for t in ctx_in)
    ql, kl, vl, il, fl = (_chunk_seq(t, reverse) for t in lat_in)
    B, H = qc.shape[:2]
    state0 = (jnp.zeros((B, H, MLSTM_DH, MLSTM_DH), jnp.float32),
              jnp.zeros((B, H, MLSTM_DH), jnp.float32),
              jnp.zeros((B, H), jnp.float32))
    bc, ac, mc, Cc, nc = _mlstm_summaries(kc, vc, ic, fc)
    starts_c, final_c = _mlstm_scan(ac, mc, Cc, nc, state0)
    bl, al, ml, Cl, nl = _mlstm_summaries(kl, vl, il, fl)
    starts_l, _ = _mlstm_scan(al, ml, Cl, nl, final_c)
    h_lat = _unchunk(_mlstm_outputs(ql, kl, vl, il, bl, starts_l), reverse)
    h_ctx = _unchunk(_mlstm_outputs(qc, kc, vc, ic, bc, starts_c), reverse) if with_ctx_out else None
    return h_lat, h_ctx

def _mlstm_branch(parts_lat, parts_ctx, b_mgates, norm_g, with_ctx_out):
    def prep(parts):
        q, k, v, o, gates = parts
        B, T = q.shape[:2]
        hd = lambda t: t.astype(jnp.float32).reshape(B, T, MLSTM_HEADS, MLSTM_DH)
        g = (gates.astype(jnp.float32) + b_mgates.astype(jnp.float32)).reshape(B, T, 2, 2, MLSTM_HEADS)
        return hd(q), hd(k) * (MLSTM_DH ** -0.5), hd(v), o, g

    ql, kl, vl, ol, gl = prep(parts_lat)
    qc, kc, vc, oc, gc = prep(parts_ctx)
    hs_lat, hs_ctx = [], []
    for d, reverse in enumerate((False, True)):
        lat_in = (ql, kl, vl, gl[:, :, d, 0], jax.nn.log_sigmoid(gl[:, :, d, 1]))
        ctx_in = (qc, kc, vc, gc[:, :, d, 0], jax.nn.log_sigmoid(gc[:, :, d, 1]))
        hl, hc = _mlstm_direction(ctx_in, lat_in, reverse, with_ctx_out)
        hs_lat.append(hl)
        hs_ctx.append(hc)

    def finish(h, o):
        B, T = h.shape[:2]
        hn = h * lax.rsqrt(jnp.mean(h * h, axis=-1, keepdims=True) + EPS)
        return hn.reshape(B, T, MLSTM_W).astype(o.dtype) * norm_g * jax.nn.sigmoid(o)

    m_lat = finish(hs_lat[0] + hs_lat[1], ol)
    m_ctx = finish(hs_ctx[0] + hs_ctx[1], oc) if with_ctx_out else None
    return m_lat, m_ctx

def _softmax_with_sink(logits, sink_b):
    sink_col = jnp.broadcast_to(sink_b, logits.shape[:-1] + (1,))
    return jax.nn.softmax(jnp.concatenate([logits, sink_col], axis=-1), axis=-1)[..., :-1]

def _window_attention(q, k, v, kc, vc, sink):
    B, T = q.shape[:2]
    nb = T // ATTN_BLOCK
    scale = ATTN_DH ** -0.5
    qb = q.reshape(B, nb, ATTN_BLOCK, ATTN_KV_HEADS, ATTN_GROUP, ATTN_DH)

    def band(t):
        tp = jnp.pad(t, ((0, 0), (ATTN_BLOCK, ATTN_BLOCK), (0, 0), (0, 0)))
        tp = tp.reshape(B, nb + 2, ATTN_BLOCK, ATTN_KV_HEADS, ATTN_DH)
        return jnp.concatenate([tp[:, :-2], tp[:, 1:-1], tp[:, 2:]], axis=2)

    kw, vw = band(k), band(v)
    qi = jnp.arange(ATTN_BLOCK)[:, None]
    kj = jnp.arange(3 * ATTN_BLOCK)[None, :]
    key_pos = jnp.arange(nb)[:, None, None] * ATTN_BLOCK - ATTN_BLOCK + kj[None]
    mask = (jnp.abs(kj - ATTN_BLOCK - qi) <= WINDOW)[None] & (key_pos >= 0) & (key_pos < T)
    s_loc = jnp.einsum('bnqhgd,bnkhd->bnhgqk', qb, kw).astype(jnp.float32) * scale
    s_loc = jnp.where(mask[None, :, None, None], s_loc, -jnp.inf)
    s_ctx = jnp.einsum('bnqhgd,bchd->bnhgqc', qb, kc).astype(jnp.float32) * scale
    sink_b = sink.astype(jnp.float32).reshape(ATTN_KV_HEADS, ATTN_GROUP, 1, 1)
    p = _softmax_with_sink(jnp.concatenate([s_loc, s_ctx], axis=-1), sink_b)
    p_loc = p[..., :3 * ATTN_BLOCK].astype(v.dtype)
    p_ctx = p[..., 3 * ATTN_BLOCK:].astype(v.dtype)
    out = (jnp.einsum('bnhgqk,bnkhd->bnqhgd', p_loc, vw)
           + jnp.einsum('bnhgqc,bchd->bnqhgd', p_ctx, vc))
    return out.reshape(B, T, ATTN_Q_W)

def _context_attention(qc, kc, vc, sink):
    B, Lc = qc.shape[:2]
    qg = qc.reshape(B, Lc, ATTN_KV_HEADS, ATTN_GROUP, ATTN_DH)
    s = jnp.einsum('bqhgd,bkhd->bhgqk', qg, kc).astype(jnp.float32) * (ATTN_DH ** -0.5)
    sink_b = sink.astype(jnp.float32).reshape(ATTN_KV_HEADS, ATTN_GROUP, 1, 1)
    p = _softmax_with_sink(s, sink_b).astype(vc.dtype)
    return jnp.einsum('bhgqk,bkhd->bqhgd', p, vc).reshape(B, Lc, ATTN_Q_W)

def _attn_branch(parts_lat, parts_ctx, q_g, k_g, sink, cos, sin, with_ctx_out):
    def heads(t, h):
        return t.reshape(t.shape[0], t.shape[1], h, ATTN_DH)
    ql, kl, vl = parts_lat
    qc, kc, vc = parts_ctx
    ql = _rope(_rms(heads(ql, ATTN_Q_HEADS), q_g), cos, sin)
    kl = _rope(_rms(heads(kl, ATTN_KV_HEADS), k_g), cos, sin)
    vl = heads(vl, ATTN_KV_HEADS)
    kc = _rms(heads(kc, ATTN_KV_HEADS), k_g)
    vc = heads(vc, ATTN_KV_HEADS)
    a_lat = _window_attention(ql, kl, vl, kc, vc, sink)
    a_ctx = None
    if with_ctx_out:
        a_ctx = _context_attention(_rms(heads(qc, ATTN_Q_HEADS), q_g), kc, vc, sink)
    return a_lat, a_ctx

def _token_mixer(h_lat, h_ctx, w_in, b_mgates, mlstm_norm_g, q_g, k_g, sink,
                 w_bm, w_ba, w_out, cos, sin, with_ctx_out):
    pl = _split_in(h_lat @ w_in)
    pc = _split_in(h_ctx @ w_in)
    m_lat, m_ctx = _mlstm_branch(pl[:5], pc[:5], b_mgates, mlstm_norm_g, with_ctx_out)
    a_lat, a_ctx = _attn_branch(pl[5:8], pc[5:8], q_g, k_g, sink, cos, sin, with_ctx_out)

    def merge(m, a, gates):
        g_m, g_a = jnp.split(gates, 2, axis=-1)
        return (jax.nn.sigmoid(g_m) * (m @ w_bm) + jax.nn.sigmoid(g_a) * (a @ w_ba)) @ w_out

    y_lat = merge(m_lat, a_lat, pl[8])
    y_ctx = merge(m_ctx, a_ctx, pc[8]) if with_ctx_out else None
    return y_lat, y_ctx

def _peer(h, w_query, sub_keys, expert_u, expert_v):
    B, T, D = h.shape
    tok = h.reshape(-1, PEER_BLOCK, D)

    def block(xb):
        q = (xb @ w_query).reshape(PEER_BLOCK, PEER_HEADS, 2, PEER_HALF)
        s = jnp.einsum('mhpd,hpnd->mhpn', q, sub_keys).astype(jnp.float32)
        s1, i1 = lax.top_k(s[:, :, 0], PEER_TOPK)
        s2, i2 = lax.top_k(s[:, :, 1], PEER_TOPK)
        cand = (s1[..., :, None] + s2[..., None, :]).reshape(PEER_BLOCK, PEER_HEADS, PEER_TOPK * PEER_TOPK)
        cidx = (i1[..., :, None] * PEER_N_KEYS + i2[..., None, :]).reshape(PEER_BLOCK, PEER_HEADS, PEER_TOPK * PEER_TOPK)
        top, pos = lax.top_k(cand, PEER_TOPK)
        idx = jnp.take_along_axis(cidx, pos, axis=-1)
        g = jax.nn.softmax(top, axis=-1)
        act = jax.nn.gelu(jnp.einsum('mhkd,md->mhk', expert_u[idx], xb).astype(jnp.float32))
        w = (g * act).astype(xb.dtype)
        return jnp.einsum('mhk,mhkd->md', w, expert_v[idx])

    return lax.map(block, tok).reshape(B, T, D)

def second_inputs(seed: int = 0) -> dict:
    key = jax.random.key(seed)
    ks = jax.random.split(key, 24)
    f32 = jnp.float32

    def nrm(k, shape, s):
        return jax.random.normal(k, shape, f32) * s

    gate_base = jnp.tile(jnp.concatenate([jnp.zeros((MLSTM_HEADS,), f32),
                                          jnp.linspace(3.0, 6.0, MLSTM_HEADS, dtype=f32)]), 2)
    return {
        'x': nrm(ks[0], (BATCH, SEQ, D_MODEL), 1.0),
        'c': nrm(ks[1], (BATCH, D_MODEL), 1.0),
        'ctx': nrm(ks[2], (BATCH, CTX_LEN, D_MODEL), 1.0),
        'c_ctx': nrm(ks[3], (D_MODEL,), 1.0),
        'w_ada': nrm(ks[4], (DEPTH_2, D_MODEL, 6 * D_MODEL), D_MODEL ** -0.5),
        'b_ada': nrm(ks[5], (DEPTH_2, 6 * D_MODEL), 0.02),
        'norm_mix_g': 1.0 + nrm(ks[6], (DEPTH_2, D_MODEL), 0.02),
        'norm_ffn_g': 1.0 + nrm(ks[7], (DEPTH_2, D_MODEL), 0.02),
        'w_in': nrm(ks[8], (DEPTH_2, D_MODEL, D_IN), D_MODEL ** -0.5),
        'b_mgates': gate_base + nrm(ks[9], (DEPTH_2, MLSTM_GATES), 0.1),
        'mlstm_norm_g': 1.0 + nrm(ks[10], (DEPTH_2, MLSTM_W), 0.02),
        'attn_q_norm_g': 1.0 + nrm(ks[11], (DEPTH_2, ATTN_DH), 0.02),
        'attn_k_norm_g': 1.0 + nrm(ks[12], (DEPTH_2, ATTN_DH), 0.02),
        'attn_sink': nrm(ks[13], (DEPTH_2, ATTN_Q_HEADS), 0.5),
        'w_branch_m': nrm(ks[14], (DEPTH_2, MLSTM_W, D_MODEL), MLSTM_W ** -0.5),
        'w_branch_a': nrm(ks[15], (DEPTH_2, ATTN_Q_W, D_MODEL), ATTN_Q_W ** -0.5),
        'w_out': nrm(ks[16], (DEPTH_2, D_MODEL, D_MODEL), D_MODEL ** -0.5),
        'peer_w_query': nrm(ks[17], (DEPTH_2, D_MODEL, PEER_HEADS * PEER_KEY_DIM), D_MODEL ** -0.5),
        'peer_sub_keys': nrm(ks[18], (DEPTH_2, PEER_HEADS, 2, PEER_N_KEYS, PEER_HALF), PEER_HALF ** -0.5),
        'peer_u': nrm(ks[19], (DEPTH_2, PEER_N_EXPERTS, D_MODEL), D_MODEL ** -0.5),
        'peer_v': nrm(ks[20], (DEPTH_2, PEER_N_EXPERTS, D_MODEL), 0.5),
    }

def second_block(x, c, ctx, c_ctx, w_ada, b_ada, norm_mix_g, norm_ffn_g, w_in, b_mgates,
              mlstm_norm_g, attn_q_norm_g, attn_k_norm_g, attn_sink, w_branch_m, w_branch_a,
              w_out, peer_w_query, peer_sub_keys, peer_u, peer_v):
    T = x.shape[1]
    cos, sin = _axial_rope(T)
    for layer in range(DEPTH_2):
        update_ctx = layer + 1 < DEPTH_2
        sh1, sc1, g1, sh2, sc2, g2 = _adaln(c, w_ada[layer], b_ada[layer])
        csh1, csc1, cg1, csh2, csc2, cg2 = _adaln(c_ctx[None], w_ada[layer], b_ada[layer])
        h_lat = _modulate(x, norm_mix_g[layer], sh1, sc1)
        h_ctx = _modulate(ctx, norm_mix_g[layer], csh1, csc1)
        y_lat, y_ctx = _token_mixer(h_lat, h_ctx, w_in[layer], b_mgates[layer], mlstm_norm_g[layer],
                                    attn_q_norm_g[layer], attn_k_norm_g[layer], attn_sink[layer],
                                    w_branch_m[layer], w_branch_a[layer], w_out[layer],
                                    cos, sin, update_ctx)
        x = x + g1 * y_lat
        x = x + g2 * _peer(_modulate(x, norm_ffn_g[layer], sh2, sc2), peer_w_query[layer],
                           peer_sub_keys[layer], peer_u[layer], peer_v[layer])
        if update_ctx:
            ctx = ctx + cg1 * y_ctx
            ctx = ctx + cg2 * _peer(_modulate(ctx, norm_ffn_g[layer], csh2, csc2), peer_w_query[layer],
                                    peer_sub_keys[layer], peer_u[layer], peer_v[layer])
    return x


def setup_inputs(seed=0):
    out = dict(first_inputs(seed))
    for name, value in second_inputs(seed + 1).items():
        if name != "x":
            out[name + "_2"] = value
    return out


def reference(
    x, c, ctx, c_ctx, w_ada, b_ada, norm1_g, norm2_g, w_in, gmlp_ws, gmlp_bs, sconv_w,
    lambda_q1, lambda_k1, lambda_q2, lambda_k2, subln_g, w_out, ffn_w_up, ffn_conv_w,
    ffn_w_down, final_g, c_2, ctx_2, c_ctx_2, w_ada_2, b_ada_2, norm_mix_g_2, norm_ffn_g_2,
    w_in_2, b_mgates_2, mlstm_norm_g_2, attn_q_norm_g_2, attn_k_norm_g_2, attn_sink_2,
    w_branch_m_2, w_branch_a_2, w_out_2, peer_w_query_2, peer_sub_keys_2, peer_u_2, peer_v_2,
):
    x = first_block(
        x, c, ctx, c_ctx, w_ada, b_ada, norm1_g, norm2_g, w_in, gmlp_ws, gmlp_bs, sconv_w,
        lambda_q1, lambda_k1, lambda_q2, lambda_k2, subln_g, w_out, ffn_w_up, ffn_conv_w,
        ffn_w_down, final_g,
    )
    return second_block(
        x, c_2, ctx_2, c_ctx_2, w_ada_2, b_ada_2, norm_mix_g_2, norm_ffn_g_2, w_in_2,
        b_mgates_2, mlstm_norm_g_2, attn_q_norm_g_2, attn_k_norm_g_2, attn_sink_2, w_branch_m_2,
        w_branch_a_2, w_out_2, peer_w_query_2, peer_sub_keys_2, peer_u_2, peer_v_2,
    )


_drawn_inputs = setup_inputs


def setup_inputs(seed=0):
    import zlib

    import numpy as np

    out = dict(_drawn_inputs(seed))
    spreads = {}
    factors = {'norm2_g': 2.895,
     'gmlp_bs': 5.136,
     'lambda_q1': 3.424,
     'lambda_q2': 4.065,
     'lambda_k2': 3.422,
     'subln_g': 4.718,
     'norm_mix_g_2': 2.935,
     'mlstm_norm_g_2': 17.555,
     'attn_q_norm_g_2': 8.0,
     'attn_k_norm_g_2': 8.0,
     'attn_sink_2': 8.0,
     'norm_ffn_g_2': 11.848}
    for name, (base, spread) in spreads.items():
        noise = np.random.default_rng([zlib.crc32(name.encode()), seed]).standard_normal(out[name].shape)
        drawn = base * np.exp(spread * noise) if base else spread * noise
        out[name] = __import__('jax').numpy.asarray(drawn.astype(out[name].dtype))
    for name, factor in factors.items():
        out[name] = (out[name] * factor).astype(out[name].dtype)
    return out
```

```python
import math
from contextlib import ExitStack
from functools import partial

import numpy as np
import concourse.bass as bass
from concourse import mybir

F32 = mybir.dt.float32
U32 = mybir.dt.uint32
ALU = mybir.AluOpType
ACT = mybir.ActivationFunctionType
AX_X = mybir.AxisListType.X

DEPTH = 2
EPS = 1e-6
NRING = 5
TILE = 2048


class Lane:

    def __init__(self, sem):
        self.sem = sem
        self.ops = []
        self.n = 0
        self.seen = {}

    @property
    def last(self):
        return (self.sem, self.n)

    def wait(self, *marks):
        for m in marks:
            if m is None or m[1] == 0:
                continue
            if self.seen.get(m[0].name, 0) < m[1]:
                self.seen[m[0].name] = m[1]
                self.ops.append((None, m))

    def __call__(self, fn, *marks, inc=True):
        self.wait(*marks)
        if inc:
            self.n += 1
        self.ops.append((fn, inc))
        return self.last

    def play(self, eng):
        for fn, x in self.ops:
            if fn is None:
                eng.wait_ge(x[0], x[1])
            else:
                ins = fn()
                if x:
                    ins.then_inc(self.sem, 1)


class Bank:
    def __init__(self, t):
        self.t = t
        self.free = ()

    def __getitem__(self, at):
        return self.t[at]

    def release(self, *marks):
        self.free = marks


def _fields(spec):
    at, out = 0, {}
    for name, n in spec:
        out[name] = (at, n)
        at += n
    return out, at


PAR, NPAR = _fields(
    [("eye", 128), ("ones", 128), ("iota", 128), ("c1", 16), ("c2", 16), ("finalg", 8)]
    + [(f"{n}{l}", k) for l in range(DEPTH) for n, k in
       (("bada", 48), ("n1g", 8), ("n2g", 8), ("sconv", 6), ("subln", 1), ("fconv", 66), ("lam", 4), ("bs", 256))]
    + [("bada2", 48), ("n1g2", 8), ("n2g2", 8), ("gbias", 4), ("mng", 4), ("qg", 1), ("kg", 1), ("sink", 8)])

CST, NCST = _fields([("blk64", 128), ("perm1", 128), ("perm2", 128), ("cos1", 256), ("sin1", 256),
                     ("cos2", 256), ("sin2", 256), ("dftn", 1024), ("cd", 128), ("sd", 128),
                     ("cf", 512), ("cb", 512), ("win", 256), ("sel", 512)])


def build(nc, ins, out):
    ctx = ExitStack()
    with ctx:
        def sb(name, n, dt=F32):
            return ctx.enter_context(nc.sbuf_tensor(name, [128, n], dt))

        def sem(name):
            return ctx.enter_context(nc.semaphore(name))

        R = sb("R", 32768)
        XT = sb("X", 4096)
        HT = sb("H", 4096)
        RING = sb("RING", NRING * TILE)
        PT = sb("P", NPAR)
        ADA = sb("ADA", 96)
        MOD = sb("MOD", 64)
        SM = sb("SM", 80)
        X = XT[:, :].rearrange("p (k t) -> p k t", k=8)
        H = HT[:, :].rearrange("p (k t) -> p k t", k=8)

        banks = [Bank(ctx.enter_context(nc.psum_tensor(f"ps{i}", [128, 512], F32))) for i in range(8)]
        ada_bank = banks.pop()
        idle = list(banks)

        def take():
            return idle.pop(0)

        def give(b, *marks):
            b.release(*marks)
            idle.append(b)

        P, D, A, G = (Lane(sem(f"s_{n}")) for n in ("pe", "dve", "act", "pool"))
        s_in = sem("s_in")
        s_c2 = sem("s_c2")
        s_out = sem("s_out")
        s_ring = [sem(f"s_ring{i}") for i in range(NRING)]

        def par(name, a=0, b=None):
            at, n = PAR[name]
            return PT[:, at + a:at + (n if b is None else b)]

        def cst(name, a=0, b=None):
            at, n = CST[name]
            return R[:, at + a:at + (n if b is None else b)]

        eye, ones, iota = par("eye"), par("ones"), par("iota")

        tiles = []

        class Tile:
            pass

        def load(src, n=TILE):
            t = Tile()
            i = len(tiles)
            t.src, t.n, t.slot = src, n, i % NRING
            t.ready = (s_ring[t.slot], 16 * (i // NRING + 1))
            t.ap = RING[:, t.slot * TILE:t.slot * TILE + n]
            t.done = None
            tiles.append(t)
            return t

        loads_in = 16 * 4
        LOADED = (s_in, loads_in)

        def mm(o, l, r, first, last, *marks, skip=False):
            return P(partial(nc.tensor.matmul, o, l, r, start=first, stop=last, skip_group_check=skip), *marks, inc=last)

        def fence():
            marks = [P.last, D.last, A.last, G.last]
            for lane in (P, D, A, G):
                lane.wait(*marks)

        class Arena:
            def __init__(self, at):
                self.at = at

            def __call__(self, n):
                v = R[:, self.at:self.at + n]
                self.at += n
                assert self.at <= 32768
                return v

        base = Arena(NCST)
        wsT = [base(512) for _ in range(DEPTH)]
        SQ = [base(512) for _ in range(3)]
        STD, RSTD = base(512), base(512)
        sq_free = [None] * 3
        sq_n = [0]

        epsc = SM[:, 0:1]
        d_eps = D(partial(nc.vector.memset, epsc, EPS))
        for lane in (P, D, A, G):
            lane.wait(LOADED)
        A.wait(d_eps)

        def stats(src, k, t0, t1, lhs, div, x_ready, free=None):
            n = t1 - t0
            b = take()
            for i in range(k):
                j = sq_n[0] % 3
                sq_n[0] += 1
                sq = SQ[j][:, 0:n]
                s = src(i)
                a = A(partial(nc.scalar.activation, sq, s, ACT.Square), x_ready, sq_free[j])
                sq_free[j] = mm(b[:, 0:n], lhs, sq, i == 0, True if i == k - 1 else False, a, *b.free)
                if i < k - 1:
                    P.ops[-1] = (P.ops[-1][0], True)
                    P.n += 1
                    sq_free[j] = P.last
            a = A(partial(nc.scalar.activation, STD[:, 0:n], b[:, 0:n], ACT.Sqrt, bias=epsc, scale=1.0 / div), P.last, D.last)
            give(b, a)
            return D(partial(nc.vector.reciprocal, RSTD[:, 0:n], STD[:, 0:n]), a, D.last, free)

        adaq = []
        SC = SM[:, 8:24]

        def ada_begin(cname):
            cc = par(cname)
            t = A(partial(nc.scalar.activation, SC, cc, ACT.Silu), P.last)
            return t

        def ada_step(src, i, ready):
            def go():
                w = load(src[i])
                wt = w.ap.rearrange("p (k m) -> p k m", k=8)
                for j in range(2):
                    o = ada_bank[:, 4 * i + 2 * j:4 * i + 2 * j + 2]
                    for k in range(8):
                        mm(o, wt[:, k, 128 * j:128 * j + 128], SC[:, 2 * k:2 * k + 2], k == 0, k == 7,
                           w.ready, ready, *ada_bank.free)
                w.done = P.last
            return go

        def ada_take(name, m0, m1, free=()):
            o = ADA[:, 2 * m0:2 * m1].rearrange("p (m c) -> p m c", c=2)
            b = ada_bank[:, 2 * m0:2 * m1].rearrange("p (m c) -> p m c", c=2)
            bias = par(name, m0, m1).rearrange("p (m o) -> p m o", o=1).to_broadcast([128, m1 - m0, 2])
            t = D(partial(nc.vector.tensor_tensor, o, b, bias, ALU.add), P.last, A.last, D.last)
            ada_bank.release(t)
            return t

        def background(n=1):
            for _ in range(n):
                if adaq:
                    adaq.pop(0)()

        def adac(part, m, s):
            return ADA[:, (8 * part + m) * 2 + s:(8 * part + m) * 2 + s + 1]

        def mods(g, part, slot):
            o = MOD[:, 16 * slot:16 * slot + 16].rearrange("p (m c) -> p m c", c=2)
            s = ADA[:, 16 * part:16 * part + 16].rearrange("p (m c) -> p m c", c=2)
            gg = par(g).rearrange("p (m o) -> p m o", o=1).to_broadcast([128, 8, 2])
            t = D(partial(nc.vector.tensor_scalar, o, s, 1.0, None, ALU.add), D.last, A.last)
            return D(partial(nc.vector.tensor_tensor, o, o, gg, ALU.mult), t)

        def modulated(slot, shift, streams, x_ready):
            t1 = 256 * len(streams)
            r = stats(lambda i: X[:, i, 0:t1], 8, 0, t1, ones, 1024.0, x_ready)
            marks = []
            h_free = P.last
            for k in range(8):
                t = D(partial(nc.vector.tensor_tensor, H[:, k, 0:t1], X[:, k, 0:t1], RSTD[:, 0:t1], ALU.mult),
                      r, h_free)
                for s in streams:
                    v = H[:, k, 256 * s:256 * s + 256]
                    sc = MOD[:, 16 * slot + 2 * k + s:16 * slot + 2 * k + s + 1]
                    sh = adac(shift, k, s)
                    m = A(partial(nc.scalar.activation, v, v, ACT.Identity, bias=sh, scale=sc), t)
                marks.append(m)
            return marks

        def residual(b, m, gate, streams, last_p):
            for s in streams:
                o = X[:, m, 256 * s:256 * s + 256]
                i = b[:, 256 * s:256 * s + 256]
                t = D(partial(nc.vector.scalar_tensor_tensor, out=o, in0=i, scalar=adac(gate, m, s), in1=o,
                                                                     op0=ALU.mult, op1=ALU.add), last_p, D.last)
            give(b, t)
            return t

        def project(w, j, rhs, T, hmarks, K=8):
            b = take()
            wt = w.ap.rearrange("p (k m) -> p k m", k=K)
            for k in range(K):
                p = mm(b[:, 0:T], wt[:, k, 128 * j:128 * j + 128], rhs(k), k == 0, k == K - 1,
                       w.ready, hmarks[k], *b.free)
            return b, p

        def token_rows(w, tb, hmarks, c0=0, c1=256, b=None, at=0):
            wt = w.ap.rearrange("p (k m) -> p k m", k=8)
            for k in range(8):
                p = mm(b[:, at:at + c1 - c0], H[:, k, 128 * tb:128 * tb + 128], wt[:, k, c0:c1], k == 0, k == 7,
                       w.ready, hmarks[k], *b.free)
            return p

        def conv_taps(o, src, wcol, n_str, first, first_mark, psum_mark):
            ov = o.rearrange("p (s t) -> p s t", t=256)
            sv = src.rearrange("p (s t) -> p s t", t=256)
            t = D(partial(nc.vector.scalar_tensor_tensor, out=ov[:, :, 1:256], in0=sv[:, :, 0:255], scalar=wcol(0),
                                                   in1=ov[:, :, 1:256], op0=ALU.mult, op1=ALU.add),
                  first_mark, psum_mark)
            return D(partial(nc.vector.scalar_tensor_tensor, out=ov[:, :, 0:255], in0=sv[:, :, 1:256], scalar=wcol(2),
                                                      in1=ov[:, :, 0:255], op0=ALU.mult, op1=ALU.add), t)

        s_ready = ada_begin("c1")
        for i in range(8):
            ada_step(ins["wada0"], i, s_ready)()
        ada_take("bada0", 0, 16)
        adaq += [ada_step(ins["wada0"], i, s_ready) for i in range(8, 24)]
        x_ready = LOADED

        for l in range(DEPTH):
            lam_init = 0.8 - 0.6 * math.exp(-0.3 * l)
            full = [0, 1]
            streams = [0, 1] if l < DEPTH - 1 else [0]
            T = 256 * len(streams)
            NTB = T // 128
            ar = Arena(base.at)
            MIX = ar(4096).rearrange("p (k t) -> p k t", k=8)
            prob = [ar(1024) for _ in range(2)]
            att = [ar(512) for _ in range(2)]
            attT = [ar(512) for _ in range(2)]
            mid_at = ar.at
            q_f = ar(1024).rearrange("p (j t) -> p j t", j=2)
            k_f = ar(1024).rearrange("p (j t) -> p j t", j=2)
            v_d = ar(1024).rearrange("p (b c) -> p b c", b=4)
            v_a = ar(1024).rearrange("p (b c) -> p b c", b=4)
            u_f = ar(1024).rearrange("p (j t) -> p j t", j=2)
            f_c = ar(1024).rearrange("p (b c) -> p b c", b=4)
            PQ = [ar(512) for _ in range(2)]
            bx = ar(1024).rearrange("p (j t) -> p j t", j=2)
            cv = ar(1024).rearrange("p (j t) -> p j t", j=2)
            rt = [ar(256) for _ in range(2)]
            o_d = ar(1024).rearrange("p (j t) -> p j t", j=2)
            st = ar(64)

            mods(f"n1g{l}", 1, 0)
            lm = par(f"lam{l}")
            lp = SM[:, 24:26]
            t = D(partial(nc.vector.tensor_tensor, lp[0:32, :], lm[0:32, 0:2], lm[0:32, 2:4], ALU.mult), D.last, P.last)
            b = take()
            p = mm(b[:, 0:2], ones[0:32, :], lp[0:32, :], True, True, t, *b.free)
            le = SM[:, 26:28]
            a = A(partial(nc.scalar.activation, le, b[:, 0:2], ACT.Exp), p, D.last)
            give(b, a)
            nlam = SM[:, 28:29]
            t = D(partial(nc.vector.tensor_tensor, nlam, le[:, 1:2], le[:, 0:1], ALU.subtract), a, D.last)
            D(partial(nc.vector.tensor_scalar, nlam, nlam, -lam_init, None, ALU.add), t)
            sg = SM[:, 29:30]
            d_sg = D(partial(nc.vector.tensor_scalar, sg, par(f"subln{l}"), 1.0 - lam_init, None, ALU.mult))

            hm = modulated(0, 0, full, x_ready)
            win = ins[f"win{l}"]

            def rope(dst, b, p, j, ctx_too):
                n = 512 if ctx_too else 256
                c = A(partial(nc.scalar.activation, dst[:, j, 0:n], b[:, 0:n], ACT.Copy), p, D.last)
                give(b, c)
                b2 = take()
                p2 = mm(b2[:, 0:256], cst("perm1"), dst[:, j, 0:256], True, True, c, *b2.free)
                t = D(partial(nc.vector.tensor_tensor, rt[j], b2[:, 0:256], cst("sin1"), ALU.mult), p2, D.last)
                give(b2, t)
                t2 = D(partial(nc.vector.tensor_tensor, dst[:, j, 0:256], dst[:, j, 0:256], cst("cos1"), ALU.mult), c, p2)
                return D(partial(nc.vector.tensor_tensor, dst[:, j, 0:256], dst[:, j, 0:256], rt[j], ALU.add), t, t2)

            fence() if l else None
            w = load(win[1])
            for half in range(NTB // 2):
                b = take()
                for tb in (2 * half, 2 * half + 1):
                    p = token_rows(w, tb, hm, b=b, at=256 * (tb % 2))
                vv = v_a[:, 2 * half:2 * half + 2, :]
                a = A(partial(nc.scalar.activation, vv, b[:, :].rearrange("p (b c) -> p b c", b=2),
                                                         ACT.Gelu_apprx_tanh), p)
                give(b, a)
            w.done = P.last
            va_ready = A.last
            w = load(win[0])
            for j in range(2):
                b, p = project(w, j, lambda k: H[:, k, 0:T], T, hm)
                a = A(partial(nc.scalar.activation, u_f[:, j, 0:T], b[:, 0:T], ACT.Gelu_apprx_tanh), p)
                give(b, a)
            w.done = P.last
            u_ready = A.last
            vsq = cv
            n = NTB * 256
            fl = v_a[:, 0:NTB, :].rearrange("p b (h d) -> p (b h) d", d=64)
            sqv = vsq.rearrange("p j t -> p (j t)")[:, 0:n].rearrange("p (b d) -> p b d", d=64)
            t = D(partial(nc.vector.tensor_tensor, sqv, fl, fl, ALU.mult), va_ready)
            sv, sv2 = st[:, 0:4 * NTB], st[:, 16:16 + 4 * NTB]
            t = D(partial(nc.vector.tensor_reduce, sv, sqv, AX_X, ALU.add), t)
            a = A(partial(nc.scalar.activation, sv2, sv, ACT.Sqrt, bias=epsc, scale=1.0 / 64), t)
            t = D(partial(nc.vector.reciprocal, sv, sv2), a, t)
            va_ok = D(partial(nc.vector.tensor_tensor, fl, fl, sv.rearrange("p (b o) -> p b o", o=1)
                                                .to_broadcast([128, 4 * NTB, 64]), ALU.mult), t)
            w = load(win[6])
            for j in range(2):
                b, p = project(w, j, lambda k: H[:, k, 0:T], T, hm)
                q_ok = rope(q_f, b, p, j, T == 512)
            w.done = P.last
            w = load(win[7])
            for j in range(2):
                b, p = project(w, j, lambda k: H[:, k, 0:512], 512, hm)
                k_ok = rope(k_f, b, p, j, True)
            w.done = P.last
            w = load(win[8])
            for half in range(2):
                b = take()
                for tb in (2 * half, 2 * half + 1):
                    p = token_rows(w, tb, hm, b=b, at=256 * (tb % 2))
                vv = v_d[:, 2 * half:2 * half + 2, :]
                vd_ok = A(partial(nc.scalar.activation, vv, b[:, :].rearrange("p (b c) -> p b c", b=2),
                                                             ACT.Copy), p)
                give(b, vd_ok)
            w.done = P.last

            fill = []

            def mix_a(j, l=l, NTB=NTB, T=T, va_ok=va_ok, u_ready=u_ready, v_a=v_a, u_f=u_f, MIX=MIX):
                b = take()
                for tb in range(NTB):
                    for hh in range(2):
                        h = 2 * j + hh
                        p = mm(b[64 * hh:64 * hh + 64, 128 * tb:128 * tb + 128], v_a[:, tb, 64 * h:64 * h + 64],
                               wsT[l][:, 128 * h:128 * h + 128], True, True, va_ok, *b.free)
                bs = par(f"bs{l}", 128 * j, 128 * j + 128).rearrange("p (o t) -> p o t", o=1)\
                    .to_broadcast([128, NTB, 128])
                o = MIX[:, j, 0:T].rearrange("p (b t) -> p b t", t=128)
                t = D(partial(nc.vector.tensor_tensor, o, b[:, 0:T].rearrange("p (b t) -> p b t", t=128), bs, ALU.add), p)
                give(b, t)
                D(partial(nc.vector.tensor_tensor, MIX[:, j, 0:T], MIX[:, j, 0:T], u_f[:, j, 0:T], ALU.mult), t, u_ready)

            fill += [lambda: mix_a(0), lambda: mix_a(1)]
            hold = {}

            def four(half, T=T, f_c=f_c, hm=hm, win=win, hold=hold):
                if half == 0:
                    hold["f"] = load(win[5])
                w = hold["f"]
                b = take()
                for tb in (2 * half, 2 * half + 1):
                    p = token_rows(w, tb, hm, b=b, at=256 * (tb % 2))
                w.done = p
                t = D(partial(nc.vector.tensor_copy, f_c[:, 2 * half:2 * half + 2, :],
                                              b[:, :].rearrange("p (b c) -> p b c", b=2)), p)
                give(b, t)
                hold["f_ok"] = t

            def four2(s, j, f_c=f_c, PQ=PQ, MIX=MIX, hold=hold):
                b = take()
                for c in range(2):
                    p = mm(b[:, :], f_c[:, 2 * s + c, 128 * j:128 * j + 128], cst("dftn", 512 * c, 512 * c + 512),
                           c == 0, c == 1, hold["f_ok"], *b.free)
                pq = PQ[j]
                t = A(partial(nc.scalar.activation, pq, b[:, :], ACT.Copy), p, hold.get(("pq", j)))
                give(b, t)
                b2 = take()
                mm(b2[:, 0:256], cst("cd"), pq[:, 0:256], True, False, t, *b2.free)
                p = mm(b2[:, 0:256], cst("sd"), pq[:, 256:512], False, True)
                hold[("pq", j)] = p
                o = MIX[:, 4 + j, 256 * s:256 * s + 256]
                t = A(partial(nc.scalar.activation, o, b2[:, 0:256], ACT.Copy), p)
                give(b2, t)

            fill += [lambda h=h: four(h) for h in range(len(streams))]
            fill += [lambda s=s, j=j: four2(s, j) for s in streams for j in range(2)]

            def gate_b(g, j, l=l, T=T, bx=bx, cv=cv, MIX=MIX, hm=hm, win=win, hold=hold):
                if j == 0:
                    hold["w"] = load(win[g])
                w = hold["w"]
                b, p = project(w, j, lambda k: H[:, k, 0:T], T, hm)
                w.done = p
                if g == 2:
                    t = A(partial(nc.scalar.activation, bx[:, j, 0:T], b[:, 0:T], ACT.Copy), p)
                    hold[("bx", j)] = t
                elif g == 4:
                    t = D(partial(nc.vector.tensor_tensor, bx[:, j, 0:T], bx[:, j, 0:T], b[:, 0:T], ALU.mult), p,
                          hold[("bx", j)])
                    o = cv[:, j, 0:T]
                    wc = lambda i, l=l, j=j: par(f"sconv{l}", 3 * j + i, 3 * j + i + 1)
                    t2 = D(partial(nc.vector.tensor_scalar, o, bx[:, j, 0:T], wc(1), None, ALU.mult), t)
                    hold[("cv", j)] = conv_taps(o, bx[:, j, 0:T], wc, len(streams), None, t2, t)
                else:
                    t = D(partial(nc.vector.tensor_tensor, MIX[:, 2 + j, 0:T], cv[:, j, 0:T], b[:, 0:T], ALU.mult), p,
                          hold[("cv", j)])
                give(b, t)

            fill += [lambda g=g, j=j: gate_b(g, j) for g in (2, 4, 3) for j in range(2)]

            SCALE = 32 ** -0.5
            units = [(s, qb, h) for s in streams for h in range(4) for qb in range(2)]
            state = {}
            ring_free = {}

            def scores(n, q_f=q_f, k_f=k_f, units=units, state=state, q_ok=q_ok, k_ok=k_ok):
                s, qb, h = units[n]
                j, r0 = h // 2, 64 * (h % 2)
                cols = 512 if s == 0 else 256
                k0 = 0 if s == 0 else 256
                bs = [take(), take()]
                views = []
                for m in range(2):
                    v = bs[m][:, 0:cols]
                    r = r0 + 32 * m
                    p = P(partial(nc.tensor.matmul, 
                        v, q_f[r:r + 32, j, 256 * s + 128 * qb:256 * s + 128 * qb + 128],
                        k_f[r:r + 32, j, k0:k0 + cols], start=True, stop=True, tile_position=(r, 0)),
                        q_ok, k_ok, *bs[m].free)
                    views.append(v)
                state[n] = (bs, views, p)

            def softmax(n, units=units, state=state, prob=prob, att=att, st=st, nlam=nlam, ring_free=ring_free):
                s, qb, h = units[n]
                bs, views, p = state[n]
                cols = 512 if s == 0 else 256
                i = n % 2
                x0 = 32 + 8 * i
                mx, sm_, rc = st[:, x0:x0 + 2], st[:, x0 + 2:x0 + 4], st[:, x0 + 4:x0 + 6]
                pr = [prob[i][:, 0:cols], prob[i][:, 512:512 + cols]]
                for m in range(2):
                    t = D(partial(nc.vector.tensor_reduce, mx[:, m:m + 1], views[m], AX_X, ALU.max), p,
                          ring_free.get(("st", i)))
                t = D(partial(nc.vector.tensor_scalar, mx, mx, -SCALE, None, ALU.mult), t)
                for m in range(2):
                    a = A(partial(nc.scalar.activation, pr[m], views[m], ACT.Exp, bias=mx[:, m:m + 1], scale=SCALE,
                                                      accum_out=sm_[:, m:m + 1]), t, ring_free.get(("prob", i)))
                for b in bs:
                    give(b, a, t)
                t = D(partial(nc.vector.reciprocal, rc, sm_), a)
                t2 = D(partial(nc.vector.tensor_tensor, rc[:, 1:2], rc[:, 1:2], nlam, ALU.mult), t)
                aa = att[i][:, 0:cols]
                t = D(partial(nc.vector.tensor_scalar, aa, pr[0], rc[:, 0:1], None, ALU.mult), t, t2,
                      ring_free.get(("att", i)))
                t = D(partial(nc.vector.scalar_tensor_tensor, out=aa, in0=pr[1], scalar=rc[:, 1:2], in1=aa,
                                                       op0=ALU.mult, op1=ALU.add), t)
                ring_free[("prob", i)] = t
                ring_free[("st", i)] = t
                state[("a", n)] = t

            def apply(n, units=units, state=state, att=att, attT=attT, v_d=v_d, o_d=o_d, ring_free=ring_free,
                      vd_ok=vd_ok):
                s, qb, h = units[n]
                i = n % 2
                nk = 4 if s == 0 else 2
                b = take()
                for c in range(nk):
                    p = P(partial(nc.tensor.transpose, b[:, 128 * c:128 * c + 128], att[i][:, 128 * c:128 * c + 128],
                                                     eye), state[("a", n)], *b.free)
                ring_free[("att", i)] = p
                a = A(partial(nc.scalar.activation, attT[i][:, 0:128 * nk], b[:, 0:128 * nk], ACT.Copy), p,
                      ring_free.get(("attT", i)))
                give(b, a)
                j, r0 = h // 2, 64 * (h % 2)
                b2 = take()
                for c in range(nk):
                    tb = c + (0 if s == 0 else 2)
                    p = mm(b2[r0:r0 + 64, 0:128], v_d[:, tb, 64 * h:64 * h + 64],
                           attT[i][:, 128 * c:128 * c + 128], c == 0, c == nk - 1, a, vd_ok, *b2.free)
                ring_free[("attT", i)] = p
                t = D(partial(nc.vector.tensor_copy, o_d[r0:r0 + 64, j, 256 * s + 128 * qb:256 * s + 128 * qb + 128],
                                              b2[r0:r0 + 64, 0:128]), p)
                give(b2, t)

            scores(0)
            softmax(0)
            scores(1)
            softmax(1)
            for n in range(len(units)):
                if fill:
                    fill.pop(0)()
                background(1)
                apply(n)
                if n + 2 < len(units):
                    scores(n + 2)
                    softmax(n + 2)
            while fill:
                fill.pop(0)()
            while adaq:
                background()
            if l == 0:
                ada_take("bada0", 16, 48)
                mods("n2g0", 4, 1)
            for j in range(2):
                r = stats(lambda i, j=j: o_d[:, j, 0:T], 1, 0, T, cst("blk64"), 64.0, D.last)
                t = D(partial(nc.vector.scalar_tensor_tensor, out=MIX[:, 6 + j, 0:T], in0=o_d[:, j, 0:T], scalar=sg,
                                                            in1=RSTD[:, 0:T], op0=ALU.mult, op1=ALU.mult), r, d_sg)
            P.wait(D.last, A.last)
            for i in range(4):
                w = load(ins[f"wout{l}"][i])
                for j in range(2):
                    b, p = project(w, j, lambda k: MIX[:, k, 0:T], T, [None] * 8)
                    x_ready = residual(b, 2 * i + j, 2, streams, p)
                w.done = P.last

            hm = modulated(1, 3, streams, x_ready)
            fence()
            ar = Arena(mid_at)
            MID = ar(11264).rearrange("p (m t) -> p m t", m=22)
            ar2 = Arena(base.at)
            OC = [ar2(512) for _ in range(3)]
            oc_free = [None] * 3
            wup = ins[f"wup{l}"]

            nxt = ["wada1", "wada2"][l]
            s_ready = ada_begin(["c1", "c2"][l]) if l else s_ready
            adaq += [ada_step(ins[nxt], i, s_ready) for i in range(24)]

            for i in range(11):
                wa = load(wup[i])
                wb = load(wup[11 + i])
                for j in range(2):
                    m = 2 * i + j
                    ba, pa = project(wa, j, lambda k: H[:, k, 0:T], T, hm)
                    if j:
                        wa.done = pa
                    o = OC[m % 3][:, 0:T]
                    wc = lambda c, m=m, l=l: par(f"fconv{l}", 3 * m + c, 3 * m + c + 1)
                    a = A(partial(nc.scalar.activation, o, ba[:, 0:T], ACT.Copy, scale=wc(1)), pa,
                          oc_free[m % 3])
                    t = conv_taps(o, ba[:, 0:T], wc, len(streams), None, a, pa)
                    give(ba, a, t)
                    a = A(partial(nc.scalar.activation, o, o, ACT.Silu), t)
                    bb, pb = project(wb, j, lambda k: H[:, k, 0:T], T, hm)
                    if j:
                        wb.done = pb
                    t = D(partial(nc.vector.tensor_tensor, MID[:, m, 0:T], o, bb[:, 0:T], ALU.mult), a, pb)
                    oc_free[m % 3] = t
                    give(bb, t)
                background(1)
            mid_ready = D.last
            ada_free = None
            for m in range(8):
                b = take()
                for hf in range(2):
                    w = load(ins[f"wdn{l}"][2 * m + hf], 1408)
                    wt = w.ap.rearrange("p (k m) -> p k m", k=11)
                    for k in range(11):
                        last = hf == 1 and k == 10
                        mm(b[:, 0:T], wt[:, k, :], MID[:, 11 * hf + k, 0:T], hf == 0 and k == 0, last,
                           w.ready, mid_ready, *b.free)
                    if hf == 0:
                        P.ops[-1] = (P.ops[-1][0], True)
                        P.n += 1
                    w.done = P.last
                x_ready = residual(b, m, 5, streams, P.last)
                background(2)
            while adaq:
                background()
            t = ada_take(["bada1", "bada2"][l], 0, 48)
            mods(["n1g1", "n1g2"][l], 1, 0)
            mods(["n2g1", "n2g2"][l], 4, 1)

        r = stats(lambda i: X[:, i, 0:256], 8, 0, 256, ones, 1024.0, x_ready)
        for k in range(8):
            t = D(partial(nc.vector.scalar_tensor_tensor, out=X[:, k, 0:256], in0=X[:, k, 0:256],
                                                        scalar=par("finalg", k, k + 1), in1=RSTD[:, 0:256],
                                                        op0=ALU.mult, op1=ALU.mult), r)
        x_ready = t
        x2_free = P.last
        x2_free_d = D.last

        fence()
        A.wait((s_c2, 16))
        D.wait((s_c2, 16))
        ar = Arena(base.at)
        q_a = ar(1024).rearrange("p (j t) -> p j t", j=4)
        k_a = ar(512)
        v_t = ar(512).rearrange("p (b c) -> p b c", b=4)
        q_m = ar(1024).rearrange("p (j t) -> p j t", j=4)
        k_m = ar(2048).rearrange("p (j t) -> p j t", j=4)
        v_m = ar(2048).rearrange("p (b c) -> p b c", b=4)
        o_g = ar(1024).rearrange("p (j t) -> p j t", j=4)
        m_T = ar(1024).rearrange("p (j t) -> p j t", j=4)
        a_T = ar(1024).rearrange("p (j t) -> p j t", j=4)
        MG = ar(2048).rearrange("p (k t) -> p k t", k=8)
        prob = [ar(512) for _ in range(3)]
        attT = [ar(512) for _ in range(2)]
        RB = [ar(512) for _ in range(2)]
        DD = [ar(256) for _ in range(3)]
        PP = [ar(1024) for _ in range(2)]
        rt = [ar(256) for _ in range(2)]
        hs = [ar(256) for _ in range(2)]
        tmp = [ar(256) for _ in range(2)]
        keep = [ar(512) for _ in range(3)]
        spare = [MG[:, 2 * i:2 * i + 2, :].rearrange("p k t -> p (k t)") for i in range(4)]
        spare += [v[:, 2 * i:2 * i + 2, :].rearrange("p k t -> p (k t)") for v in (m_T, a_T) for i in range(2)]
        st = ar(64)
        cT = ar(32)
        wg = ar(128).rearrange("p (k m) -> p k m", k=8)

        hm = modulated(0, 0, [0, 1], x_ready)
        w2 = ins["win2"]

        w = load(ins["wg2"], 128)
        wv = w.ap.rearrange("p (k m) -> p k m", k=8)
        gb = []
        for g in range(4):
            b = take()
            for k in range(8):
                p = mm(b[0:4, :], wv[:, k, 4 * g:4 * g + 4], H[:, k, :], k == 0, k == 7, w.ready, hm[k], *b.free)
            gb.append((b, p))
        w.done = P.last
        ONE = keep[2][0:4, :]
        D(partial(nc.vector.memset, ONE, 1.0))
        dirs = []
        for d in range(2):
            (bi, pi), (bf, pf) = gb[2 * d], gb[2 * d + 1]
            gi, t1_, t2_, c_n = (spare[4 * d + i][0:4, :] for i in range(4))
            gf = keep[d][0:4, :]
            bias = lambda g: par("gbias", g, g + 1)[0:4, :]

            def seq(v, half, d=d):
                s = v[:, 256:512] if half == 0 else v[:, 0:256]
                return s[:, ::-1] if d else s

            for half in range(2):
                o = gi[:, 256 * half:256 * half + 256]
                t = D(partial(nc.vector.tensor_scalar, o, seq(bi[0:4, :], half), bias(2 * d), None, ALU.add),
                      pi)
                o = gf[:, 256 * half:256 * half + 256]
                t = D(partial(nc.vector.tensor_scalar, o, seq(bf[0:4, :], half), bias(2 * d + 1), None,
                                                                ALU.add), pf)
            give(bi, t)
            give(bf, t)
            a = A(partial(nc.scalar.activation, t1_, gf, ACT.Abs), t)
            a = A(partial(nc.scalar.activation, t1_, t1_, ACT.Exp, scale=-1.0), a)
            t = D(partial(nc.vector.tensor_scalar, t1_, t1_, 1.0, None, ALU.add), a)
            a = A(partial(nc.scalar.activation, t1_, t1_, ACT.Ln), t)
            t = D(partial(nc.vector.tensor_scalar, gf, gf, 0.0, None, ALU.min), a)
            t = D(partial(nc.vector.tensor_tensor, gf, gf, t1_, ALU.subtract), a, t)
            t = D(partial(nc.vector.tensor_tensor_scan, t2_, ONE, gf, 0.0, ALU.mult, ALU.add), t)
            t = D(partial(nc.vector.tensor_tensor, gi, gi, t2_, ALU.subtract), t)
            t = D(partial(nc.vector.tensor_tensor_scan, t1_, gi, gi, 0.0, ALU.max, ALU.max), t)
            t = D(partial(nc.vector.tensor_tensor, t2_, t2_, t1_, ALU.add), t)
            rw = gf
            mseg, eseg, cseg = t1_[:, 256:512], t2_[:, 256:512], gi
            t = D(partial(nc.vector.tensor_scalar, rw[:, 0:256], mseg[:, ::-1] if d else mseg, -1.0, None, ALU.mult), t)
            a = A(partial(nc.scalar.activation, rw[:, 256:512], eseg[:, ::-1] if d else eseg, ACT.Exp, scale=-1.0), t)
            t = D(partial(nc.vector.tensor_copy, c_n[:, 256:512], gi[:, 255::-1] if d else gi[:, 0:256]), t)
            t = D(partial(nc.vector.tensor_copy, c_n[:, 0:256], gi[:, 256:512][:, ::-1] if d else gi[:, 256:512]), t)
            b = take()
            for tb in range(4):
                p = P(partial(nc.tensor.transpose, b[:, 4 * tb:4 * tb + 4], c_n[:, 128 * tb:128 * tb + 128],
                                                        eye[0:4, 0:4]), t, *b.free)
            o = cT[:, 16 * d:16 * d + 16]
            t = D(partial(nc.vector.tensor_copy, o, b[:, 0:16]), p)
            give(b, t)
            dirs.append((rw, a, t))

        def head_norm_rope(dst, n, b, p, g, i):
            c = A(partial(nc.scalar.activation, dst[:, 0:n], b[:, 0:n], ACT.Copy), p)
            give(b, c)
            r = stats(lambda _: dst[:, 0:n], 1, 0, n, cst("blk64"), 64.0, c)
            t = D(partial(nc.vector.scalar_tensor_tensor, out=dst[:, 0:n], in0=dst[:, 0:n], scalar=g, in1=RSTD[:, 0:n],
                                                   op0=ALU.mult, op1=ALU.mult), r)
            b2 = take()
            p2 = mm(b2[:, 0:256], cst("perm2"), dst[:, 0:256], True, True, t, *b2.free)
            t = D(partial(nc.vector.tensor_tensor, rt[i], b2[:, 0:256], cst("sin2"), ALU.mult), p2, D.last)
            give(b2, t)
            t2 = D(partial(nc.vector.tensor_tensor, dst[:, 0:256], dst[:, 0:256], cst("cos2"), ALU.mult), t)
            return D(partial(nc.vector.tensor_tensor, dst[:, 0:256], dst[:, 0:256], rt[i], ALU.add), t2)

        pend = []
        for i in range(2):
            w = load(w2[8 + i])
            for j in range(2):
                b, p = project(w, j, lambda k: H[:, k, 0:256], 256, hm)
                pend.append((q_a[:, 2 * i + j, :], 256, b, p, par("qg")))
                if len(pend) > 1:
                    qa_ok = head_norm_rope(*pend.pop(0), j)
            w.done = P.last
        w = load(w2[10])
        b, p = project(w, 0, lambda k: H[:, k, :], 512, hm)
        pend.append((k_a, 512, b, p, par("kg")))
        qa_ok = head_norm_rope(*pend.pop(0), 0)
        b = take()
        for tb in range(4):
            p = token_rows(w, tb, hm, 128, 256, b=b, at=128 * tb)
        w.done = P.last
        vt_ok = A(partial(nc.scalar.activation, v_t, b[:, :].rearrange("p (b c) -> p b c", b=4), ACT.Copy), p)
        give(b, vt_ok)
        ka_ok = head_norm_rope(*pend.pop(0), 1)

        fill = []

        def proj_m(dst, tile, j, T, fn, key, hold={}):
            def go():
                if j == 0:
                    hold["w"] = load(w2[tile])
                w = hold["w"]
                b, p = project(w, j, lambda k: H[:, k, 0:T], T, hm)
                w.done = p
                t = fn(dst, b[:, 0:T], p)
                give(b, t)
                marks[key] = t
            return go

        marks = {}

        def dcopy(dst, src, p):
            return D(partial(nc.vector.tensor_copy, dst, src), p)

        def acopy(dst, src, p):
            return A(partial(nc.scalar.activation, dst, src, ACT.Copy), p)

        for c in range(4):
            fill.append(proj_m(q_m[:, c, :], c // 2, c % 2, 256, dcopy, ("q", c)))
        for c in range(4):
            fill.append(proj_m(k_m[:, c, :], 2 + c // 2, c % 2, 512, dcopy, ("k", c)))

        def rows_v(i, half, hold={}):
            def go():
                if half == 0:
                    hold["w"] = load(w2[4 + i])
                w = hold["w"]
                b = take()
                for tb in (2 * half, 2 * half + 1):
                    p = token_rows(w, tb, hm, b=b, at=256 * (tb % 2))
                w.done = p
                t = D(partial(nc.vector.tensor_copy, v_m[:, 2 * half:2 * half + 2, 256 * i:256 * i + 256],
                                              b[:, :].rearrange("p (b c) -> p b c", b=2)), p)
                give(b, t)
                marks[("v", i, half)] = t
            return go

        for i in range(2):
            for half in range(2):
                fill.append(rows_v(i, half))
        for c in range(4):
            fill.append(proj_m(o_g[:, c, :], 6 + c // 2, c % 2, 256, acopy, ("o", c)))

        SC2 = 64 ** -0.5
        units = [(c, kv, qb) for c in range(4) for kv in range(2) for qb in range(2)]
        state = {}
        ring_free = {}
        sinkb = par("sink")

        def scores2(n):
            c, kv, qb = units[n]
            r = 64 * kv
            b = take()
            p = P(partial(nc.tensor.matmul, b[:, :], q_a[r:r + 64, c, 128 * qb:128 * qb + 128], k_a[r:r + 64, :],
                                     start=True, stop=True, tile_position=(r, 0)), qa_ok, ka_ok, *b.free)
            edge = b[:, 128:256] if qb == 0 else b[:, 0:128]
            t = D(partial(nc.vector.tensor_tensor, edge, edge, cst("win", 128 * qb, 128 * qb + 128), ALU.add), p)
            i = n % 3
            x0 = 8 * i
            mx, sm_, es, rc = (st[:, x0 + z:x0 + z + 1] for z in range(4))
            h = c + 4 * kv
            sk = sinkb[:, h:h + 1]
            t = D(partial(nc.vector.tensor_reduce, mx, b[:, :], AX_X, ALU.max), t, ring_free.get(("st", i)))
            t = D(partial(nc.vector.scalar_tensor_tensor, out=mx, in0=mx, scalar=SC2, in1=sk, op0=ALU.mult, op1=ALU.max), t)
            t = D(partial(nc.vector.tensor_scalar, mx, mx, -1.0, None, ALU.mult), t)
            pr = prob[i]
            A(partial(nc.scalar.activation, pr, b[:, :], ACT.Exp, bias=mx, scale=SC2, accum_out=sm_), t,
              ring_free.get(("prob", i)))
            a = A(partial(nc.scalar.activation, es, sk, ACT.Exp, bias=mx), t)
            give(b, a)
            t = D(partial(nc.vector.tensor_tensor, rc, sm_, es, ALU.add), a)
            t = D(partial(nc.vector.reciprocal, rc, rc), t)
            t = D(partial(nc.vector.tensor_scalar, pr, pr, rc, None, ALU.mult), t)
            ring_free[("st", i)] = t
            state[n] = t

        def apply2(n):
            c, kv, qb = units[n]
            b = take()
            i = n % 3
            for kc in range(4):
                p = P(partial(nc.tensor.transpose, b[:, 128 * kc:128 * kc + 128],
                                                   prob[i][:, 128 * kc:128 * kc + 128], eye), state[n], *b.free)
            ring_free[("prob", i)] = p
            at = attT[n % 2]
            a = A(partial(nc.scalar.activation, at, b[:, :], ACT.Copy), p, ring_free.get(("attT", n % 2)))
            give(b, a)
            b2 = take()
            r = 64 * kv
            for kc in range(4):
                p = mm(b2[r:r + 64, 0:128], v_t[:, kc, 64 * kv:64 * kv + 64], at[:, 128 * kc:128 * kc + 128],
                       kc == 0, kc == 3, a, vt_ok, *b2.free)
            ring_free[("attT", n % 2)] = p
            t = D(partial(nc.vector.tensor_copy, a_T[r:r + 64, c, 128 * qb:128 * qb + 128], b2[r:r + 64, 0:128]), p)
            give(b2, t)

        scores2(0)
        scores2(1)
        for n in range(16):
            if fill:
                fill.pop(0)()
            apply2(n)
            if n + 2 < 16:
                scores2(n + 2)
        while fill:
            fill.pop(0)()
        a_ok = D.last
        for c in range(4):
            og_ok = A(partial(nc.scalar.activation, o_g[:, c, :], o_g[:, c, :], ACT.Sigmoid), marks[("o", c)])

        SM2 = 128 ** -0.5
        pp_free = [None, None]
        rb_free = [None, None]
        dd_free = [None] * 3
        nd = 0
        mt_ok = []

        def lstm_scores(h):
            sbk = [take(), take()]
            for tb in range(4):
                b = sbk[tb // 2]
                p = mm(b[:, 256 * (tb % 2):256 * (tb % 2) + 256], k_m[:, h, 128 * tb:128 * tb + 128], q_m[:, h, :],
                       True, True, marks[("k", h)], marks[("q", h)], *b.free)
            return sbk, p

        nxt_s = lstm_scores(0)
        for h in range(4):
            sbk, ps_ = nxt_s
            for d in range(2):
                rw, ra, ct = dirs[d]
                b = take()
                p = mm(b[:, :], cst("sel", 128 * h, 128 * h + 128)[0:4, :], rw, True, True, ra, D.last, *b.free)
                rb = RB[d]
                a = A(partial(nc.scalar.activation, rb, b[:, :], ACT.Copy), p, rb_free[d])
                give(b, a)
                pp = PP[d]
                for tb in range(4):
                    dd = DD[nd % 3]
                    cc = cT[:, 16 * d + 4 * tb + h:16 * d + 4 * tb + h + 1]
                    t = D(partial(nc.vector.tensor_scalar, dd, rb[:, 0:256], cc, 0.0, ALU.add, ALU.min), a, ct,
                          dd_free[nd % 3])
                    ax = A(partial(nc.scalar.activation, dd, dd, ACT.Exp), t)
                    o = pp[:, 256 * tb:256 * tb + 256]
                    s = sbk[tb // 2][:, 256 * (tb % 2):256 * (tb % 2) + 256]
                    t = D(partial(nc.vector.scalar_tensor_tensor, out=o, in0=s, scalar=SM2, in1=dd,
                                                                           op0=ALU.mult, op1=ALU.mult), ax, ps_,
                          pp_free[d])
                    dd_free[nd % 3] = t
                    nd += 1
                    if tb < 2:
                        mk = cst("cb" if d else "cf", 256 * tb, 256 * tb + 256)
                        t = D(partial(nc.vector.tensor_tensor, o, o, mk, ALU.mult), t)
                if d == 1:
                    for b_ in sbk:
                        give(b_, t)
                if d == 0 and h < 3:
                    nxt_s = lstm_scores(h + 1)
                b = take()
                for which, c0 in (("num", 0), ("den", 256)):
                    for tb in range(4):
                        lhs = v_m[:, tb, 128 * h:128 * h + 128] if which == "num" else ones
                        p = mm(b[:, c0:c0 + 256], lhs, pp[:, 256 * tb:256 * tb + 256], tb == 0, tb == 3, t,
                               marks[("v", h // 2, 1)], *b.free)
                pp_free[d] = p
                tm = tmp[d]
                ab_ = A(partial(nc.scalar.activation, tm, b[:, 256:512], ACT.Abs), p, D.last)
                t = D(partial(nc.vector.tensor_tensor, tm, tm, rb[:, 256:512], ALU.max), ab_)
                rb_free[d] = t
                t = D(partial(nc.vector.reciprocal, tm, tm), t)
                hd = hs[d]
                t = D(partial(nc.vector.tensor_tensor, hd, tm, b[:, 0:256], ALU.mult), t)
                give(b, t)
            t = D(partial(nc.vector.tensor_tensor, hs[0], hs[0], hs[1], ALU.add), t)
            r = stats(lambda _: hs[0], 1, 0, 256, ones, 128.0, t)
            t = D(partial(nc.vector.scalar_tensor_tensor, out=hs[0], in0=hs[0], scalar=par("mng", h, h + 1),
                                                        in1=RSTD[:, 0:256], op0=ALU.mult, op1=ALU.mult), r)
            t = D(partial(nc.vector.tensor_tensor, m_T[:, h, :], hs[0], o_g[:, h, :], ALU.mult), t, og_ok)
            mt_ok.append(t)

        gsb = [prob[0][:, 0:256], prob[0][:, 256:512], prob[1][:, 0:256], prob[1][:, 256:512]]
        g_free = [None] * 4
        for i in range(4):
            wm, wa, wb = load(w2[11 + i]), load(w2[15 + i]), load(ins["wbr2"][i])
            for j in range(2):
                m = 2 * i + j
                sg_ = []
                for z, w in ((0, wm), (1, wa)):
                    b, p = project(w, j, lambda k: H[:, k, 0:256], 256, hm)
                    if j:
                        w.done = p
                    gg = gsb[2 * j + z]
                    a = A(partial(nc.scalar.activation, gg, b[:, 0:256], ACT.Sigmoid), p, g_free[2 * j + z])
                    give(b, a)
                    sg_.append((gg, a))
                wt = wb.ap.rearrange("p (k m) -> p k m", k=8)
                b = take()
                for k in range(4):
                    mm(b[:, 0:256], wt[:, k, 128 * j:128 * j + 128], m_T[:, k, :], k == 0, k == 3, wb.ready,
                       mt_ok[k], *b.free)
                for k in range(4):
                    p = mm(b[:, 256:512], wt[:, 4 + k, 128 * j:128 * j + 128], a_T[:, k, :], k == 0, k == 3, a_ok)
                wb.done = p
                o = MG[:, m, :]
                t1_ = D(partial(nc.vector.tensor_tensor, o, sg_[0][0], b[:, 0:256], ALU.mult), p, sg_[0][1])
                t2_ = D(partial(nc.vector.tensor_tensor, sg_[1][0], sg_[1][0], b[:, 256:512], ALU.mult), sg_[1][1])
                give(b, t2_)
                t = D(partial(nc.vector.tensor_tensor, o, o, sg_[1][0], ALU.add), t1_, t2_)
                g_free[2 * j] = g_free[2 * j + 1] = t
        mg_ok = D.last
        for i in range(4):
            w = load(ins["wout2"][i])
            for j in range(2):
                b, p = project(w, j, lambda k: MG[:, k, :], 256, [mg_ok] * 8)
                x_ready = residual(b, 2 * i + j, 2, [0], p)
            w.done = P.last

        hm = modulated(1, 3, [0], x_ready)
        fence()
        ar = Arena(0)
        q_p = ar(4096).rearrange("p (j t) -> p j t", j=16)
        S = ar(2048)
        S2 = ar(2048)
        W1, W2 = ar(2048), ar(2048)
        top = ar(256).rearrange("p (j k) -> p j k", k=16)
        tid = ar(256).rearrange("p (j k) -> p j k", k=16)
        tidf = ar(256)
        ctop = ar(128)
        cpos = ar(128)
        ca, cb_ = ar(128), ar(128)
        gsm = ar(128)
        gs = ar(16)
        idA, idB = ar(128), ar(128)
        for i in range(8):
            w = load(ins["wq2"][i])
            for j in range(2):
                b, p = project(w, j, lambda k: H[:, k, 0:256], 256, hm)
                c = 2 * i + j
                a = A(partial(nc.scalar.activation, q_p[:, c, :], b[:, 0:256], ACT.Copy), p)
                give(b, a)
            w.done = P.last
        wk = load(ins["keys2"])
        HC = [HT[:, 512 * i + 256:512 * i + 512] for i in range(8)]
        XC = [XT[:, 512 * i + 256:512 * i + 512] for i in range(8)]
        iAT, iBT, gT = HC[0], HC[1], HC[2]
        NEG = -3.0e38
        for tb in range(2):
            free_s = D.last
            for q4 in range(4):
                b = take()
                for z in range(4):
                    c = 4 * q4 + z
                    p = mm(b[:, 128 * z:128 * z + 128], q_p[:, c, 128 * tb:128 * tb + 128],
                           wk.ap[:, 128 * c:128 * c + 128], True, True, a, wk.ready, *b.free)
                sv = S[:, 512 * q4:512 * q4 + 512]
                ac = A(partial(nc.scalar.activation, sv, b[:, :], ACT.Copy), p, free_s)
                give(b, ac)
            wk.done = P.last
            for c in range(16):
                sv = S[:, 128 * c:128 * c + 128]
                s2 = S2[:, 128 * c:128 * c + 128]
                v0, v1 = top[:, c, 0:8], top[:, c, 8:16]
                i0, i1 = tid[:, c, 0:8].bitcast(U32), tid[:, c, 8:16].bitcast(U32)
                t = D(partial(nc.vector.max, v0, sv), ac, free_s)
                D(partial(nc.vector.max_index, i0, v0, sv), t)
                t = D(partial(nc.vector.match_replace, s2, v0, sv, NEG), t)
                t = D(partial(nc.vector.max, v1, s2), t)
                t = D(partial(nc.vector.max_index, i1, v1, s2), t)
            ti = tid.rearrange("p j k -> p (j k)").bitcast(U32)
            t_ids = D(partial(nc.vector.tensor_copy, tidf, ti), t)
            hp = top.rearrange("p (h z) k -> p h z k", z=2)
            for h in range(8):
                o = W1[:, 256 * h:256 * h + 256].rearrange("p (a b) -> p a b", b=16)
                s1b = top[:, 2 * h, :].rearrange("p (a o) -> p a o", o=1).to_broadcast([128, 16, 16])
                s2b = top[:, 2 * h + 1, :].rearrange("p (o b) -> p o b", o=1).to_broadcast([128, 16, 16])
                t = D(partial(nc.vector.tensor_tensor, o, s1b, s2b, ALU.add), t)
                sv, s2 = W1[:, 256 * h:256 * h + 256], W2[:, 256 * h:256 * h + 256]
                v0, v1 = ctop[:, 16 * h:16 * h + 8], ctop[:, 16 * h + 8:16 * h + 16]
                i0, i1 = (cpos[:, 16 * h + 8 * z:16 * h + 8 * z + 8].bitcast(U32) for z in range(2))
                t = D(partial(nc.vector.max, v0, sv), t)
                D(partial(nc.vector.max_index, i0, v0, sv), t)
                t = D(partial(nc.vector.match_replace, s2, v0, sv, NEG), t)
                t = D(partial(nc.vector.max, v1, s2), t)
                t = D(partial(nc.vector.max_index, i1, v1, s2), t)
            c3 = ctop.rearrange("p (h k) -> p h k", k=16)
            g3 = gsm.rearrange("p (h k) -> p h k", k=16)
            tg = D(partial(nc.vector.tensor_tensor, g3, c3, c3[:, :, 0:1].to_broadcast([128, 8, 16]), ALU.subtract), t)
            ag = A(partial(nc.scalar.activation, gsm, gsm, ACT.Exp), tg)
            cp = cpos.bitcast(U32)
            cau, cbu = ca.bitcast(U32), cb_.bitcast(U32)
            t = D(partial(nc.vector.tensor_scalar, cau, cp, 4, None, ALU.logical_shift_right), t)
            t1_ = D(partial(nc.vector.tensor_scalar, cbu, cp, 15, None, ALU.bitwise_and), t)
            fa, fb = W2[:, 0:128], W2[:, 128:256]
            t = D(partial(nc.vector.tensor_copy, fa, cau), t1_)
            t = D(partial(nc.vector.tensor_copy, fb, cbu), t)
            for z, f, idx in ((0, fa, idA), (1, fb, idB)):
                e3 = W1.rearrange("p (a j) -> p a j", j=16)
                e4 = W1.rearrange("p (h k j) -> p h k j", k=16, j=16)
                fo = f.rearrange("p (a o) -> p a o", o=1).to_broadcast([128, 128, 16])
                io = iota[:, 0:16].rearrange("p (o j) -> p o j", o=1).to_broadcast([128, 128, 16])
                t = D(partial(nc.vector.tensor_tensor, e3, fo, io, ALU.is_equal), t, t_ids)
                src = tidf.rearrange("p (h z j) -> p h z j", z=2, j=16)[:, :, z:z + 1, :].to_broadcast([128, 8, 16, 16])
                t = D(partial(nc.vector.tensor_tensor, e4, e4, src, ALU.mult), t)
                t = D(partial(nc.vector.tensor_reduce, idx, e3, AX_X, ALU.add), t)
            tg = D(partial(nc.vector.tensor_reduce, gs[:, 0:8], g3, AX_X, ALU.add), ag)
            tg = D(partial(nc.vector.reciprocal, gs[:, 8:16], gs[:, 0:8]), tg)
            tg = D(partial(nc.vector.tensor_tensor, g3, g3, gs[:, 8:16].rearrange("p (h o) -> p h o", o=1)
                                             .to_broadcast([128, 8, 16]), ALU.mult), tg)
            b = take()
            for z, v in enumerate((idA, idB, gsm)):
                p = P(partial(nc.tensor.transpose, b[:, 128 * z:128 * z + 128], v, eye), t, tg, *b.free)
            for z, v in enumerate((iAT, iBT, gT)):
                o = v[:, 128 * tb:128 * tb + 128]
                t = D(partial(nc.vector.tensor_copy, o, b[:, 128 * z:128 * z + 128]), p)
            give(b, t)

        fence()
        GG = R[:, :].rearrange("p (a t) -> p a t", a=128)
        oh = [(XC[i], XC[4 + i]) for i in range(4)]
        oh_free = [None] * 4
        for q in range(64):
            b = take()
            for z in range(2):
                i = (2 * q + z) % 4
                oa, ob = oh[i]
                for y in range(2):
                    tk = 4 * q + 2 * z + y
                    o1, o2 = oa[:, 128 * y:128 * y + 128], ob[:, 128 * y:128 * y + 128]
                    ia, ib, gg = iAT[:, tk:tk + 1], iBT[:, tk:tk + 1], gT[:, tk:tk + 1]
                    D(partial(nc.vector.tensor_scalar, o1, iota, ia, None, ALU.is_equal), oh_free[i])
                    t = D(partial(nc.vector.tensor_scalar, o2, iota, ib, gg, ALU.is_equal, ALU.mult),
                          oh_free[i])
                for y in range(2):
                    o1, o2 = oa[:, 128 * y:128 * y + 128], ob[:, 128 * y:128 * y + 128]
                    c0 = 128 * (2 * z + y)
                    p = mm(b[:, c0:c0 + 128], o2, o1, True, True, t, *b.free)
                oh_free[i] = p
            dst = GG[:, :, 4 * q:4 * q + 4].rearrange("p a t -> p t a")
            a = A(partial(nc.scalar.activation, dst, b[:, :].rearrange("p (t a) -> p t a", t=4), ACT.Copy), p)
            give(b, a)
        fence()
        yb = [take() for _ in range(4)]
        ab = [take() for _ in range(3)]
        actb = [XC[i] for i in range(4)]
        act_free = [None] * 4
        U2, V2 = ins["ut2"], ins["v2"]
        tu = {}
        tv = {}
        wact = {}

        def up(a_):
            if a_ % 2 == 0:
                tu[a_ // 2] = load(U2[a_ // 2])
                tv[a_ // 2] = load(V2[a_ // 2])
            w = tu[a_ // 2]
            wt = w.ap.rearrange("p (k m) -> p k m", k=8)
            b = ab[a_ % 3]
            j = a_ % 2
            for k in range(8):
                p = mm(b[:, 0:256], wt[:, k, 128 * j:128 * j + 128], H[:, k, 0:256], k == 0, k == 7, w.ready, *b.free)
            w.done = p
            o = actb[a_ % 4]
            t = A(partial(nc.scalar.activation, o, b[:, 0:256], ACT.Gelu_apprx_tanh), p, act_free[a_ % 4])
            b.release(t)
            wact[a_] = D(partial(nc.vector.tensor_tensor, o, o, GG[:, a_, :], ALU.mult), t)

        def down(a_):
            w = tv[a_ // 2]
            wt = w.ap.rearrange("p (e d) -> p e d", e=2)
            o = actb[a_ % 4]
            for m in range(8):
                b = yb[m // 2]
                last = m == 7
                P(partial(nc.tensor.matmul, b[:, 256 * (m % 2):256 * (m % 2) + 256],
                                               wt[:, a_ % 2, 128 * m:128 * m + 128], o,
                                               start=(a_ == 0 and m % 2 == 0), stop=(a_ == 127),
                                               skip_group_check=True),
                  w.ready, wact[a_], *b.free, inc=last)
            w.done = P.last
            act_free[a_ % 4] = P.last

        up(0)
        for a_ in range(128):
            if a_ < 127:
                up(a_ + 1)
            down(a_)
        pl = P.last
        for b in ab:
            give(b, *b.free)
        outs = [HT[:, 1024 * i:1024 * i + 1024] for i in range(2)]
        for m in range(8):
            i = yb[m // 2][:, 256 * (m % 2):256 * (m % 2) + 256]
            o = X[:, m, 0:256]
            t = D(partial(nc.vector.scalar_tensor_tensor, out=o, in0=i, scalar=adac(5, m, 0), in1=o,
                                                                  op0=ALU.mult, op1=ALU.add), pl)
        out_marks = []
        for tb in range(2):
            for half in range(2):
                b = take()
                for z in range(4):
                    m = 4 * half + z
                    p = P(partial(nc.tensor.transpose, b[:, 128 * z:128 * z + 128],
                                                                     X[:, m, 128 * tb:128 * tb + 128], eye),
                          t, *b.free)
                o = outs[tb][:, 512 * half:512 * half + 512]
                a = A(partial(nc.scalar.activation, o, b[:, :], ACT.Copy), p)
                give(b, a)
            out_marks.append(a)

        block = ctx.enter_context(nc.Block())

        @block.sync
        def _(e):
            e.dma_start(PT[:, :], ins["par"]).then_inc(s_in, 16)
            e.dma_start(XT[:, :], ins["xt"]).then_inc(s_in, 16)
            e.dma_start(R[:, 0:NCST], ins["cst"]).then_inc(s_in, 16)
            e.dma_start(R[:, NCST:NCST + 1024], ins["wst"]).then_inc(s_in, 16)
            c2 = [False]
            for i, t in enumerate(tiles):
                if i >= NRING:
                    dn = tiles[i - NRING].done
                    if not c2[0] and dn[1] > x2_free[1]:
                        e.wait_ge(x2_free[0], x2_free[1])
                        e.wait_ge(x2_free_d[0], x2_free_d[1])
                        e.dma_start(X[:, :, 256:512], ins["ctx2t"].rearrange("p (k t) -> p k t", k=8))\
                            .then_inc(s_c2, 16)
                        c2[0] = True
                    e.wait_ge(dn[0], dn[1])
                e.dma_start(t.ap, t.src).then_inc(s_ring[t.slot], 16)
            for tb in range(2):
                e.wait_ge(out_marks[tb][0], out_marks[tb][1])
                e.dma_start(out[0, 128 * tb:128 * tb + 128, :], outs[tb]).then_inc(s_out, 16)
            e.wait_ge(s_out, 32)

        @block.tensor
        def _(e):
            P.play(e)

        @block.vector
        def _(e):
            D.play(e)

        @block.scalar
        def _(e):
            A.play(e)

        @block.gpsimd
        def _(e):
            G.play(e)


def _cols(v):
    return np.ascontiguousarray(v.reshape(-1, 128).T)


def _tiles(w, cols=256):
    k, n = w.shape
    return np.ascontiguousarray(w.reshape(k // 128, 128, n // cols, cols).transpose(2, 1, 0, 3)
                                .reshape(n // cols, 128, (k // 128) * cols))


def _constants():
    c = np.zeros((128, NCST), np.float32)

    def put(name, v):
        at, n = CST[name]
        c[:v.shape[0], at:at + n] = v.reshape(v.shape[0], n)

    p = np.arange(128)
    put("blk64", (p[:, None] // 64 == p[None, :] // 64).astype(np.float32))
    t = np.arange(256)
    row, col = (t // 64).astype(np.float32), (t % 64).astype(np.float32)
    d = p % 32
    j = d % 16
    perm = np.zeros((128, 128), np.float32)
    perm[np.where(j < 8, p + 8, p - 8), p] = np.where(j < 8, -1.0, 1.0)
    put("perm1", perm)
    inv = (np.float32(10000.0) ** (-np.arange(0, 16, 2, dtype=np.float32) / np.float32(16))).astype(np.float32)
    ang = np.where((d // 16 == 0)[:, None], row[None, :], col[None, :]) * inv[j % 8][:, None]
    put("cos1", np.cos(ang.astype(np.float32)))
    put("sin1", np.sin(ang.astype(np.float32)))
    d = p % 64
    perm = np.zeros((128, 128), np.float32)
    perm[np.where(d < 32, p + 32, p - 32), p] = np.where(d < 32, -1.0, 1.0)
    put("perm2", perm)
    inv = (np.float32(10000.0) ** (-np.arange(16, dtype=np.float32) / np.float32(16))).astype(np.float32)
    i = d % 32
    ang = np.where((i < 16)[:, None], row[None, :], col[None, :]) * inv[i % 16][:, None]
    put("cos2", np.cos(ang.astype(np.float32)))
    put("sin2", np.sin(ang.astype(np.float32)))
    n = np.arange(256)
    th = 2 * np.pi * ((n[:, None] * n[None, :]) % 256) / 256
    cs = np.concatenate([np.cos(th), np.sin(th)], axis=1) / 16
    put("dftn", cs.reshape(2, 128, 512).transpose(1, 0, 2).reshape(128, 1024).astype(np.float32))
    n = np.arange(64)
    th = 2 * np.pi * ((n[:, None] * n[None, :]) % 64) / 64
    z = np.zeros((128, 128))
    z[:64, :64] = z[64:, 64:] = np.cos(th) / 8
    put("cd", z.astype(np.float32))
    z = np.zeros((128, 128))
    z[:64, :64] = z[64:, 64:] = -np.sin(th) / 8
    put("sd", z.astype(np.float32))
    s = 128 * np.arange(2)[None, :, None] + p[:, None, None]
    put("cf", (t[None, None, :] >= s).astype(np.float32).reshape(128, 512))
    put("cb", (t[None, None, :] <= s).astype(np.float32).reshape(128, 512))
    q, k = p[:, None], p[None, :]
    win = np.concatenate([np.where(k + 128 - q <= 128, 0.0, -1e30), np.where(q + 128 - k <= 128, 0.0, -1e30)], axis=1)
    put("win", win.astype(np.float32))
    sel = np.zeros((4, 4, 128), np.float32)
    for r in range(4):
        sel[r, r, :] = 1.0
    put("sel", sel.reshape(4, 512))
    return c


def kernel(**inputs):
    import concourse.bacc as _bacc
    from concourse.bass_utils import run_bass_kernel_spmd as _run

    v = {k: np.asarray(a) for k, a in inputs.items()}
    pa = np.zeros((128, NPAR), np.float32)

    def put(name, a):
        at, n = PAR[name]
        pa[:a.shape[0], at:at + n] = a.reshape(a.shape[0], n)

    put("eye", np.eye(128, dtype=np.float32))
    put("ones", np.ones((128, 128), np.float32))
    put("iota", np.tile(np.arange(128, dtype=np.float32), (128, 1)))
    put("c1", np.stack([_cols(v["c"][0]), _cols(v["c_ctx"])], axis=2))
    put("c2", np.stack([_cols(v["c_2"][0]), _cols(v["c_ctx_2"])], axis=2))
    put("finalg", _cols(v["final_g"]))
    for l in range(DEPTH):
        put(f"bada{l}", _cols(v["b_ada"][l]))
        put(f"n1g{l}", _cols(v["norm1_g"][l]))
        put(f"n2g{l}", _cols(v["norm2_g"][l]))
        put(f"sconv{l}", v["sconv_w"][l].reshape(3, 2, 128).transpose(2, 1, 0))
        put(f"subln{l}", np.concatenate([v["subln_g"][l]] * 2)[:, None])
        put(f"fconv{l}", v["ffn_conv_w"][l].reshape(3, 22, 128).transpose(2, 1, 0))
        put(f"lam{l}", np.stack([v[n][l] for n in ("lambda_q1", "lambda_q2", "lambda_k1", "lambda_k2")], axis=1))
        put(f"bs{l}", np.repeat(v["gmlp_bs"][l].reshape(2, 2, 1, 128), 64, axis=2).reshape(2, 128, 128)
            .transpose(1, 0, 2))
    put("bada2", _cols(v["b_ada_2"][0]))
    put("n1g2", _cols(v["norm_mix_g_2"][0]))
    put("n2g2", _cols(v["norm_ffn_g_2"][0]))
    put("gbias", v["b_mgates_2"][0].reshape(4, 4).T)
    put("mng", _cols(v["mlstm_norm_g_2"][0]))
    put("qg", np.concatenate([v["attn_q_norm_g_2"][0]] * 2)[:, None])
    put("kg", np.concatenate([v["attn_k_norm_g_2"][0]] * 2)[:, None])
    put("sink", np.tile(v["attn_sink_2"][0], (128, 1)))

    def toks(a):
        return a.reshape(256, 8, 128).transpose(2, 1, 0)

    arr = {"par": pa, "cst": _constants()}
    arr["xt"] = np.concatenate([toks(v["x"][0]), toks(v["ctx"][0])], axis=2).reshape(128, 4096)
    arr["ctx2t"] = toks(v["ctx_2"][0]).reshape(128, 2048)
    arr["wst"] = v["gmlp_ws"].transpose(3, 0, 1, 2).reshape(128, 1024)
    for l in range(DEPTH):
        arr[f"wada{l}"] = _tiles(v["w_ada"][l])
        arr[f"win{l}"] = _tiles(v["w_in"][l])
        arr[f"wout{l}"] = _tiles(v["w_out"][l])
        arr[f"wup{l}"] = _tiles(v["ffn_w_up"][l])
        arr[f"wdn{l}"] = v["ffn_w_down"][l].reshape(2, 11, 128, 8, 128).transpose(3, 0, 2, 1, 4).reshape(16, 128, 1408)
    arr["wada2"] = _tiles(v["w_ada_2"][0])
    w = v["w_in_2"][0]
    qo = np.concatenate([np.arange(64 * h, 64 * h + 64) for c in range(4) for h in (c, c + 4)])
    arr["win2"] = _tiles(np.concatenate([w[:, 0:2048], w[:, 2064:2576][:, qo], w[:, 2576:]], axis=1))
    arr["wg2"] = w[:, 2048:2064].reshape(8, 128, 16).transpose(1, 0, 2).reshape(128, 128)
    arr["wbr2"] = _tiles(np.concatenate([v["w_branch_m_2"][0], v["w_branch_a_2"][0][qo]], axis=0))
    arr["wout2"] = _tiles(v["w_out_2"][0])
    arr["wq2"] = _tiles(v["peer_w_query_2"][0])
    arr["keys2"] = v["peer_sub_keys_2"][0].reshape(16, 128, 128).transpose(2, 0, 1).reshape(128, 2048)
    arr["ut2"] = np.ascontiguousarray(v["peer_u_2"][0].reshape(64, 256, 8, 128).transpose(0, 3, 2, 1)
                                      .reshape(64, 128, 2048))
    arr["v2"] = np.ascontiguousarray(v["peer_v_2"][0].reshape(64, 2, 128, 1024).transpose(0, 2, 1, 3)
                                     .reshape(64, 128, 2048))

    nc = _bacc.Bacc("TRN2", target_bir_lowering=False, num_devices=1)
    feeds, args = {}, {}
    for name, a in arr.items():
        a = np.ascontiguousarray(a)
        feeds[f"in_{name}"] = a
        args[name] = nc.dram_tensor(f"in_{name}", a.shape, mybir.dt.from_np(a.dtype), kind="ExternalInput").ap()
    out = nc.dram_tensor("out_0", (1, 256, 1024), F32, kind="ExternalOutput").ap()
    build(nc, args, out)
    r = _run(nc, [feeds], core_ids=[0])
    return r.results[0]["out_0"]
```

```python
import math
from contextlib import ExitStack
from functools import partial

import numpy as np
import concourse.bass as bass
from concourse import mybir

F32 = mybir.dt.float32
F32R = mybir.dt.float32r
U32 = mybir.dt.uint32
ALU = mybir.AluOpType
ACT = mybir.ActivationFunctionType
AX_X = mybir.AxisListType.X

DEPTH = 2
EPS = 1e-6
NRAW = 4
NSPLIT = 3
AHEAD = 2
TILE = 1024


class Lane:

    def __init__(self, sem):
        self.sem = sem
        self.ops = []
        self.n = 0
        self.seen = {}

    @property
    def last(self):
        return (self.sem, self.n)

    def wait(self, *marks):
        for m in marks:
            if m is None or m[1] == 0:
                continue
            if self.seen.get(m[0].name, 0) < m[1]:
                self.seen[m[0].name] = m[1]
                self.ops.append((None, m))

    def __call__(self, fn, *marks, inc=True):
        self.wait(*marks)
        if inc:
            self.n += 1
        self.ops.append((fn, inc))
        return self.last

    def play(self, eng):
        for fn, x in self.ops:
            if fn is None:
                eng.wait_ge(x[0], x[1])
            else:
                ins = fn()
                if x:
                    ins.then_inc(self.sem, 1)


class Bank:
    def __init__(self, t):
        self.t = t
        self.free = ()

    def __getitem__(self, at):
        return self.t[at]

    def release(self, *marks):
        self.free = marks


def _fields(spec):
    at, out = 0, {}
    for name, n in spec:
        out[name] = (at, n)
        at += n
    return out, at


PAR, NPAR = _fields(
    [("eye", 128), ("ones", 128), ("blk64", 128), ("iota", 128), ("sum2", 2), ("c1", 16), ("c2", 16), ("finalg", 8)]
    + [(f"{n}{l}", k) for l in range(DEPTH) for n, k in
       (("bada", 48), ("n1g", 8), ("n2g", 8), ("sconv", 6), ("subln", 1), ("fconv", 66), ("lam", 4), ("bs", 256))]
    + [("bada2", 48), ("n1g2", 8), ("n2g2", 8), ("gbias", 4), ("mng", 4), ("qg", 1), ("kg", 1), ("sink", 8)])

CST, NCST = _fields([("perm1", 128), ("cos1", 256), ("sin1", 256), ("dftn", 1024), ("cd", 128), ("sd", 128),
                     ("ws", 1024)])
CS2, NCS2 = _fields([("perm2", 128), ("cos2", 256), ("sin2", 256), ("cf", 512), ("cb", 512), ("win", 256),
                     ("sel", 512)])


def build(nc, ins, out):
    with ExitStack() as ctx:
        order = program(nc, ctx, ins, out, None)
    with ExitStack() as ctx:
        program(nc, ctx, ins, out, order)


def program(nc, ctx, ins, out, order):
    if True:
        def sb(name, n, dt=F32, at=ctx):
            return at.enter_context(nc.sbuf_tensor(name if order else name + "_", [128, n], dt))

        def sem(name):
            return ctx.enter_context(nc.semaphore(name if order else name + "_"))

        RAW = sb("RAW", NRAW * TILE)
        TH = sb("TH", NSPLIT * TILE, F32R)
        TL = sb("TL", NSPLIT * TILE, F32R)
        HXh = sb("HXh", 2048, F32R)
        HXl = sb("HXl", 2048, F32R)
        XX = sb("XX", 2048)
        PT = sb("P", NPAR)
        ADAS = [sb(f"ADA{i}", 96) for i in range(2)]
        MOD = sb("MOD", 64)
        SM = sb("SM", 56)
        CC = sb("CC", 32, F32R)
        early = ExitStack()
        XT = sb("X", 4096, at=early)
        HTh = sb("Hh", 4096, F32R, at=early)
        HTl = sb("Hl", 4096, F32R, at=early)
        CT = sb("C", NCST, at=early)
        X = XT[:, :].rearrange("p (k t) -> p k t", k=8)
        Hh = HTh[:, :].rearrange("p (k t) -> p k t", k=8)
        Hl = HTl[:, :].rearrange("p (k t) -> p k t", k=8)

        banks = [Bank(ctx.enter_context(nc.psum_tensor(f"ps{i}" if order else f"ps{i}_", [128, 512], F32))) for i in range(8)]
        ada_bank = banks.pop()
        idle = list(banks)

        def take():
            return idle.pop(0)

        def give(b, *marks):
            b.release(*marks)
            idle.append(b)

        P, D, A, G = (Lane(sem(f"s_{n}")) for n in ("pe", "dve", "act", "pool"))
        s_in = sem("s_in")
        s_c2 = sem("s_c2")
        s_out = sem("s_out")
        s_c = sem("s_c")
        s_ring = [sem(f"s_ring{i}") for i in range(NRAW)]

        def par(name, a=0, b=None):
            at, n = PAR[name]
            return PT[:, at + a:at + (n if b is None else b)]

        def cst(name, a=0, b=None):
            at, n = (CST if name in CST else CS2)[name]
            return CT[:, at + a:at + (n if b is None else b)]

        eye, ones, iota = par("eye"), par("ones"), par("iota")

        tiles = []

        class Tile:
            pass

        def arrive(i):
            t = Tile()
            t.src, t.n, split = order[i] if order else (None, TILE, True)
            t.raw = RAW[:, (i % NRAW) * TILE:(i % NRAW) * TILE + t.n]
            t.ready = (s_ring[i % NRAW], 16 * (i // NRAW + 1))
            t.slot = nsplit[0] % NSPLIT
            t.done = None
            t.freed = None
            tiles.append(t)
            if split:
                o = t.slot * TILE
                t.hi, t.lo = TH[:, o:o + t.n], TL[:, o:o + t.n]
                before = holders[t.slot]
                nsplit[0] += 1
                a = A(partial(nc.scalar.activation, t.hi, t.raw, ACT.Copy), t.ready, before and before.done)
                t.split = D(partial(nc.vector.tensor_tensor, t.lo, t.raw, t.hi.bitcast(F32), ALU.subtract), a)
                t.freed = t.split
                holders[t.slot] = t

        holders = [None] * NSPLIT
        nsplit = [0]
        asked = []

        def load(src, n=TILE, split=True):
            i = len(asked)
            asked.append((src, n, split))
            if order:
                assert order[i][1:] == (n, split)
            while len(tiles) <= min(i + (AHEAD if order else 0), len(order or asked) - 1):
                arrive(len(tiles))
            return tiles[i]

        loads_in = 16 * 3
        LOADED = (s_in, loads_in)

        def mm(o, l, r, first, last, *marks, skip=False, inc=None):
            return P(partial(nc.tensor.matmul, o, l, r, start=first, stop=last, skip_group_check=skip), *marks,
                     inc=last if inc is None else inc)

        def mm3(o, l, r, first, last, *marks, skip=False, inc=None):
            (lh, ll), (rh, rl) = l, r
            mm(o, lh, rl, first, False, *marks, skip=skip)
            mm(o, ll, rh, False, False, skip=skip)
            return mm(o, lh, rh, False, last, skip=skip, inc=last if inc is None else inc)

        def split_to(hi, lo, src, *marks):
            a = A(partial(nc.scalar.activation, hi, src, ACT.Copy), *marks)
            return D(partial(nc.vector.tensor_tensor, lo, src, hi.bitcast(F32), ALU.subtract), a, *marks)

        def fence():
            marks = [P.last, D.last, A.last, G.last]
            for lane in (P, D, A, G):
                lane.wait(*marks)

        def scratch(at, tag):
            count = [0]

            def new(n, dt=F32):
                count[0] += 1
                return sb(f"{tag}{count[0]}", n, dt, at)[:, :]
            return new

        base = scratch(early, "b")
        wsT = [cst("ws", 512 * l, 512 * l + 512) for l in range(DEPTH)]
        SQ = [base(512) for _ in range(3)]
        STD, RSTD = base(512), base(512)
        sq_free = [None] * 3
        sq_n = [0]
        sq_busy = [None] * 3

        epsc = SM[:, 0:1]
        d_eps = D(partial(nc.vector.memset, epsc, EPS))
        for lane in (P, D, A, G):
            lane.wait(LOADED)
        A.wait(d_eps)

        def stats(src, k, t0, t1, lhs, div, x_ready, free=None):
            n = t1 - t0
            b = take()
            for i in range(k):
                j = sq_n[0] % 3
                sq_n[0] += 1
                sq = SQ[j][:, 0:n]
                s = src(i)
                a = A(partial(nc.scalar.activation, sq, s, ACT.Square), x_ready, sq_free[j], sq_busy[j])
                sq_free[j] = mm(b[:, 0:n], lhs, sq, i == 0, i == k - 1, a, *b.free, inc=True)
            a = A(partial(nc.scalar.activation, STD[:, 0:n], b[:, 0:n], ACT.Sqrt, bias=epsc, scale=1.0 / div), P.last, D.last)
            give(b, a)
            return D(partial(nc.vector.reciprocal, RSTD[:, 0:n], STD[:, 0:n]), a, D.last, free)

        adaq = []
        SC = SM[:, 8:24]
        cur = [0]
        arow = base(512)
        arow_free = [None]

        def ada_begin(cname):
            cc = par(cname)
            t = A(partial(nc.scalar.activation, SC, cc, ACT.Silu), P.last, D.last)
            c4 = CC[:, :].rearrange("p (k h) -> p k h", h=2)
            hi, lo = c4[:, :, 0:1], c4[:, :, 1:2]
            s3 = SC.rearrange("p (k o) -> p k o", o=1)
            return split_to(hi, lo, s3, t)

        def ada_step(src, i, ready, bias, buf):
            def go():
                w = load(src[i])
                wh, wl = (v.rearrange("p (k m) -> p k m", k=8) for v in (w.hi, w.lo))
                o = ada_bank[0:4, 128 * (i % 4):128 * (i % 4) + 128]
                for k in range(8):
                    c = CC[:, 4 * k:4 * k + 4]
                    mm(o, c, wl[:, k, :], k == 0, False, w.split, ready, *ada_bank.free)
                    mm(o, c, wh[:, k, :], False, k == 7)
                w.done = P.last
                if i % 4 == 3:
                    g = i // 4
                    r = arow[0:4, :]
                    a = A(partial(nc.scalar.activation, r, ada_bank[0:4, :], ACT.Copy), P.last, arow_free[0])
                    ada_bank.release(a)
                    adaw.append((g, r, a, bias, buf))
                if i % 4 == 1 or i == 47:
                    ada_columns()
            return go

        adaw = []
        ada_got = {}

        def ada_columns():
            while adaw:
                g, r, a, bias, buf = adaw.pop(0)
                b = take()
                for z in range(4):
                    mm(b[:, 2 * z:2 * z + 2], r[:, 128 * z:128 * z + 128], par("sum2")[0:4, :], True, True, a, *b.free)
                p = P.last
                arow_free[0] = p
                o = ADAS[buf][:, 8 * g:8 * g + 8].rearrange("p (m c) -> p m c", c=2)
                bb = par(bias, 4 * g, 4 * g + 4).rearrange("p (m o) -> p m o", o=1).to_broadcast([128, 4, 2])
                t = D(partial(nc.vector.tensor_tensor, o, b[:, 0:8].rearrange("p (m c) -> p m c", c=2), bb, ALU.add), p)
                give(b, t)

        def background(n=1):
            for _ in range(n):
                if adaq:
                    adaq.pop(0)()

        def adac(part, m, s):
            return ADAS[cur[0]][:, (8 * part + m) * 2 + s:(8 * part + m) * 2 + s + 1]

        def mods(g, part, slot):
            o = MOD[:, 16 * slot:16 * slot + 16].rearrange("p (m c) -> p m c", c=2)
            s = ADAS[cur[0]][:, 16 * part:16 * part + 16].rearrange("p (m c) -> p m c", c=2)
            gg = par(g).rearrange("p (m o) -> p m o", o=1).to_broadcast([128, 8, 2])
            t = D(partial(nc.vector.tensor_scalar, o, s, 1.0, None, ALU.add), D.last, A.last)
            return D(partial(nc.vector.tensor_tensor, o, o, gg, ALU.mult), t)

        VT = SQ[0:2]
        vt_free = [None, None]

        def modulated(slot, shift, streams, x_ready, dst=None):
            t1 = 256 * len(streams)
            dh, dl = dst or (Hh, Hl)
            r = stats(lambda i: X[:, i, 0:t1], 8, 0, t1, ones, 1024.0, x_ready)
            marks = []
            h_free = P.last
            for k in range(8):
                v = VT[k % 2][:, 0:t1]
                t = D(partial(nc.vector.tensor_tensor, v, X[:, k, 0:t1], RSTD[:, 0:t1], ALU.mult), r,
                      vt_free[k % 2])
                for s in streams:
                    vs = v[:, 256 * s:256 * s + 256]
                    sc = MOD[:, 16 * slot + 2 * k + s:16 * slot + 2 * k + s + 1]
                    sh = adac(shift, k, s)
                    u = D(partial(nc.vector.tensor_scalar, vs, vs, sc, sh, ALU.mult, ALU.add), t)
                m = split_to(dh[:, k, 0:t1], dl[:, k, 0:t1], v, u, h_free)
                vt_free[k % 2] = sq_busy[k % 2] = m
                marks.append(m)
            return marks

        def residual(b, m, gate, streams, last_p):
            for s in streams:
                o = X[:, m, 256 * s:256 * s + 256]
                i = b[:, 256 * s:256 * s + 256]
                t = D(partial(nc.vector.scalar_tensor_tensor, out=o, in0=i, scalar=adac(gate, m, s), in1=o,
                                                                     op0=ALU.mult, op1=ALU.add), last_p, D.last)
            give(b, t)
            return t

        def project(src, rhs, T, hmarks):
            w = load(src)
            b = take()
            wh, wl = (v.rearrange("p (k m) -> p k m", k=8) for v in (w.hi, w.lo))
            for k in range(8):
                p = mm3(b[:, 0:T], (wh[:, k, :], wl[:, k, :]), rhs(k), k == 0, k == 7, w.split, hmarks[k], *b.free)
            w.done = p
            return b, p

        def hk(T):
            return lambda k: (Hh[:, k, 0:T], Hl[:, k, 0:T])

        def token_rows(w, tb, hmarks, b, at):
            wh, wl = (v.rearrange("p (k m) -> p k m", k=8) for v in (w.hi, w.lo))
            c = slice(128 * tb, 128 * tb + 128)
            for k in range(8):
                p = mm3(b[:, at:at + 128], (Hh[:, k, c], Hl[:, k, c]), (wh[:, k, :], wl[:, k, :]), k == 0, k == 7,
                        w.split, hmarks[k], *b.free)
            return p

        def rows256(src, j, ntb, hmarks, dst, lane, fn):
            w = load(src)
            b = take()
            for tb in range(ntb):
                p = token_rows(w, tb, hmarks, b, 128 * tb)
            w.done = p
            t = lane(fn(dst, b[:, 0:128 * ntb].rearrange("p (b c) -> p b c", c=128)), p)
            give(b, t)
            return t

        def conv_taps(o, src, wcol, n_str, first, first_mark, psum_mark):
            ov = o.rearrange("p (s t) -> p s t", t=256)
            sv = src.rearrange("p (s t) -> p s t", t=256)
            t = D(partial(nc.vector.scalar_tensor_tensor, out=ov[:, :, 1:256], in0=sv[:, :, 0:255], scalar=wcol(0),
                                                   in1=ov[:, :, 1:256], op0=ALU.mult, op1=ALU.add),
                  first_mark, psum_mark)
            return D(partial(nc.vector.scalar_tensor_tensor, out=ov[:, :, 0:255], in0=sv[:, :, 1:256], scalar=wcol(2),
                                                      in1=ov[:, :, 0:255], op0=ALU.mult, op1=ALU.add), t)

        s_ready = ada_begin("c1")
        adaq += [ada_step(ins["wada0"], i, s_ready, "bada0", 0) for i in range(48)]
        background(16)
        ada_columns()
        x_ready = LOADED
        consts_free = []

        for l in range(DEPTH):
            lam_init = 0.8 - 0.6 * math.exp(-0.3 * l)
            full = [0, 1]
            streams = [0, 1] if l < DEPTH - 1 else [0]
            T = 256 * len(streams)
            NTB = T // 128
            phase = ExitStack()
            ar = scratch(phase, f"l{l}a")
            MIX = ar(4096).rearrange("p (k t) -> p k t", k=8)
            temps = ExitStack()
            ar = scratch(temps, f"l{l}b")
            prob = [ar(1024) for _ in range(2)]
            att = [ar(512) for _ in range(2)]
            attT = [ar(512) for _ in range(2)]
            q_f = ar(1024).rearrange("p (j t) -> p j t", j=2)
            k_f = ar(1024).rearrange("p (j t) -> p j t", j=2)
            v_d = ar(1024).rearrange("p (b c) -> p b c", b=4)
            v_a = ar(1024).rearrange("p (b c) -> p b c", b=4)
            u_f = ar(1024).rearrange("p (j t) -> p j t", j=2)
            f_c = XX[:, 0:1024].rearrange("p (b c) -> p b c", b=4)
            PQ = [ar(512) for _ in range(2)]
            bx = XX[:, 1024:2048].rearrange("p (j t) -> p j t", j=2)
            cv = ar(1024).rearrange("p (j t) -> p j t", j=2)
            rt = [SQ[2][:, 256 * i:256 * i + 256] for i in range(2)]
            o_d = ar(1024).rearrange("p (j t) -> p j t", j=2)
            st = ar(64)

            mods(f"n1g{l}", 1, 0)
            lm = par(f"lam{l}")
            lp = SM[:, 24:26]
            t = D(partial(nc.vector.tensor_tensor, lp[0:32, :], lm[0:32, 0:2], lm[0:32, 2:4], ALU.mult), D.last, P.last)
            b = take()
            p = mm(b[:, 0:2], ones[0:32, :], lp[0:32, :], True, True, t, *b.free)
            le = SM[:, 26:28]
            a = A(partial(nc.scalar.activation, le, b[:, 0:2], ACT.Exp), p, D.last)
            give(b, a)
            nlam = SM[:, 28:29]
            t = D(partial(nc.vector.tensor_tensor, nlam, le[:, 1:2], le[:, 0:1], ALU.subtract), a, D.last)
            D(partial(nc.vector.tensor_scalar, nlam, nlam, -lam_init, None, ALU.add), t)
            sg = SM[:, 29:30]
            d_sg = D(partial(nc.vector.tensor_scalar, sg, par(f"subln{l}"), 1.0 - lam_init, None, ALU.mult))

            hm = modulated(0, 0, full, x_ready)
            win = ins[f"win{l}"]

            def rope(dst, b, p, j, ctx_too):
                n = 512 if ctx_too else 256
                c = A(partial(nc.scalar.activation, dst[:, j, 0:n], b[:, 0:n], ACT.Copy), p, D.last)
                give(b, c)
                b2 = take()
                p2 = mm(b2[:, 0:256], cst("perm1"), dst[:, j, 0:256], True, True, c, *b2.free)
                t = D(partial(nc.vector.tensor_tensor, rt[j], b2[:, 0:256], cst("sin1"), ALU.mult), p2, D.last, sq_free[2])
                give(b2, t)
                t2 = D(partial(nc.vector.tensor_tensor, dst[:, j, 0:256], dst[:, j, 0:256], cst("cos1"), ALU.mult), c, p2)
                sq_busy[2] = D(partial(nc.vector.tensor_tensor, dst[:, j, 0:256], dst[:, j, 0:256], rt[j], ALU.add), t, t2)
                return sq_busy[2]

            gelu = lambda o, i: partial(nc.scalar.activation, o, i, ACT.Gelu_apprx_tanh)
            acopy_ = lambda o, i: partial(nc.scalar.activation, o, i, ACT.Copy)
            dcopy_ = lambda o, i: partial(nc.vector.tensor_copy, o, i)
            for j in range(2):
                va_ready = rows256(win[2 + j], j, NTB, hm, v_a[:, 0:NTB, 128 * j:128 * j + 128], A, gelu)
            for j in range(2):
                b, p = project(win[j], hk(T), T, hm)
                a = A(gelu(u_f[:, j, 0:T], b[:, 0:T]), p)
                give(b, a)
            u_ready = A.last
            n = NTB * 256
            fl = v_a[:, 0:NTB, :].rearrange("p b (h d) -> p (b h) d", d=64)
            sqv = cv.rearrange("p j t -> p (j t)")[:, 0:n].rearrange("p (b d) -> p b d", d=64)
            t = D(partial(nc.vector.tensor_tensor, sqv, fl, fl, ALU.mult), va_ready)
            sv, sv2 = st[:, 0:4 * NTB], st[:, 16:16 + 4 * NTB]
            t = D(partial(nc.vector.tensor_reduce, sv, sqv, AX_X, ALU.add), t)
            a = A(partial(nc.scalar.activation, sv2, sv, ACT.Sqrt, bias=epsc, scale=1.0 / 64), t)
            t = D(partial(nc.vector.reciprocal, sv, sv2), a, t)
            va_ok = D(partial(nc.vector.tensor_tensor, fl, fl, sv.rearrange("p (b o) -> p b o", o=1)
                                                .to_broadcast([128, 4 * NTB, 64]), ALU.mult), t)
            for j in range(2):
                b, p = project(win[12 + j], hk(T), T, hm)
                q_ok = rope(q_f, b, p, j, T == 512)
            for j in range(2):
                b, p = project(win[14 + j], hk(512), 512, hm)
                k_ok = rope(k_f, b, p, j, True)
            for j in range(2):
                vd_ok = rows256(win[16 + j], j, 4, hm, v_d[:, :, 128 * j:128 * j + 128], A, acopy_)

            fill = []

            def mix_a(j, l=l, NTB=NTB, T=T, va_ok=va_ok, u_ready=u_ready, v_a=v_a, u_f=u_f, MIX=MIX):
                b = take()
                for tb in range(NTB):
                    for hh in range(2):
                        h = 2 * j + hh
                        p = mm(b[64 * hh:64 * hh + 64, 128 * tb:128 * tb + 128], v_a[:, tb, 64 * h:64 * h + 64],
                               wsT[l][:, 128 * h:128 * h + 128], True, True, va_ok, *b.free)
                bs = par(f"bs{l}", 128 * j, 128 * j + 128).rearrange("p (o t) -> p o t", o=1)\
                    .to_broadcast([128, NTB, 128])
                o = MIX[:, j, 0:T].rearrange("p (b t) -> p b t", t=128)
                t = D(partial(nc.vector.tensor_tensor, o, b[:, 0:T].rearrange("p (b t) -> p b t", t=128), bs, ALU.add), p)
                give(b, t)
                D(partial(nc.vector.tensor_tensor, MIX[:, j, 0:T], MIX[:, j, 0:T], u_f[:, j, 0:T], ALU.mult), t, u_ready)

            fill += [lambda: mix_a(0), lambda: mix_a(1)]
            hold = {}

            def four(j, NTB=NTB, f_c=f_c, hm=hm, win=win, hold=hold, dcopy_=dcopy_):
                hold["f_ok"] = rows256(win[10 + j], j, NTB, hm, f_c[:, 0:NTB, 128 * j:128 * j + 128], D, dcopy_)

            def four2(s, j, f_c=f_c, PQ=PQ, MIX=MIX, hold=hold):
                b = take()
                for c in range(2):
                    p = mm(b[:, :], f_c[:, 2 * s + c, 128 * j:128 * j + 128], cst("dftn", 512 * c, 512 * c + 512),
                           c == 0, c == 1, hold["f_ok"], *b.free)
                pq = PQ[j]
                t = A(partial(nc.scalar.activation, pq, b[:, :], ACT.Copy), p, hold.get(("pq", j)))
                give(b, t)
                b2 = take()
                mm(b2[:, 0:256], cst("cd"), pq[:, 0:256], True, False, t, *b2.free)
                p = mm(b2[:, 0:256], cst("sd"), pq[:, 256:512], False, True)
                hold[("pq", j)] = p
                o = MIX[:, 4 + j, 256 * s:256 * s + 256]
                t = A(partial(nc.scalar.activation, o, b2[:, 0:256], ACT.Copy), p)
                give(b2, t)

            fill += [lambda h=h: four(h) for h in range(2)]
            fill += [lambda s=s, j=j: four2(s, j) for s in streams for j in range(2)]

            def gate_b(g, j, l=l, T=T, bx=bx, cv=cv, MIX=MIX, hm=hm, win=win, hold=hold):
                b, p = project(win[2 * g + j], hk(T), T, hm)
                if g == 2:
                    t = A(partial(nc.scalar.activation, bx[:, j, 0:T], b[:, 0:T], ACT.Copy), p)
                    hold[("bx", j)] = t
                elif g == 4:
                    t = D(partial(nc.vector.tensor_tensor, bx[:, j, 0:T], bx[:, j, 0:T], b[:, 0:T], ALU.mult), p,
                          hold[("bx", j)])
                    o = cv[:, j, 0:T]
                    wc = lambda i, l=l, j=j: par(f"sconv{l}", 3 * j + i, 3 * j + i + 1)
                    t2 = D(partial(nc.vector.tensor_scalar, o, bx[:, j, 0:T], wc(1), None, ALU.mult), t)
                    hold[("cv", j)] = conv_taps(o, bx[:, j, 0:T], wc, len(streams), None, t2, t)
                else:
                    t = D(partial(nc.vector.tensor_tensor, MIX[:, 2 + j, 0:T], cv[:, j, 0:T], b[:, 0:T], ALU.mult), p,
                          hold[("cv", j)])
                give(b, t)

            fill += [lambda g=g, j=j: gate_b(g, j) for g in (2, 4, 3) for j in range(2)]

            SCALE = 32 ** -0.5
            units = [(s, qb, h) for s in streams for h in range(4) for qb in range(2)]
            state = {}
            ring_free = {}

            def scores(n, q_f=q_f, k_f=k_f, units=units, state=state, q_ok=q_ok, k_ok=k_ok):
                s, qb, h = units[n]
                j, r0 = h // 2, 64 * (h % 2)
                cols = 512 if s == 0 else 256
                k0 = 0 if s == 0 else 256
                bs = [take(), take()]
                views = []
                for m in range(2):
                    v = bs[m][:, 0:cols]
                    r = r0 + 32 * m
                    p = P(partial(nc.tensor.matmul, 
                        v, q_f[r:r + 32, j, 256 * s + 128 * qb:256 * s + 128 * qb + 128],
                        k_f[r:r + 32, j, k0:k0 + cols], start=True, stop=True, tile_position=(r, 0)),
                        q_ok, k_ok, *bs[m].free)
                    views.append(v)
                state[n] = (bs, views, p)

            def softmax(n, units=units, state=state, prob=prob, att=att, st=st, nlam=nlam, ring_free=ring_free):
                s, qb, h = units[n]
                bs, views, p = state[n]
                cols = 512 if s == 0 else 256
                i = n % 2
                x0 = 32 + 8 * i
                mx, sm_, rc = st[:, x0:x0 + 2], st[:, x0 + 2:x0 + 4], st[:, x0 + 4:x0 + 6]
                pr = [prob[i][:, 0:cols], prob[i][:, 512:512 + cols]]
                for m in range(2):
                    t = D(partial(nc.vector.tensor_reduce, mx[:, m:m + 1], views[m], AX_X, ALU.max), p,
                          ring_free.get(("st", i)))
                t = D(partial(nc.vector.tensor_scalar, mx, mx, -SCALE, None, ALU.mult), t)
                for m in range(2):
                    a = A(partial(nc.scalar.activation, pr[m], views[m], ACT.Exp, bias=mx[:, m:m + 1], scale=SCALE,
                                                      accum_out=sm_[:, m:m + 1]), t, ring_free.get(("prob", i)))
                for b in bs:
                    give(b, a, t)
                t = D(partial(nc.vector.reciprocal, rc, sm_), a)
                t2 = D(partial(nc.vector.tensor_tensor, rc[:, 1:2], rc[:, 1:2], nlam, ALU.mult), t)
                aa = att[i][:, 0:cols]
                t = D(partial(nc.vector.tensor_scalar, aa, pr[0], rc[:, 0:1], None, ALU.mult), t, t2,
                      ring_free.get(("att", i)))
                t = D(partial(nc.vector.scalar_tensor_tensor, out=aa, in0=pr[1], scalar=rc[:, 1:2], in1=aa,
                                                       op0=ALU.mult, op1=ALU.add), t)
                ring_free[("prob", i)] = t
                ring_free[("st", i)] = t
                state[("a", n)] = t

            def apply(n, units=units, state=state, att=att, attT=attT, v_d=v_d, o_d=o_d, ring_free=ring_free,
                      vd_ok=vd_ok):
                s, qb, h = units[n]
                i = n % 2
                nk = 4 if s == 0 else 2
                b = take()
                for c in range(nk):
                    p = P(partial(nc.tensor.transpose, b[:, 128 * c:128 * c + 128], att[i][:, 128 * c:128 * c + 128],
                                                     eye), state[("a", n)], *b.free)
                ring_free[("att", i)] = p
                a = A(partial(nc.scalar.activation, attT[i][:, 0:128 * nk], b[:, 0:128 * nk], ACT.Copy), p,
                      ring_free.get(("attT", i)))
                give(b, a)
                j, r0 = h // 2, 64 * (h % 2)
                b2 = take()
                for c in range(nk):
                    tb = c + (0 if s == 0 else 2)
                    p = mm(b2[r0:r0 + 64, 0:128], v_d[:, tb, 64 * h:64 * h + 64],
                           attT[i][:, 128 * c:128 * c + 128], c == 0, c == nk - 1, a, vd_ok, *b2.free)
                ring_free[("attT", i)] = p
                t = D(partial(nc.vector.tensor_copy, o_d[r0:r0 + 64, j, 256 * s + 128 * qb:256 * s + 128 * qb + 128],
                                              b2[r0:r0 + 64, 0:128]), p)
                give(b2, t)

            scores(0)
            softmax(0)
            scores(1)
            softmax(1)
            for n in range(len(units)):
                if fill:
                    fill.pop(0)()
                background(2)
                apply(n)
                if n + 2 < len(units):
                    scores(n + 2)
                    softmax(n + 2)
            while fill:
                fill.pop(0)()
            while adaq:
                background()
            if l == 0:
                mods("n2g0", 4, 1)
            for j in range(2):
                r = stats(lambda i, j=j: o_d[:, j, 0:T], 1, 0, T, par("blk64"), 64.0, D.last)
                t = D(partial(nc.vector.scalar_tensor_tensor, out=MIX[:, 6 + j, 0:T], in0=o_d[:, j, 0:T], scalar=sg,
                                                            in1=RSTD[:, 0:T], op0=ALU.mult, op1=ALU.mult), r, d_sg)
            v4 = lambda t: t.rearrange("p (k t) -> p k t", k=4)
            fence()
            temps.close()
            d_mix = D.last
            mixp = []
            Mh2, Ml2 = (v4(sb(f"l{l}m{z}", 2048, F32R, phase)[:, :]) for z in "hl")
            Mh1, Ml1 = (v4(t[:, :]) for t in (HXh, HXl))
            for k in range(8):
                h_, l_ = (Mh1, Ml1) if k < 4 else (Mh2, Ml2)
                m_ = split_to(h_[:, k % 4, 0:T], l_[:, k % 4, 0:T], MIX[:, k, 0:T], D.last if k == 0 else d_mix, A.last
                              if k == 0 else None, P.last if k == 0 else None)
                mixp.append((h_[:, k % 4, 0:T], l_[:, k % 4, 0:T], m_))
            for i in range(8):
                b, p = project(ins[f"wout{l}"][i], lambda k: mixp[k][0:2], T, [z[2] for z in mixp])
                x_ready = residual(b, i, 2, streams, p)

            hm = modulated(1, 3, streams, x_ready)
            fence()
            if l == DEPTH - 1:
                consts_free.append((P.last, D.last, A.last))
            phase.close()
            phase = ExitStack()
            ar = scratch(phase, f"l{l}f")
            MIDh, MIDl = (ar(4096, F32R).rearrange("p (m t) -> p m t", m=8) for _ in range(2))
            OC = [ar(512) for _ in range(3)]
            oc_free = [None] * 3
            wup = ins[f"wup{l}"]

            nxt = ["wada1", "wada2"][l]
            s_ready = ada_begin(["c1", "c2"][l]) if l else s_ready
            adaq += [ada_step(ins[nxt], i, s_ready, ["bada1", "bada2"][l], (cur[0] + 1) % 2) for i in range(48)]

            mid_free = None
            for third in range(3):
                ms = range(8 * third, min(8 * third + 8, 22))
                mid = []
                for m in ms:
                    ba, pa = project(wup[m], hk(T), T, hm)
                    o = OC[m % 3][:, 0:T]
                    wc = lambda c: par(f"fconv{l}", 3 * m + c, 3 * m + c + 1)
                    a = A(partial(nc.scalar.activation, o, ba[:, 0:T], ACT.Copy, scale=wc(1)), pa, oc_free[m % 3])
                    t = conv_taps(o, ba[:, 0:T], wc, len(streams), None, a, pa)
                    give(ba, a, t)
                    a = A(partial(nc.scalar.activation, o, o, ACT.Silu), t)
                    bb, pb = project(wup[22 + m], hk(T), T, hm)
                    t = D(partial(nc.vector.tensor_tensor, o, o, bb[:, 0:T], ALU.mult), a, pb)
                    give(bb, t)
                    h_, l_ = MIDh[:, m % 8, 0:T], MIDl[:, m % 8, 0:T]
                    t = split_to(h_, l_, o, t, mid_free)
                    oc_free[m % 3] = t
                    mid.append((h_, l_, t))
                    background(1)
                for m in range(8):
                    b = take()
                    w = load(ins[f"wdn{l}"][8 * third + m, :, 0:128 * len(ms)], 128 * len(ms))
                    wh, wl = (v.rearrange("p (k m) -> p k m", m=128) for v in (w.hi, w.lo))
                    for k in range(len(ms)):
                        p = mm3(b[:, 0:T], (wh[:, k, :], wl[:, k, :]), mid[k][0:2], k == 0, k == len(ms) - 1,
                                w.split, mid[k][2], *b.free)
                    w.done = p
                    x_ready = residual(b, m, 5, streams, p)
                    background(1)
                mid_free = P.last
            while adaq:
                background()
            fence()
            phase.close()
            cur[0] = (cur[0] + 1) % 2
            mods(["n1g1", "n1g2"][l], 1, 0)
            mods(["n2g1", "n2g2"][l], 4, 1)

        r = stats(lambda i: X[:, i, 0:256], 8, 0, 256, ones, 1024.0, x_ready)
        for k in range(8):
            t = D(partial(nc.vector.scalar_tensor_tensor, out=X[:, k, 0:256], in0=X[:, k, 0:256],
                                                        scalar=par("finalg", k, k + 1), in1=RSTD[:, 0:256],
                                                        op0=ALU.mult, op1=ALU.mult), r)
        x_ready = t
        x2_free = (P.last, D.last, A.last)

        fence()
        for lane in (P, A, D):
            lane.wait((s_c2, 16), (s_c, 16))
        merge = ExitStack()
        m_T, a_T = (v.rearrange("p (j t) -> p j t", j=4) for v in (XX[:, 0:1024], XX[:, 1024:2048]))
        ar = scratch(merge, "m")
        q_a = ar(1024).rearrange("p (j t) -> p j t", j=4)
        k_a = ar(512)
        v_t = ar(512).rearrange("p (b c) -> p b c", b=4)
        q_m = ar(1024).rearrange("p (j t) -> p j t", j=4)
        k_m = ar(2048).rearrange("p (j t) -> p j t", j=4)
        v_m = ar(2048).rearrange("p (b c) -> p b c", b=4)
        o_g = ar(1024).rearrange("p (j t) -> p j t", j=4)
        prob = [ar(512) for _ in range(3)]
        RB = [ar(512) for _ in range(2)]
        DDa = ar(768)
        DD = [DDa[:, 256 * i:256 * i + 256] for i in range(3)]
        PP = [ar(1024) for _ in range(2)]
        attT = [v[:, 0:512] for v in PP]
        rt = [SQ[2][:, 256 * i:256 * i + 256] for i in range(2)]
        hs = [ar(256) for _ in range(2)]
        tmp = [ar(256) for _ in range(2)]
        keep = [ar(512) for _ in range(2)]
        spare = [PP[i // 2][:, 512 * (i % 2):512 * (i % 2) + 512] for i in range(4)]
        spare += [v[:, 2 * i:2 * i + 2, :].rearrange("p k t -> p (k t)") for v in (m_T, a_T) for i in range(2)]
        st = ar(64)
        cT = ar(32)

        hm = modulated(0, 0, [0, 1], x_ready)
        w2 = ins["win2"]

        w = load(ins["wg2"], 128)
        wvh, wvl = (v.rearrange("p (k m) -> p k m", k=8) for v in (w.hi, w.lo))
        gb = []
        for g in range(4):
            b = take()
            for k in range(8):
                c = slice(4 * g, 4 * g + 4)
                p = mm3(b[0:4, :], (wvh[:, k, c], wvl[:, k, c]), (Hh[:, k, :], Hl[:, k, :]), k == 0, k == 7,
                        w.split, hm[k], *b.free)
            gb.append((b, p))
        w.done = P.last
        ONE = DDa[0:4, 0:512]
        D(partial(nc.vector.memset, ONE, 1.0))
        dirs = []
        for d in range(2):
            (bi, pi), (bf, pf) = gb[2 * d], gb[2 * d + 1]
            gi, t1_, t2_, c_n = (spare[4 * d + i][0:4, :] for i in range(4))
            gf = keep[d][0:4, :]
            bias = lambda g: par("gbias", g, g + 1)[0:4, :]

            def seq(v, half, d=d):
                s = v[:, 256:512] if half == 0 else v[:, 0:256]
                return s[:, ::-1] if d else s

            for half in range(2):
                o = gi[:, 256 * half:256 * half + 256]
                t = D(partial(nc.vector.tensor_scalar, o, seq(bi[0:4, :], half), bias(2 * d), None, ALU.add),
                      pi)
                o = gf[:, 256 * half:256 * half + 256]
                t = D(partial(nc.vector.tensor_scalar, o, seq(bf[0:4, :], half), bias(2 * d + 1), None,
                                                                ALU.add), pf)
            give(bi, t)
            give(bf, t)
            a = A(partial(nc.scalar.activation, t1_, gf, ACT.Abs), t)
            a = A(partial(nc.scalar.activation, t1_, t1_, ACT.Exp, scale=-1.0), a)
            t = D(partial(nc.vector.tensor_scalar, t1_, t1_, 1.0, None, ALU.add), a)
            a = A(partial(nc.scalar.activation, t1_, t1_, ACT.Ln), t)
            t = D(partial(nc.vector.tensor_scalar, gf, gf, 0.0, None, ALU.min), a)
            t = D(partial(nc.vector.tensor_tensor, gf, gf, t1_, ALU.subtract), a, t)
            t = D(partial(nc.vector.tensor_tensor_scan, t2_, ONE, gf, 0.0, ALU.mult, ALU.add), t)
            t = D(partial(nc.vector.tensor_tensor, gi, gi, t2_, ALU.subtract), t)
            t = D(partial(nc.vector.tensor_tensor_scan, t1_, gi, gi, 0.0, ALU.max, ALU.max), t)
            t = D(partial(nc.vector.tensor_tensor, t2_, t2_, t1_, ALU.add), t)
            rw = gf
            mseg, eseg, cseg = t1_[:, 256:512], t2_[:, 256:512], gi
            t = D(partial(nc.vector.tensor_scalar, rw[:, 0:256], mseg[:, ::-1] if d else mseg, -1.0, None, ALU.mult), t)
            a = A(partial(nc.scalar.activation, rw[:, 256:512], eseg[:, ::-1] if d else eseg, ACT.Exp, scale=-1.0), t)
            t = D(partial(nc.vector.tensor_copy, c_n[:, 256:512], gi[:, 255::-1] if d else gi[:, 0:256]), t)
            t = D(partial(nc.vector.tensor_copy, c_n[:, 0:256], gi[:, 256:512][:, ::-1] if d else gi[:, 256:512]), t)
            b = take()
            for tb in range(4):
                p = P(partial(nc.tensor.transpose, b[:, 4 * tb:4 * tb + 4], c_n[:, 128 * tb:128 * tb + 128],
                                                        eye[0:4, 0:4]), t, *b.free)
            o = cT[:, 16 * d:16 * d + 16]
            t = D(partial(nc.vector.tensor_copy, o, b[:, 0:16]), p)
            give(b, t)
            dirs.append((rw, a, t))

        def head_norm_rope(dst, n, b, p, g, i):
            c = A(partial(nc.scalar.activation, dst[:, 0:n], b[:, 0:n], ACT.Copy), p)
            give(b, c)
            r = stats(lambda _: dst[:, 0:n], 1, 0, n, par("blk64"), 64.0, c)
            t = D(partial(nc.vector.scalar_tensor_tensor, out=dst[:, 0:n], in0=dst[:, 0:n], scalar=g, in1=RSTD[:, 0:n],
                                                   op0=ALU.mult, op1=ALU.mult), r)
            b2 = take()
            p2 = mm(b2[:, 0:256], cst("perm2"), dst[:, 0:256], True, True, t, *b2.free)
            t = D(partial(nc.vector.tensor_tensor, rt[i], b2[:, 0:256], cst("sin2"), ALU.mult), p2, D.last, sq_free[2])
            give(b2, t)
            t2 = D(partial(nc.vector.tensor_tensor, dst[:, 0:256], dst[:, 0:256], cst("cos2"), ALU.mult), t)
            sq_busy[2] = D(partial(nc.vector.tensor_tensor, dst[:, 0:256], dst[:, 0:256], rt[i], ALU.add), t2)
            return sq_busy[2]

        pend = []
        for c in range(4):
            b, p = project(w2[16 + c], hk(256), 256, hm)
            pend.append((q_a[:, c, :], 256, b, p, par("qg")))
            if len(pend) > 1:
                qa_ok = head_norm_rope(*pend.pop(0), c % 2)
        b, p = project(w2[20], hk(512), 512, hm)
        pend.append((k_a, 512, b, p, par("kg")))
        qa_ok = head_norm_rope(*pend.pop(0), 0)
        vt_ok = rows256(w2[21], 0, 4, hm, v_t, A, acopy_)
        ka_ok = head_norm_rope(*pend.pop(0), 1)

        fill = []

        def proj_m(dst, tile, T, fn, key):
            def go():
                b, p = project(w2[tile], hk(T), T, hm)
                t = fn(dst, b[:, 0:T], p)
                give(b, t)
                marks[key] = t
            return go

        marks = {}

        def dcopy(dst, src, p):
            return D(partial(nc.vector.tensor_copy, dst, src), p)

        def acopy(dst, src, p):
            return A(partial(nc.scalar.activation, dst, src, ACT.Copy), p)

        for c in range(4):
            fill.append(proj_m(q_m[:, c, :], c, 256, dcopy, ("q", c)))
        for c in range(4):
            fill.append(proj_m(k_m[:, c, :], 4 + c, 512, dcopy, ("k", c)))

        def rows_v(c):
            def go():
                marks[("v", c)] = rows256(w2[8 + c], 0, 4, hm, v_m[:, :, 128 * c:128 * c + 128], D, dcopy_)
            return go

        for c in range(4):
            fill.append(rows_v(c))
        for c in range(4):
            fill.append(proj_m(o_g[:, c, :], 12 + c, 256, acopy, ("o", c)))

        SC2 = 64 ** -0.5
        units = [(c, kv, qb) for c in range(4) for kv in range(2) for qb in range(2)]
        state = {}
        ring_free = {}
        sinkb = par("sink")

        def scores2(n):
            c, kv, qb = units[n]
            r = 64 * kv
            b = take()
            p = P(partial(nc.tensor.matmul, b[:, :], q_a[r:r + 64, c, 128 * qb:128 * qb + 128], k_a[r:r + 64, :],
                                     start=True, stop=True, tile_position=(r, 0)), qa_ok, ka_ok, *b.free)
            edge = b[:, 128:256] if qb == 0 else b[:, 0:128]
            t = D(partial(nc.vector.tensor_tensor, edge, edge, cst("win", 128 * qb, 128 * qb + 128), ALU.add), p)
            i = n % 3
            x0 = 8 * i
            mx, sm_, es, rc = (st[:, x0 + z:x0 + z + 1] for z in range(4))
            h = c + 4 * kv
            sk = sinkb[:, h:h + 1]
            t = D(partial(nc.vector.tensor_reduce, mx, b[:, :], AX_X, ALU.max), t, ring_free.get(("st", i)))
            t = D(partial(nc.vector.scalar_tensor_tensor, out=mx, in0=mx, scalar=SC2, in1=sk, op0=ALU.mult, op1=ALU.max), t)
            t = D(partial(nc.vector.tensor_scalar, mx, mx, -1.0, None, ALU.mult), t)
            pr = prob[i]
            A(partial(nc.scalar.activation, pr, b[:, :], ACT.Exp, bias=mx, scale=SC2, accum_out=sm_), t,
              ring_free.get(("prob", i)))
            a = A(partial(nc.scalar.activation, es, sk, ACT.Exp, bias=mx), t)
            give(b, a)
            t = D(partial(nc.vector.tensor_tensor, rc, sm_, es, ALU.add), a)
            t = D(partial(nc.vector.reciprocal, rc, rc), t)
            t = D(partial(nc.vector.tensor_scalar, pr, pr, rc, None, ALU.mult), t)
            ring_free[("st", i)] = t
            state[n] = t

        def apply2(n):
            c, kv, qb = units[n]
            b = take()
            i = n % 3
            for kc in range(4):
                p = P(partial(nc.tensor.transpose, b[:, 128 * kc:128 * kc + 128],
                                                   prob[i][:, 128 * kc:128 * kc + 128], eye), state[n], *b.free)
            ring_free[("prob", i)] = p
            at = attT[n % 2]
            a = A(partial(nc.scalar.activation, at, b[:, :], ACT.Copy), p, ring_free.get(("attT", n % 2)))
            give(b, a)
            b2 = take()
            r = 64 * kv
            for kc in range(4):
                p = mm(b2[r:r + 64, 0:128], v_t[:, kc, 64 * kv:64 * kv + 64], at[:, 128 * kc:128 * kc + 128],
                       kc == 0, kc == 3, a, vt_ok, *b2.free)
            ring_free[("attT", n % 2)] = p
            t = D(partial(nc.vector.tensor_copy, a_T[r:r + 64, c, 128 * qb:128 * qb + 128], b2[r:r + 64, 0:128]), p)
            give(b2, t)

        scores2(0)
        scores2(1)
        for n in range(16):
            if fill:
                fill.pop(0)()
            apply2(n)
            if n + 2 < 16:
                scores2(n + 2)
        while fill:
            fill.pop(0)()
        a_ok = D.last
        for c in range(4):
            og_ok = A(partial(nc.scalar.activation, o_g[:, c, :], o_g[:, c, :], ACT.Sigmoid), marks[("o", c)])

        SM2 = 128 ** -0.5
        pp_free = [None, None]
        rb_free = [None, None]
        dd_free = [None] * 3
        nd = 0
        mt_ok = []

        def lstm_scores(h):
            sbk = [take(), take()]
            for tb in range(4):
                b = sbk[tb // 2]
                p = mm(b[:, 256 * (tb % 2):256 * (tb % 2) + 256], k_m[:, h, 128 * tb:128 * tb + 128], q_m[:, h, :],
                       True, True, marks[("k", h)], marks[("q", h)], *b.free)
            return sbk, p

        nxt_s = lstm_scores(0)
        for h in range(4):
            sbk, ps_ = nxt_s
            for d in range(2):
                rw, ra, ct = dirs[d]
                b = take()
                p = mm(b[:, :], cst("sel", 128 * h, 128 * h + 128)[0:4, :], rw, True, True, ra, D.last, *b.free)
                rb = RB[d]
                a = A(partial(nc.scalar.activation, rb, b[:, :], ACT.Copy), p, rb_free[d])
                give(b, a)
                pp = PP[d]
                for tb in range(4):
                    dd = DD[nd % 3]
                    cc = cT[:, 16 * d + 4 * tb + h:16 * d + 4 * tb + h + 1]
                    t = D(partial(nc.vector.tensor_scalar, dd, rb[:, 0:256], cc, 0.0, ALU.add, ALU.min), a, ct,
                          dd_free[nd % 3])
                    ax = A(partial(nc.scalar.activation, dd, dd, ACT.Exp), t)
                    o = pp[:, 256 * tb:256 * tb + 256]
                    s = sbk[tb // 2][:, 256 * (tb % 2):256 * (tb % 2) + 256]
                    t = D(partial(nc.vector.scalar_tensor_tensor, out=o, in0=s, scalar=SM2, in1=dd,
                                                                           op0=ALU.mult, op1=ALU.mult), ax, ps_,
                          pp_free[d])
                    dd_free[nd % 3] = t
                    nd += 1
                    if tb < 2:
                        mk = cst("cb" if d else "cf", 256 * tb, 256 * tb + 256)
                        t = D(partial(nc.vector.tensor_tensor, o, o, mk, ALU.mult), t)
                if d == 1:
                    for b_ in sbk:
                        give(b_, t)
                if d == 0 and h < 3:
                    nxt_s = lstm_scores(h + 1)
                b = take()
                for which, c0 in (("num", 0), ("den", 256)):
                    for tb in range(4):
                        lhs = v_m[:, tb, 128 * h:128 * h + 128] if which == "num" else ones
                        p = mm(b[:, c0:c0 + 256], lhs, pp[:, 256 * tb:256 * tb + 256], tb == 0, tb == 3, t,
                               marks[("v", h)], *b.free)
                pp_free[d] = p
                tm = tmp[d]
                ab_ = A(partial(nc.scalar.activation, tm, b[:, 256:512], ACT.Abs), p, D.last)
                t = D(partial(nc.vector.tensor_tensor, tm, tm, rb[:, 256:512], ALU.max), ab_)
                rb_free[d] = t
                t = D(partial(nc.vector.reciprocal, tm, tm), t)
                hd = hs[d]
                t = D(partial(nc.vector.tensor_tensor, hd, tm, b[:, 0:256], ALU.mult), t)
                give(b, t)
            t = D(partial(nc.vector.tensor_tensor, hs[0], hs[0], hs[1], ALU.add), t)
            r = stats(lambda _: hs[0], 1, 0, 256, ones, 128.0, t)
            t = D(partial(nc.vector.scalar_tensor_tensor, out=hs[0], in0=hs[0], scalar=par("mng", h, h + 1),
                                                        in1=RSTD[:, 0:256], op0=ALU.mult, op1=ALU.mult), r)
            t = D(partial(nc.vector.tensor_tensor, m_T[:, h, :], hs[0], o_g[:, h, :], ALU.mult), t, og_ok)
            mt_ok.append(t)

        fence()
        merge.close()
        merge = ExitStack()
        ar = scratch(merge, "n")
        MG = ar(2048).rearrange("p (k t) -> p k t", k=8)
        gsb = [ar(256) for _ in range(4)]
        BRh, BRl, MGh, MGl = (ar(2048, F32R).rearrange("p (k t) -> p k t", k=8) for _ in range(4))
        br = []
        for k in range(8):
            src = m_T[:, k, :] if k < 4 else a_T[:, k - 4, :]
            br.append(split_to(BRh[:, k, :], BRl[:, k, :], src))
        g_free = [None] * 4
        mg = []
        for m in range(8):
            j = m % 2
            sg_ = []
            for z in range(2):
                b, p = project(w2[22 + 8 * z + m], hk(256), 256, hm)
                gg = gsb[2 * j + z]
                a = A(partial(nc.scalar.activation, gg, b[:, 0:256], ACT.Sigmoid), p, g_free[2 * j + z])
                give(b, a)
                sg_.append((gg, a))
            w = load(ins["wbr2"][m])
            wh, wl = (v.rearrange("p (k m) -> p k m", k=8) for v in (w.hi, w.lo))
            b = take()
            for k in range(8):
                p = mm3(b[:, 256 * (k // 4):256 * (k // 4) + 256], (wh[:, k, :], wl[:, k, :]),
                        (BRh[:, k, :], BRl[:, k, :]), k % 4 == 0, k % 4 == 3, w.split, br[k], *b.free)
            w.done = p
            o = MG[:, m, :]
            t1_ = D(partial(nc.vector.tensor_tensor, o, sg_[0][0], b[:, 0:256], ALU.mult), p, sg_[0][1])
            t2_ = D(partial(nc.vector.tensor_tensor, sg_[1][0], sg_[1][0], b[:, 256:512], ALU.mult), sg_[1][1])
            give(b, t2_)
            t = D(partial(nc.vector.tensor_tensor, o, o, sg_[1][0], ALU.add), t1_, t2_)
            g_free[2 * j] = g_free[2 * j + 1] = t
            mg.append(split_to(MGh[:, m, :], MGl[:, m, :], o, t))
        for i in range(8):
            b, p = project(ins["wout2"][i], lambda k: (MGh[:, k, :], MGl[:, k, :]), 256, mg)
            x_ready = residual(b, i, 2, [0], p)

        HX = [t[:, :].rearrange("p (k t) -> p k t", k=8) for t in (HXh, HXl)]
        XP = XX[:, :].rearrange("p (k t) -> p k t", k=8)
        hm = modulated(1, 3, [0], x_ready, HX)
        d_xx = D(partial(nc.vector.tensor_copy, XP, X[:, :, 0:256]), A.last)
        fence()
        merge.close()
        early.close()
        late = ExitStack()
        GT = sb("G", 32768, at=late)
        WP = [[sb(f"W{z}{i}", 256, F32R, late)[:, :] for z in "hl"] for i in range(4)]
        at = [0]

        def ar(n):
            at[0] += n
            return GT[:, at[0] - n:at[0]]

        q_p = ar(4096).rearrange("p (j t) -> p j t", j=16)
        Sb = [ar(2048) for _ in range(2)]
        S2 = ar(2048)
        W1, W2 = ar(2048), ar(2048)
        top = ar(256).rearrange("p (j k) -> p j k", k=16)
        tid = ar(256).rearrange("p (j k) -> p j k", k=16)
        tidf = ar(256)
        ctop = ar(128)
        cpos = ar(128)
        ca, cb_ = ar(128), ar(128)
        gsm = ar(128)
        gs = ar(16)
        idA, idB = ar(128), ar(128)
        for c in range(16):
            b, p = project(ins["wq2"][c], lambda k: (HX[0][:, k, :], HX[1][:, k, :]), 256, hm)
            a = A(partial(nc.scalar.activation, q_p[:, c, :], b[:, 0:256], ACT.Copy), p)
            give(b, a)
        for half in range(2):
            wk = load(ins["keys2"][half], TILE, False)
            for tb in range(2):
                for q4 in (2 * half, 2 * half + 1):
                    b = take()
                    for z in range(4):
                        c = 4 * q4 + z
                        p = mm(b[:, 128 * z:128 * z + 128], q_p[:, c, 128 * tb:128 * tb + 128],
                               wk.raw[:, 128 * (c % 8):128 * (c % 8) + 128], True, True, a, wk.ready, *b.free)
                    sv = Sb[tb][:, 512 * q4:512 * q4 + 512]
                    ac = A(partial(nc.scalar.activation, sv, b[:, :], ACT.Copy), p)
                    give(b, ac)
            wk.done = wk.freed = p
        TT = [ar(256) for _ in range(3)]
        iAT, iBT, gT = TT
        NEG = -3.0e38
        for tb in range(2):
            S = Sb[tb]
            free_s = ac
            for c in range(16):
                sv = S[:, 128 * c:128 * c + 128]
                s2 = S2[:, 128 * c:128 * c + 128]
                v0, v1 = top[:, c, 0:8], top[:, c, 8:16]
                i0, i1 = tid[:, c, 0:8].bitcast(U32), tid[:, c, 8:16].bitcast(U32)
                t = D(partial(nc.vector.max, v0, sv), ac, free_s)
                D(partial(nc.vector.max_index, i0, v0, sv), t)
                t = D(partial(nc.vector.match_replace, s2, v0, sv, NEG), t)
                t = D(partial(nc.vector.max, v1, s2), t)
                t = D(partial(nc.vector.max_index, i1, v1, s2), t)
            ti = tid.rearrange("p j k -> p (j k)").bitcast(U32)
            t_ids = D(partial(nc.vector.tensor_copy, tidf, ti), t)
            hp = top.rearrange("p (h z) k -> p h z k", z=2)
            for h in range(8):
                o = W1[:, 256 * h:256 * h + 256].rearrange("p (a b) -> p a b", b=16)
                s1b = top[:, 2 * h, :].rearrange("p (a o) -> p a o", o=1).to_broadcast([128, 16, 16])
                s2b = top[:, 2 * h + 1, :].rearrange("p (o b) -> p o b", o=1).to_broadcast([128, 16, 16])
                t = D(partial(nc.vector.tensor_tensor, o, s1b, s2b, ALU.add), t)
                sv, s2 = W1[:, 256 * h:256 * h + 256], W2[:, 256 * h:256 * h + 256]
                v0, v1 = ctop[:, 16 * h:16 * h + 8], ctop[:, 16 * h + 8:16 * h + 16]
                i0, i1 = (cpos[:, 16 * h + 8 * z:16 * h + 8 * z + 8].bitcast(U32) for z in range(2))
                t = D(partial(nc.vector.max, v0, sv), t)
                D(partial(nc.vector.max_index, i0, v0, sv), t)
                t = D(partial(nc.vector.match_replace, s2, v0, sv, NEG), t)
                t = D(partial(nc.vector.max, v1, s2), t)
                t = D(partial(nc.vector.max_index, i1, v1, s2), t)
            c3 = ctop.rearrange("p (h k) -> p h k", k=16)
            g3 = gsm.rearrange("p (h k) -> p h k", k=16)
            tg = D(partial(nc.vector.tensor_tensor, g3, c3, c3[:, :, 0:1].to_broadcast([128, 8, 16]), ALU.subtract), t)
            ag = A(partial(nc.scalar.activation, gsm, gsm, ACT.Exp), tg)
            cp = cpos.bitcast(U32)
            cau, cbu = ca.bitcast(U32), cb_.bitcast(U32)
            t = D(partial(nc.vector.tensor_scalar, cau, cp, 4, None, ALU.logical_shift_right), t)
            t1_ = D(partial(nc.vector.tensor_scalar, cbu, cp, 15, None, ALU.bitwise_and), t)
            fa, fb = W2[:, 0:128], W2[:, 128:256]
            t = D(partial(nc.vector.tensor_copy, fa, cau), t1_)
            t = D(partial(nc.vector.tensor_copy, fb, cbu), t)
            for z, f, idx in ((0, fa, idA), (1, fb, idB)):
                e3 = W1.rearrange("p (a j) -> p a j", j=16)
                e4 = W1.rearrange("p (h k j) -> p h k j", k=16, j=16)
                fo = f.rearrange("p (a o) -> p a o", o=1).to_broadcast([128, 128, 16])
                io = iota[:, 0:16].rearrange("p (o j) -> p o j", o=1).to_broadcast([128, 128, 16])
                t = D(partial(nc.vector.tensor_tensor, e3, fo, io, ALU.is_equal), t, t_ids)
                src = tidf.rearrange("p (h z j) -> p h z j", z=2, j=16)[:, :, z:z + 1, :].to_broadcast([128, 8, 16, 16])
                t = D(partial(nc.vector.tensor_tensor, e4, e4, src, ALU.mult), t)
                t = D(partial(nc.vector.tensor_reduce, idx, e3, AX_X, ALU.add), t)
            tg = D(partial(nc.vector.tensor_reduce, gs[:, 0:8], g3, AX_X, ALU.add), ag)
            tg = D(partial(nc.vector.reciprocal, gs[:, 8:16], gs[:, 0:8]), tg)
            tg = D(partial(nc.vector.tensor_tensor, g3, g3, gs[:, 8:16].rearrange("p (h o) -> p h o", o=1)
                                             .to_broadcast([128, 8, 16]), ALU.mult), tg)
            b = take()
            for z, v in enumerate((idA, idB, gsm)):
                p = P(partial(nc.tensor.transpose, b[:, 128 * z:128 * z + 128], v, eye), t, tg, *b.free)
            for z, v in enumerate((iAT, iBT, gT)):
                o = v[:, 128 * tb:128 * tb + 128]
                t = D(partial(nc.vector.tensor_copy, o, b[:, 128 * z:128 * z + 128]), p)
            give(b, t)

        fence()
        GG = GT[:, :].rearrange("p (a t) -> p a t", a=128)
        keepT = [RAW[:, 256 * i:256 * i + 256] for i in range(3)]
        for i in range(3):
            D(partial(nc.vector.tensor_copy, keepT[i], TT[i]))
        iAT, iBT, gT = keepT
        fence()
        oh = [(RAW[:, 1024 + 512 * i:1280 + 512 * i], RAW[:, 1280 + 512 * i:1536 + 512 * i]) for i in range(4)]
        oh_free = [None] * 4
        for q in range(64):
            b = take()
            for z in range(2):
                i = (2 * q + z) % 4
                oa, ob = oh[i]
                for y in range(2):
                    tk = 4 * q + 2 * z + y
                    o1, o2 = oa[:, 128 * y:128 * y + 128], ob[:, 128 * y:128 * y + 128]
                    ia, ib, gg = iAT[:, tk:tk + 1], iBT[:, tk:tk + 1], gT[:, tk:tk + 1]
                    D(partial(nc.vector.tensor_scalar, o1, iota, ia, None, ALU.is_equal), oh_free[i])
                    t = D(partial(nc.vector.tensor_scalar, o2, iota, ib, gg, ALU.is_equal, ALU.mult),
                          oh_free[i])
                for y in range(2):
                    o1, o2 = oa[:, 128 * y:128 * y + 128], ob[:, 128 * y:128 * y + 128]
                    c0 = 128 * (2 * z + y)
                    p = mm(b[:, c0:c0 + 128], o2, o1, True, True, t, *b.free)
                oh_free[i] = p
            dst = GG[:, :, 4 * q:4 * q + 4].rearrange("p a t -> p t a")
            a = A(partial(nc.scalar.activation, dst, b[:, :].rearrange("p (t a) -> p t a", t=4), ACT.Copy), p)
            give(b, a)
        fence()
        lent = [P.last, D.last]
        yb = [take() for _ in range(4)]
        ab = [take() for _ in range(3)]
        act_free = [None] * 4
        wact = {}

        def up(a_):
            w = load(ins["ut2"][a_])
            wh, wl = (v.rearrange("p (k m) -> p k m", k=8) for v in (w.hi, w.lo))
            b = ab[a_ % 3]
            for k in range(8):
                p = mm3(b[:, 0:256], (wh[:, k, :], wl[:, k, :]), (HX[0][:, k, :], HX[1][:, k, :]), k == 0, k == 7,
                        w.split, *b.free)
            w.done = p
            t = A(partial(nc.scalar.activation, b[:, 256:512], b[:, 0:256], ACT.Gelu_apprx_tanh), p)
            g = GG[:, a_, :]
            t = D(partial(nc.vector.tensor_tensor, g, b[:, 256:512], g, ALU.mult), t)
            b.release(t)
            wact[a_] = split_to(WP[a_ % 4][0], WP[a_ % 4][1], g, t, act_free[a_ % 4])

        def down(a_):
            w = load(ins["v2"][a_])
            for m in range(8):
                b = yb[m // 2]
                c = slice(128 * m, 128 * m + 128)
                mm3(b[:, 256 * (m % 2):256 * (m % 2) + 256], (w.hi[:, c], w.lo[:, c]), WP[a_ % 4],
                    a_ == 0 and m % 2 == 0, a_ == 127, w.split, wact[a_], *b.free, skip=True, inc=m == 7)
            w.done = P.last
            act_free[a_ % 4] = P.last

        n_before_lent = [len(asked)]
        up(0)
        for a_ in range(128):
            if a_ < 127:
                up(a_ + 1)
            down(a_)
        pl = P.last
        for b in ab:
            give(b, *b.free)
        outs = [GT[:, 1024 * i:1024 * i + 1024] for i in range(2)]
        for m in range(8):
            i = yb[m // 2][:, 256 * (m % 2):256 * (m % 2) + 256]
            o = XP[:, m, :]
            t = D(partial(nc.vector.scalar_tensor_tensor, out=o, in0=i, scalar=adac(5, m, 0), in1=o,
                                                                  op0=ALU.mult, op1=ALU.add), pl)
        out_marks = []
        for tb in range(2):
            for half in range(2):
                b = take()
                for z in range(4):
                    m = 4 * half + z
                    p = P(partial(nc.tensor.transpose, b[:, 128 * z:128 * z + 128],
                                                                     XP[:, m, 128 * tb:128 * tb + 128], eye),
                          t, *b.free)
                o = outs[tb][:, 512 * half:512 * half + 512]
                a = A(partial(nc.scalar.activation, o, b[:, :], ACT.Copy), p)
                give(b, a)
            out_marks.append(a)

        late.close()
        if not order:
            return asked

        block = ctx.enter_context(nc.Block())

        @block.sync
        def _(e):
            e.dma_start(PT[:, :], ins["par"]).then_inc(s_in, 16)
            e.dma_start(XT[:, :], ins["xt"]).then_inc(s_in, 16)
            e.dma_start(CT[:, :], ins["cst"]).then_inc(s_in, 16)
            first_up = n_before_lent[0]
            todo = [(x2_free, X[:, :, 256:512], ins["ctx2t"].rearrange("p (k t) -> p k t", k=8), s_c2),
                    (consts_free[0], CT[:, 0:NCS2], ins["cs2"], s_c)]
            todo.sort(key=lambda x: x[0][0][1])
            for i, t in enumerate(tiles):
                if i >= NRAW:
                    last = tiles[i - NRAW]
                    frees = [last.freed]
                    while todo and tiles[i - 1].done and (tiles[i - NRAW].done[1] > todo[0][0][0][1]):
                        for m in todo[0][0]:
                            e.wait_ge(m[0], m[1])
                        e.dma_start(todo[0][1], todo[0][2]).then_inc(todo[0][3], 16)
                        todo.pop(0)
                    if first_up + AHEAD <= i < first_up + AHEAD + NRAW:
                        frees += lent
                    for m in frees:
                        e.wait_ge(m[0], m[1])
                e.dma_start(t.raw, t.src).then_inc(s_ring[i % NRAW], 16)
            assert not todo
            for tb in range(2):
                e.wait_ge(out_marks[tb][0], out_marks[tb][1])
                e.dma_start(out[0, 128 * tb:128 * tb + 128, :], outs[tb]).then_inc(s_out, 16)
            e.wait_ge(s_out, 32)

        @block.tensor
        def _(e):
            P.play(e)

        @block.vector
        def _(e):
            D.play(e)

        @block.scalar
        def _(e):
            A.play(e)

        @block.gpsimd
        def _(e):
            G.play(e)


def _cols(v):
    return np.ascontiguousarray(v.reshape(-1, 128).T)


def _tiles(w, cols=128):
    k, n = w.shape
    return np.ascontiguousarray(w.reshape(k // 128, 128, n // cols, cols).transpose(2, 1, 0, 3)
                                .reshape(n // cols, 128, (k // 128) * cols))


def _constants():
    c, c2 = np.zeros((128, NCST), np.float32), np.zeros((128, NCS2), np.float32)

    def put(name, v):
        at, n = (CST if name in CST else CS2)[name]
        (c if name in CST else c2)[:v.shape[0], at:at + n] = v.reshape(v.shape[0], n)

    p = np.arange(128)
    t = np.arange(256)
    row, col = (t // 64).astype(np.float32), (t % 64).astype(np.float32)
    d = p % 32
    j = d % 16
    perm = np.zeros((128, 128), np.float32)
    perm[np.where(j < 8, p + 8, p - 8), p] = np.where(j < 8, -1.0, 1.0)
    put("perm1", perm)
    inv = (np.float32(10000.0) ** (-np.arange(0, 16, 2, dtype=np.float32) / np.float32(16))).astype(np.float32)
    ang = np.where((d // 16 == 0)[:, None], row[None, :], col[None, :]) * inv[j % 8][:, None]
    put("cos1", np.cos(ang.astype(np.float32)))
    put("sin1", np.sin(ang.astype(np.float32)))
    d = p % 64
    perm = np.zeros((128, 128), np.float32)
    perm[np.where(d < 32, p + 32, p - 32), p] = np.where(d < 32, -1.0, 1.0)
    put("perm2", perm)
    inv = (np.float32(10000.0) ** (-np.arange(16, dtype=np.float32) / np.float32(16))).astype(np.float32)
    i = d % 32
    ang = np.where((i < 16)[:, None], row[None, :], col[None, :]) * inv[i % 16][:, None]
    put("cos2", np.cos(ang.astype(np.float32)))
    put("sin2", np.sin(ang.astype(np.float32)))
    n = np.arange(256)
    th = 2 * np.pi * ((n[:, None] * n[None, :]) % 256) / 256
    cs = np.concatenate([np.cos(th), np.sin(th)], axis=1) / 16
    put("dftn", cs.reshape(2, 128, 512).transpose(1, 0, 2).reshape(128, 1024).astype(np.float32))
    n = np.arange(64)
    th = 2 * np.pi * ((n[:, None] * n[None, :]) % 64) / 64
    z = np.zeros((128, 128))
    z[:64, :64] = z[64:, 64:] = np.cos(th) / 8
    put("cd", z.astype(np.float32))
    z = np.zeros((128, 128))
    z[:64, :64] = z[64:, 64:] = -np.sin(th) / 8
    put("sd", z.astype(np.float32))
    s = 128 * np.arange(2)[None, :, None] + p[:, None, None]
    put("cf", (t[None, None, :] >= s).astype(np.float32).reshape(128, 512))
    put("cb", (t[None, None, :] <= s).astype(np.float32).reshape(128, 512))
    q, k = p[:, None], p[None, :]
    win = np.concatenate([np.where(k + 128 - q <= 128, 0.0, -1e30), np.where(q + 128 - k <= 128, 0.0, -1e30)], axis=1)
    put("win", win.astype(np.float32))
    sel = np.zeros((4, 4, 128), np.float32)
    for r in range(4):
        sel[r, r, :] = 1.0
    put("sel", sel.reshape(4, 512))
    return c, c2


def kernel(**inputs):
    import concourse.bacc as _bacc
    from concourse.bass_utils import run_bass_kernel_spmd as _run

    v = {k: np.asarray(a) for k, a in inputs.items()}
    pa = np.zeros((128, NPAR), np.float32)

    def put(name, a):
        at, n = PAR[name]
        pa[:a.shape[0], at:at + n] = a.reshape(a.shape[0], n)

    put("eye", np.eye(128, dtype=np.float32))
    put("ones", np.ones((128, 128), np.float32))
    p_ = np.arange(128)
    put("blk64", (p_[:, None] // 64 == p_[None, :] // 64).astype(np.float32))
    put("sum2", np.array([[1, 0], [1, 0], [0, 1], [0, 1]], np.float32))
    put("iota", np.tile(np.arange(128, dtype=np.float32), (128, 1)))
    put("c1", np.stack([_cols(v["c"][0]), _cols(v["c_ctx"])], axis=2))
    put("c2", np.stack([_cols(v["c_2"][0]), _cols(v["c_ctx_2"])], axis=2))
    put("finalg", _cols(v["final_g"]))
    for l in range(DEPTH):
        put(f"bada{l}", _cols(v["b_ada"][l]))
        put(f"n1g{l}", _cols(v["norm1_g"][l]))
        put(f"n2g{l}", _cols(v["norm2_g"][l]))
        put(f"sconv{l}", v["sconv_w"][l].reshape(3, 2, 128).transpose(2, 1, 0))
        put(f"subln{l}", np.concatenate([v["subln_g"][l]] * 2)[:, None])
        put(f"fconv{l}", v["ffn_conv_w"][l].reshape(3, 22, 128).transpose(2, 1, 0))
        put(f"lam{l}", np.stack([v[n][l] for n in ("lambda_q1", "lambda_q2", "lambda_k1", "lambda_k2")], axis=1))
        put(f"bs{l}", np.repeat(v["gmlp_bs"][l].reshape(2, 2, 1, 128), 64, axis=2).reshape(2, 128, 128)
            .transpose(1, 0, 2))
    put("bada2", _cols(v["b_ada_2"][0]))
    put("n1g2", _cols(v["norm_mix_g_2"][0]))
    put("n2g2", _cols(v["norm_ffn_g_2"][0]))
    put("gbias", v["b_mgates_2"][0].reshape(4, 4).T)
    put("mng", _cols(v["mlstm_norm_g_2"][0]))
    put("qg", np.concatenate([v["attn_q_norm_g_2"][0]] * 2)[:, None])
    put("kg", np.concatenate([v["attn_k_norm_g_2"][0]] * 2)[:, None])
    put("sink", np.tile(v["attn_sink_2"][0], (128, 1)))

    def toks(a):
        return a.reshape(256, 8, 128).transpose(2, 1, 0)

    c1, c2 = _constants()
    at, n = CST["ws"]
    c1[:, at:at + n] = v["gmlp_ws"].transpose(3, 0, 1, 2).reshape(128, 1024)
    arr = {"par": pa, "cst": c1, "cs2": c2}
    arr["xt"] = np.concatenate([toks(v["x"][0]), toks(v["ctx"][0])], axis=2).reshape(128, 4096)
    arr["ctx2t"] = toks(v["ctx_2"][0]).reshape(128, 2048)
    for l in range(DEPTH):
        arr[f"wada{l}"] = _tiles(v["w_ada"][l])
        arr[f"win{l}"] = _tiles(v["w_in"][l])
        arr[f"wout{l}"] = _tiles(v["w_out"][l])
        arr[f"wup{l}"] = _tiles(v["ffn_w_up"][l])
        wd = np.zeros((3072, 1024), np.float32)
        wd[:2816] = v["ffn_w_down"][l]
        arr[f"wdn{l}"] = wd.reshape(3, 8, 128, 8, 128).transpose(0, 3, 2, 1, 4).reshape(24, 128, 1024)
    arr["wada2"] = _tiles(v["w_ada_2"][0])
    w = v["w_in_2"][0]
    qo = np.concatenate([np.arange(64 * h, 64 * h + 64) for c in range(4) for h in (c, c + 4)])
    arr["win2"] = _tiles(np.concatenate([w[:, 0:2048], w[:, 2064:2576][:, qo], w[:, 2576:]], axis=1))
    arr["wg2"] = w[:, 2048:2064].reshape(8, 128, 16).transpose(1, 0, 2).reshape(128, 128)
    arr["wbr2"] = _tiles(np.concatenate([v["w_branch_m_2"][0], v["w_branch_a_2"][0][qo]], axis=0))
    arr["wout2"] = _tiles(v["w_out_2"][0])
    arr["wq2"] = _tiles(v["peer_w_query_2"][0])
    arr["keys2"] = v["peer_sub_keys_2"][0].reshape(2, 8, 128, 128).transpose(0, 3, 1, 2).reshape(2, 128, 1024)
    arr["ut2"] = np.ascontiguousarray(v["peer_u_2"][0].reshape(128, 128, 8, 128).transpose(0, 3, 2, 1)
                                      .reshape(128, 128, 1024))
    arr["v2"] = np.ascontiguousarray(v["peer_v_2"][0].reshape(128, 128, 1024))

    nc = _bacc.Bacc("TRN2", target_bir_lowering=False, num_devices=1)
    feeds, args = {}, {}
    for name, a in arr.items():
        a = np.ascontiguousarray(a)
        feeds[f"in_{name}"] = a
        args[name] = nc.dram_tensor(f"in_{name}", a.shape, mybir.dt.from_np(a.dtype), kind="ExternalInput").ap()
    out = nc.dram_tensor("out_0", (1, 256, 1024), F32, kind="ExternalOutput").ap()
    build(nc, args, out)
    r = _run(nc, [feeds], core_ids=[0])
    return r.results[0]["out_0"]
```

```python
import math
from contextlib import ExitStack
from functools import partial

import numpy as np
import concourse.bass as bass
from concourse import mybir

F32 = mybir.dt.float32
F32R = mybir.dt.float32r
U32 = mybir.dt.uint32
ALU = mybir.AluOpType
ACT = mybir.ActivationFunctionType
AX_X = mybir.AxisListType.X

DEPTH = 2
EPS = 1e-6
NRAW = 4
NSPLIT = 3
AHEAD = 2
TILE = 1024


class Lane:

    def __init__(self, sem):
        self.sem = sem
        self.ops = []
        self.n = 0
        self.seen = {}

    @property
    def last(self):
        return (self.sem, self.n)

    def wait(self, *marks):
        for m in marks:
            if m is None or m[1] == 0:
                continue
            if self.seen.get(m[0].name, 0) < m[1]:
                self.seen[m[0].name] = m[1]
                self.ops.append((None, m))

    def __call__(self, fn, *marks, inc=True):
        self.wait(*marks)
        if inc:
            self.n += 1
        self.ops.append((fn, inc))
        return self.last

    def play(self, eng):
        for fn, x in self.ops:
            if fn is None:
                eng.wait_ge(x[0], x[1])
            else:
                ins = fn()
                if x:
                    ins.then_inc(self.sem, 1)


class Bank:
    def __init__(self, t):
        self.t = t
        self.free = ()

    def __getitem__(self, at):
        return self.t[at]

    def release(self, *marks):
        self.free = marks


def _fields(spec):
    at, out = 0, {}
    for name, n in spec:
        out[name] = (at, n)
        at += n
    return out, at


PAR, NPAR = _fields(
    [("eye", 128), ("ones", 128), ("blk64", 128), ("iota", 128), ("sum2", 2), ("c1", 16), ("c2", 16), ("finalg", 8)]
    + [(f"{n}{l}", k) for l in range(DEPTH) for n, k in
       (("bada", 48), ("n1g", 8), ("n2g", 8), ("sconv", 6), ("subln", 1), ("fconv", 66), ("lam", 4))]
    + [("bada2", 48), ("n1g2", 8), ("n2g2", 8), ("gbias", 4), ("mng", 4), ("qg", 1), ("kg", 1), ("sink", 8)])

CST, NCST = _fields([("perm1", 128), ("cos1", 256), ("sin1", 256), ("dftn", 1024), ("cd", 128), ("sd", 128),
                     ("ws", 1024), ("bs", 512)])
CS2, NCS2 = _fields([("perm2", 128), ("cos2", 256), ("sin2", 256), ("cf", 512), ("cb", 512), ("win", 256),
                     ("sel", 512)])


def build(nc, ins, out):
    with ExitStack() as ctx:
        order = program(nc, ctx, ins, out, None)
    with ExitStack() as ctx:
        program(nc, ctx, ins, out, order)


def program(nc, ctx, ins, out, order):
    def sb(name, n, dt=F32, at=ctx):
        return at.enter_context(nc.sbuf_tensor(name if order else name + "_", [128, n], dt))

    def sem(name):
        return ctx.enter_context(nc.semaphore(name if order else name + "_"))

    RAW = sb("RAW", NRAW * TILE)
    TH = sb("TH", NSPLIT * TILE, F32R)
    TL = sb("TL", NSPLIT * TILE, F32R)
    HXh = sb("HXh", 2048, F32R)
    HXl = sb("HXl", 2048, F32R)
    XX = sb("XX", 2048)
    PT = sb("P", NPAR)
    ADAS = [sb(f"ADA{i}", 96) for i in range(2)]
    MOD = sb("MOD", 64)
    SM = sb("SM", 56)
    CC = sb("CC", 32, F32R)
    early = ExitStack()
    XT = sb("X", 4096, at=early)
    HTh = sb("Hh", 4096, F32R, at=early)
    HTl = sb("Hl", 4096, F32R, at=early)
    CT = sb("C", NCST, at=early)
    X = XT[:, :].rearrange("p (k t) -> p k t", k=8)
    Hh = HTh[:, :].rearrange("p (k t) -> p k t", k=8)
    Hl = HTl[:, :].rearrange("p (k t) -> p k t", k=8)

    banks = [Bank(ctx.enter_context(nc.psum_tensor(f"ps{i}" if order else f"ps{i}_", [128, 512], F32))) for i in range(8)]
    ada_bank = banks.pop()
    idle = list(banks)

    def take():
        return idle.pop(0)

    def give(b, *marks):
        b.release(*marks)
        idle.append(b)

    P, D, A, G = (Lane(sem(f"s_{n}")) for n in ("pe", "dve", "act", "pool"))
    s_in = sem("s_in")
    s_x = sem("s_x")
    s_k = sem("s_k")
    s_c2 = sem("s_c2")
    s_out = sem("s_out")
    s_c = sem("s_c")
    s_ring = [sem(f"s_ring{i}") for i in range(NRAW)]

    def par(name, a=0, b=None):
        at, n = PAR[name]
        return PT[:, at + a:at + (n if b is None else b)]

    def cst(name, a=0, b=None):
        at, n = (CST if name in CST else CS2)[name]
        return CT[:, at + a:at + (n if b is None else b)]

    eye, ones, iota = par("eye"), par("ones"), par("iota")

    tiles = []

    class Tile:
        pass

    def arrive(i):
        t = Tile()
        t.src, t.n, split = order[i] if order else (None, TILE, True)
        t.raw = RAW[:, (i % NRAW) * TILE:(i % NRAW) * TILE + t.n]
        t.ready = (s_ring[i % NRAW], 16 * (i // NRAW + 1))
        t.slot = nsplit[0] % NSPLIT
        t.done = None
        t.freed = None
        tiles.append(t)
        if split:
            o = t.slot * TILE
            t.hi, t.lo = TH[:, o:o + t.n], TL[:, o:o + t.n]
            before = holders[t.slot]
            nsplit[0] += 1
            a = A(partial(nc.scalar.activation, t.hi, t.raw, ACT.Copy), t.ready, before and before.done)
            if low_on_pool[0] and i % low_on_pool[0] == 0:
                t.split = G(partial(nc.gpsimd.tensor_tensor, t.lo, t.raw, t.hi.bitcast(F32), ALU.subtract), a)
            else:
                t.split = D(partial(nc.vector.tensor_tensor, t.lo, t.raw, t.hi.bitcast(F32), ALU.subtract), a)
            t.freed = t.split
            holders[t.slot] = t

    holders = [None] * NSPLIT
    nsplit = [0]
    low_on_pool = [0]
    asked = []

    def load(src, n=TILE, split=True, ahead=AHEAD):
        i = len(asked)
        asked.append((src, n, split))
        if order:
            assert order[i][1:] == (n, split)
        while len(tiles) <= min(i + (ahead if order else 0), len(order or asked) - 1):
            arrive(len(tiles))
        return tiles[i]

    LOADED = (s_in, 16)

    def mm(o, l, r, first, last, *marks, skip=False, inc=None):
        return P(partial(nc.tensor.matmul, o, l, r, start=first, stop=last, skip_group_check=skip), *marks,
                 inc=last if inc is None else inc)

    def mm3(o, l, r, first, last, *marks, skip=False, inc=None):
        (lh, ll), (rh, rl) = l, r
        mm(o, lh, rl, first, False, *marks, skip=skip)
        mm(o, ll, rh, False, False, skip=skip)
        return mm(o, lh, rh, False, last, skip=skip, inc=last if inc is None else inc)

    def split_to(hi, lo, src, *marks, pool=False):
        a = A(partial(nc.scalar.activation, hi, src, ACT.Copy), *marks)
        if pool:
            return G(partial(nc.gpsimd.tensor_tensor, lo, src, hi.bitcast(F32), ALU.subtract), a, *marks)
        return D(partial(nc.vector.tensor_tensor, lo, src, hi.bitcast(F32), ALU.subtract), a, *marks)

    def fence():
        marks = [P.last, D.last, A.last, G.last]
        for lane in (P, D, A, G):
            lane.wait(*marks)

    def scratch(at, tag):
        count = [0]

        def new(n, dt=F32):
            count[0] += 1
            return sb(f"{tag}{count[0]}", n, dt, at)[:, :]
        return new

    base = scratch(early, "b")
    wsT = [cst("ws", 512 * l, 512 * l + 512) for l in range(DEPTH)]
    SQ = [base(512) for _ in range(3)]
    STD, RSTD = base(512), base(512)
    sq_free = [None] * 3
    sq_n = [0]
    sq_busy = [None] * 3

    epsc = SM[:, 0:1]
    d_eps = D(partial(nc.vector.memset, epsc, EPS))
    for lane in (P, D, A, G):
        lane.wait(LOADED)
    A.wait(d_eps)

    def stats(src, k, t0, t1, lhs, div, x_ready, free=None):
        n = t1 - t0
        b = take()
        for i in range(k):
            j = sq_n[0] % 3
            sq_n[0] += 1
            sq = SQ[j][:, 0:n]
            s = src(i)
            a = A(partial(nc.scalar.activation, sq, s, ACT.Square), x_ready, sq_free[j], sq_busy[j])
            sq_free[j] = mm(b[:, 0:n], lhs, sq, i == 0, i == k - 1, a, *b.free, inc=True)
        a = A(partial(nc.scalar.activation, STD[:, 0:n], b[:, 0:n], ACT.Sqrt, bias=epsc, scale=1.0 / div), P.last, D.last)
        give(b, a)
        return D(partial(nc.vector.reciprocal, RSTD[:, 0:n], STD[:, 0:n]), a, D.last, free)

    adaq = []
    LEFT = 8
    SC = SM[:, 8:24]
    cur = [0]
    arow = base(512)
    arow_free = [None]

    def ada_begin(cname):
        cc = par(cname)
        t = A(partial(nc.scalar.activation, SC, cc, ACT.Silu), P.last, D.last)
        c4 = CC[:, :].rearrange("p (k h) -> p k h", h=2)
        hi, lo = c4[:, :, 0:1], c4[:, :, 1:2]
        s3 = SC.rearrange("p (k o) -> p k o", o=1)
        return split_to(hi, lo, s3, t)

    def ada_step(src, i, ready, bias, buf):
        def go():
            if ready[0] is None:
                ready[0] = ada_begin(ready[1])
            w = load(src[i])
            wh, wl = (v.rearrange("p (k m) -> p k m", k=8) for v in (w.hi, w.lo))
            o = ada_bank[0:4, 128 * (i % 4):128 * (i % 4) + 128]
            for k in range(8):
                c = CC[:, 4 * k:4 * k + 4]
                mm(o, c, wl[:, k, :], k == 0, False, w.split, ready[0], *ada_bank.free)
                mm(o, c, wh[:, k, :], False, k == 7)
            w.done = P.last
            if i % 4 == 3:
                g = i // 4
                r = arow[0:4, :]
                a = A(partial(nc.scalar.activation, r, ada_bank[0:4, :], ACT.Copy), P.last, arow_free[0])
                ada_bank.release(a)
                adaw.append((g, r, a, bias, buf))
            if i % 4 == 1 or i == 47:
                ada_columns()
        return go

    adaw = []
    ada_got = {}

    def ada_columns():
        while adaw:
            g, r, a, bias, buf = adaw.pop(0)
            b = take()
            for z in range(4):
                mm(b[:, 2 * z:2 * z + 2], r[:, 128 * z:128 * z + 128], par("sum2")[0:4, :], True, True, a, *b.free)
            p = P.last
            arow_free[0] = p
            o = ADAS[buf][:, 8 * g:8 * g + 8].rearrange("p (m c) -> p m c", c=2)
            bb = par(bias, 4 * g, 4 * g + 4).rearrange("p (m o) -> p m o", o=1).to_broadcast([128, 4, 2])
            t = D(partial(nc.vector.tensor_tensor, o, b[:, 0:8].rearrange("p (m c) -> p m c", c=2), bb, ALU.add), p)
            give(b, t)

    def background(n=1, left=0):
        for _ in range(n):
            if len(adaq) > left:
                adaq.pop(0)()

    def drain(left=0):
        background(len(adaq), left)
        ada_columns()

    def adac(part, m, s):
        return ADAS[cur[0]][:, (8 * part + m) * 2 + s:(8 * part + m) * 2 + s + 1]

    def mods(g, part, slot):
        o = MOD[:, 16 * slot:16 * slot + 16].rearrange("p (m c) -> p m c", c=2)
        s = ADAS[cur[0]][:, 16 * part:16 * part + 16].rearrange("p (m c) -> p m c", c=2)
        gg = par(g).rearrange("p (m o) -> p m o", o=1).to_broadcast([128, 8, 2])
        t = D(partial(nc.vector.tensor_scalar, o, s, 1.0, None, ALU.add), D.last, A.last)
        return D(partial(nc.vector.tensor_tensor, o, o, gg, ALU.mult), t)

    VT = SQ[0:2]
    vt_free = [None, None]

    def modulated(slot, shift, streams, x_ready, dst=None, r=None, left=0):
        t1 = 256 * len(streams)
        dh, dl = dst or (Hh, Hl)
        r = r or stats(lambda i: X[:, i, 0:t1], 8, 0, t1, ones, 1024.0, x_ready)
        marks = []
        h_free = P.last
        background(1, left)
        for k in range(8):
            v = VT[k % 2][:, 0:t1]
            t = D(partial(nc.vector.tensor_tensor, v, X[:, k, 0:t1], RSTD[:, 0:t1], ALU.mult), r,
                  vt_free[k % 2])
            for s in streams:
                vs = v[:, 256 * s:256 * s + 256]
                sc = MOD[:, 16 * slot + 2 * k + s:16 * slot + 2 * k + s + 1]
                sh = adac(shift, k, s)
                u = D(partial(nc.vector.tensor_scalar, vs, vs, sc, sh, ALU.mult, ALU.add), t)
            m = split_to(dh[:, k, 0:t1], dl[:, k, 0:t1], v, u, h_free, pool=True)
            vt_free[k % 2] = sq_busy[k % 2] = m
            marks.append(m)
        return marks

    def residual(b, m, gate, streams, last_p):
        for s in streams:
            o = X[:, m, 256 * s:256 * s + 256]
            i = b[:, 256 * s:256 * s + 256]
            t = D(partial(nc.vector.scalar_tensor_tensor, out=o, in0=i, scalar=adac(gate, m, s), in1=o,
                                                                 op0=ALU.mult, op1=ALU.add), last_p, D.last)
        give(b, t)
        return t

    def project(src, rhs, T, hmarks):
        w = load(src)
        b = take()
        wh, wl = (v.rearrange("p (k m) -> p k m", k=8) for v in (w.hi, w.lo))
        for k in range(8):
            p = mm3(b[:, 0:T], (wh[:, k, :], wl[:, k, :]), rhs(k), k == 0, k == 7, w.split, hmarks[k], *b.free)
        w.done = p
        return b, p

    def project2(srcs, rhs, T, hmarks):
        w = [load(src, ahead=1) for src in srcs]
        b = [take() for _ in srcs]
        wv = [[v.rearrange("p (k m) -> p k m", k=8) for v in (t.hi, t.lo)] for t in w]
        for k in range(8):
            for z in range(2):
                p = mm3(b[z][:, 0:T], (wv[z][0][:, k, :], wv[z][1][:, k, :]), rhs(k), k == 0, k == 7, w[z].split,
                        hmarks[k], *b[z].free, inc=k == 7)
                if k == 7:
                    w[z].done = p
        return [(b[z], w[z].done) for z in range(2)]

    def hk(T):
        return lambda k: (Hh[:, k, 0:T], Hl[:, k, 0:T])

    TR = SQ[0:2]
    tr_n = [0]

    def rows(src, ntb, hmarks, dst, lane, fn):
        n = 128 * ntb
        i = tr_n[0] % 2
        tr_n[0] += 1
        b, p = project(src, hk(n), n, hmarks)
        a = A(partial(nc.scalar.activation, TR[i][:, 0:n], b[:, 0:n], ACT.Copy), p, sq_free[i],
              sq_busy[i], vt_free[i])
        give(b, a)

        def turn_rows():
            b = take()
            for tb in range(ntb):
                c = slice(128 * tb, 128 * tb + 128)
                p = P(partial(nc.tensor.transpose, b[:, c], TR[i][:, c], eye), a, *b.free)
            vt_free[i] = sq_busy[i] = p
            t = lane(fn(dst, b[:, 0:n].rearrange("p (b c) -> p b c", c=128)), p)
            give(b, t)
            return t
        return turn_rows

    def conv_taps(o, src, wcol, n_str, first, first_mark, psum_mark):
        ov = o.rearrange("p (s t) -> p s t", t=256)
        sv = src.rearrange("p (s t) -> p s t", t=256)
        t = D(partial(nc.vector.scalar_tensor_tensor, out=ov[:, :, 1:256], in0=sv[:, :, 0:255], scalar=wcol(0),
                                               in1=ov[:, :, 1:256], op0=ALU.mult, op1=ALU.add),
              first_mark, psum_mark)
        return D(partial(nc.vector.scalar_tensor_tensor, out=ov[:, :, 0:255], in0=sv[:, :, 1:256], scalar=wcol(2),
                                                  in1=ov[:, :, 0:255], op0=ALU.mult, op1=ALU.add), t)

    ready = [None, "c1"]
    adaq += [ada_step(ins["wada0"], i, ready, "bada0", 0) for i in range(48)]
    background(2)
    first_r = stats(lambda i: X[:, i, :], 8, 0, 512, ones, 1024.0, (s_x, 16))
    drain(32)
    for lane in (P, A, D):
        lane.wait((s_x, 16))
    x_ready = None
    consts_free = []

    for l in range(DEPTH):
        lam_init = 0.8 - 0.6 * math.exp(-0.3 * l)
        full = [0, 1]
        streams = [0, 1] if l < DEPTH - 1 else [0]
        T = 256 * len(streams)
        NTB = T // 128
        phase = ExitStack()
        ar = scratch(phase, f"l{l}a")
        MIX = ar(4096).rearrange("p (k t) -> p k t", k=8)
        temps = ExitStack()
        ar = scratch(temps, f"l{l}b")
        prob = [ar(1024) for _ in range(2)]
        att = [ar(512) for _ in range(2)]
        attT = [ar(512) for _ in range(2)]
        q_f = ar(1024).rearrange("p (j t) -> p j t", j=2)
        k_f = ar(1024).rearrange("p (j t) -> p j t", j=2)
        v_d = ar(1024).rearrange("p (b c) -> p b c", b=4)
        v_a = ar(1024).rearrange("p (b c) -> p b c", b=4)
        u_f = ar(1024).rearrange("p (j t) -> p j t", j=2)
        f_c = XX[:, 0:1024].rearrange("p (b c) -> p b c", b=4)
        PQ = [ar(512) for _ in range(2)]
        bx = XX[:, 1024:2048].rearrange("p (j t) -> p j t", j=2)
        cv = ar(1024).rearrange("p (j t) -> p j t", j=2)
        rt = [SQ[2][:, 256 * i:256 * i + 256] for i in range(2)]
        o_d = ar(1024).rearrange("p (j t) -> p j t", j=2)
        st = ar(64)

        mods(f"n1g{l}", 1, 0)
        lm = par(f"lam{l}")
        lp = SM[:, 24:26]
        t = D(partial(nc.vector.tensor_tensor, lp[0:32, :], lm[0:32, 0:2], lm[0:32, 2:4], ALU.mult), D.last, P.last)
        b = take()
        p = mm(b[:, 0:2], ones[0:32, :], lp[0:32, :], True, True, t, *b.free)
        le = SM[:, 26:28]
        a = A(partial(nc.scalar.activation, le, b[:, 0:2], ACT.Exp), p, D.last)
        give(b, a)
        nlam = SM[:, 28:29]
        t = D(partial(nc.vector.tensor_tensor, nlam, le[:, 1:2], le[:, 0:1], ALU.subtract), a, D.last)
        D(partial(nc.vector.tensor_scalar, nlam, nlam, -lam_init, None, ALU.add), t)
        sg = SM[:, 29:30]
        d_sg = D(partial(nc.vector.tensor_scalar, sg, par(f"subln{l}"), 1.0 - lam_init, None, ALU.mult))

        hm = modulated(0, 0, full, x_ready, r=None if l else first_r)
        for lane in (P, A, D):
            lane.wait((s_k, 16))
        x2_free = (P.last, D.last, A.last)
        low_on_pool[0] = 2
        win = ins[f"win{l}"]

        def rope(dst, b, p, j, ctx_too):
            n = 512 if ctx_too else 256
            c = A(partial(nc.scalar.activation, dst[:, j, 0:n], b[:, 0:n], ACT.Copy), p, D.last)
            give(b, c)

            def rest():
                b2 = take()
                p2 = mm(b2[:, 0:256], cst("perm1"), dst[:, j, 0:256], True, True, c, *b2.free)
                t = D(partial(nc.vector.tensor_tensor, rt[j], b2[:, 0:256], cst("sin1"), ALU.mult), p2, D.last,
                      sq_free[2])
                give(b2, t)
                t2 = D(partial(nc.vector.tensor_tensor, dst[:, j, 0:256], dst[:, j, 0:256], cst("cos1"), ALU.mult),
                       c, p2)
                sq_busy[2] = D(partial(nc.vector.tensor_tensor, dst[:, j, 0:256], dst[:, j, 0:256], rt[j], ALU.add),
                               t, t2)
                return sq_busy[2]
            return rest

        gelu = lambda o, i: partial(nc.scalar.activation, o, i, ACT.Gelu_apprx_tanh)
        acopy_ = lambda o, i: partial(nc.scalar.activation, o, i, ACT.Copy)
        dcopy_ = lambda o, i: partial(nc.vector.tensor_copy, o, i)
        for j, (b, p) in enumerate(project2([win[0], win[1]], hk(T), T, hm)):
            a = A(gelu(u_f[:, j, 0:T], b[:, 0:T]), p)
            give(b, a)
        u_ready = A.last
        ends = [rows(win[2 + j], NTB, hm, v_a[:, 0:NTB, 128 * j:128 * j + 128], A, gelu) for j in range(2)]
        va_ready = [end() for end in ends][-1]
        n = NTB * 256
        fl = v_a[:, 0:NTB, :].rearrange("p b (h d) -> p (b h) d", d=64)
        sqv = cv.rearrange("p j t -> p (j t)")[:, 0:n].rearrange("p (b d) -> p b d", d=64)
        t = D(partial(nc.vector.tensor_tensor, sqv, fl, fl, ALU.mult), va_ready)
        sv, sv2 = st[:, 0:4 * NTB], st[:, 16:16 + 4 * NTB]
        t = D(partial(nc.vector.tensor_reduce, sv, sqv, AX_X, ALU.add), t)
        a = A(partial(nc.scalar.activation, sv2, sv, ACT.Sqrt, bias=epsc, scale=1.0 / 64), t)
        t = D(partial(nc.vector.reciprocal, sv, sv2), a, t)
        va_ok = D(partial(nc.vector.tensor_tensor, fl, fl, sv.rearrange("p (b o) -> p b o", o=1)
                                            .to_broadcast([128, 4 * NTB, 64]), ALU.mult), t)
        rest = None
        for z, dst, n in ((12, q_f, T), (14, k_f, 512)):
            for j in range(2):
                b, p = project(win[z + j], hk(n), n, hm)
                if rest:
                    rest()
                rest = rope(dst, b, p, j, n == 512)
        ends = [rows(win[16 + j], 4, hm, v_d[:, :, 128 * j:128 * j + 128], A, acopy_) for j in range(2)]
        q_ok = k_ok = rest()
        vd_ok = [end() for end in ends][-1]

        fill = []

        def mix_a(j, l=l, NTB=NTB, T=T, va_ok=va_ok, u_ready=u_ready, v_a=v_a, u_f=u_f, MIX=MIX):
            b = take()
            for tb in range(NTB):
                for hh in range(2):
                    h = 2 * j + hh
                    p = mm(b[64 * hh:64 * hh + 64, 128 * tb:128 * tb + 128], v_a[:, tb, 64 * h:64 * h + 64],
                           wsT[l][:, 128 * h:128 * h + 128], True, True, va_ok, *b.free)
            bs = cst("bs", 256 * l + 128 * j, 256 * l + 128 * j + 128).rearrange("p (o t) -> p o t", o=1)\
                .to_broadcast([128, NTB, 128])
            o = MIX[:, j, 0:T].rearrange("p (b t) -> p b t", t=128)
            t = D(partial(nc.vector.tensor_tensor, o, b[:, 0:T].rearrange("p (b t) -> p b t", t=128), bs, ALU.add), p)
            give(b, t)
            D(partial(nc.vector.tensor_tensor, MIX[:, j, 0:T], MIX[:, j, 0:T], u_f[:, j, 0:T], ALU.mult), t, u_ready)

        fill += [lambda: mix_a(0), lambda: mix_a(1)]
        hold = {}

        def four(j, NTB=NTB, f_c=f_c, hm=hm, win=win, hold=hold, dcopy_=dcopy_):
            hold[("f", j)] = rows(win[10 + j], NTB, hm, f_c[:, 0:NTB, 128 * j:128 * j + 128], D, dcopy_)

        def four1(hold=hold):
            hold[("f", 0)]()
            hold["f_ok"] = hold[("f", 1)]()

        def four2(s, j, f_c=f_c, PQ=PQ, MIX=MIX, hold=hold):
            b = take()
            for c in range(2):
                p = mm(b[:, :], f_c[:, 2 * s + c, 128 * j:128 * j + 128], cst("dftn", 512 * c, 512 * c + 512),
                       c == 0, c == 1, hold["f_ok"], *b.free)
            pq = PQ[j]
            t = A(partial(nc.scalar.activation, pq, b[:, :], ACT.Copy), p, hold.get(("pq", j)))
            give(b, t)
            background(1, LEFT + 3)
            b2 = take()
            mm(b2[:, 0:256], cst("cd"), pq[:, 0:256], True, False, t, *b2.free)
            p = mm(b2[:, 0:256], cst("sd"), pq[:, 256:512], False, True)
            hold[("pq", j)] = p
            o = MIX[:, 4 + j, 256 * s:256 * s + 256]
            t = A(partial(nc.scalar.activation, o, b2[:, 0:256], ACT.Copy), p)
            give(b2, t)

        fill += [lambda h=h: four(h) for h in range(2)] + [four1]
        fill += [lambda s=s, j=j: four2(s, j) for s in streams for j in range(2)]

        def gate_b(g, j, l=l, T=T, bx=bx, cv=cv, MIX=MIX, hm=hm, win=win, hold=hold):
            b, p = project(win[2 * g + j], hk(T), T, hm)
            if g == 2:
                t = A(partial(nc.scalar.activation, bx[:, j, 0:T], b[:, 0:T], ACT.Copy), p)
                hold[("bx", j)] = t
            elif g == 4:
                t = D(partial(nc.vector.tensor_tensor, bx[:, j, 0:T], bx[:, j, 0:T], b[:, 0:T], ALU.mult), p,
                      hold[("bx", j)])
                o = cv[:, j, 0:T]
                wc = lambda i, l=l, j=j: par(f"sconv{l}", 3 * j + i, 3 * j + i + 1)
                t2 = D(partial(nc.vector.tensor_scalar, o, bx[:, j, 0:T], wc(1), None, ALU.mult), t)
                hold[("cv", j)] = conv_taps(o, bx[:, j, 0:T], wc, len(streams), None, t2, t)
            else:
                t = D(partial(nc.vector.tensor_tensor, MIX[:, 2 + j, 0:T], cv[:, j, 0:T], b[:, 0:T], ALU.mult), p,
                      hold[("cv", j)])
            give(b, t)

        fill += [lambda g=g, j=j: gate_b(g, j) for g in (2, 4, 3) for j in range(2)]

        SCALE = 32 ** -0.5
        units = [(s, qb, h) for s in streams for h in range(4) for qb in range(2)]
        state = {}
        ring_free = {}

        def scores(n, q_f=q_f, k_f=k_f, units=units, state=state, q_ok=q_ok, k_ok=k_ok):
            s, qb, h = units[n]
            j, r0 = h // 2, 64 * (h % 2)
            cols = 512 if s == 0 else 256
            k0 = 0 if s == 0 else 256
            bs = [take(), take()]
            views = []
            for m in range(2):
                v = bs[m][:, 0:cols]
                r = r0 + 32 * m
                p = P(partial(nc.tensor.matmul, 
                    v, q_f[r:r + 32, j, 256 * s + 128 * qb:256 * s + 128 * qb + 128],
                    k_f[r:r + 32, j, k0:k0 + cols], start=True, stop=True, tile_position=(r, 0)),
                    q_ok, k_ok, *bs[m].free)
                views.append(v)
            state[n] = (bs, views, p)

        def softmax(n, units=units, state=state, prob=prob, st=st, ring_free=ring_free):
            s, qb, h = units[n]
            bs, views, p = state[n]
            cols = 512 if s == 0 else 256
            i = n % 2
            x0 = 32 + 8 * i
            mx, sm_ = st[:, x0:x0 + 2], st[:, x0 + 2:x0 + 4]
            pr = [prob[i][:, 0:cols], prob[i][:, 512:512 + cols]]
            for m in range(2):
                t = D(partial(nc.vector.tensor_reduce, mx[:, m:m + 1], views[m], AX_X, ALU.max), p,
                      ring_free.get(("st", i)))
            t = D(partial(nc.vector.tensor_scalar, mx, mx, -SCALE, None, ALU.mult), t)
            for m in range(2):
                a = A(partial(nc.scalar.activation, pr[m], views[m], ACT.Exp, bias=mx[:, m:m + 1], scale=SCALE,
                                                  accum_out=sm_[:, m:m + 1]), t, ring_free.get(("prob", i)))
            for b in bs:
                give(b, a, t)
            state[("e", n)] = a

        def normal(n, units=units, state=state, prob=prob, att=att, st=st, nlam=nlam, ring_free=ring_free):
            cols = 512 if units[n][0] == 0 else 256
            i = n % 2
            x0 = 32 + 8 * i
            sm_, rc = st[:, x0 + 2:x0 + 4], st[:, x0 + 4:x0 + 6]
            pr = [prob[i][:, 0:cols], prob[i][:, 512:512 + cols]]
            t = D(partial(nc.vector.reciprocal, rc, sm_), state[("e", n)])
            t2 = D(partial(nc.vector.tensor_tensor, rc[:, 1:2], rc[:, 1:2], nlam, ALU.mult), t)
            aa = att[i][:, 0:cols]
            t = D(partial(nc.vector.tensor_scalar, aa, pr[0], rc[:, 0:1], None, ALU.mult), t, t2,
                  ring_free.get(("att", i)))
            t = D(partial(nc.vector.scalar_tensor_tensor, out=aa, in0=pr[1], scalar=rc[:, 1:2], in1=aa,
                                                   op0=ALU.mult, op1=ALU.add), t)
            ring_free[("prob", i)] = t
            ring_free[("st", i)] = t
            state[("a", n)] = t

        def turn(n, units=units, state=state, att=att, attT=attT, ring_free=ring_free):
            s, qb, h = units[n]
            i = n % 2
            nk = 4 if s == 0 else 2
            b = take()
            for c in range(nk):
                p = P(partial(nc.tensor.transpose, b[:, 128 * c:128 * c + 128], att[i][:, 128 * c:128 * c + 128],
                                                 eye), state[("a", n)], *b.free)
            ring_free[("att", i)] = p
            a = A(partial(nc.scalar.activation, attT[i][:, 0:128 * nk], b[:, 0:128 * nk], ACT.Copy), p,
                  ring_free.get(("attT", i)))
            give(b, a)
            state[("t", n)] = a

        def apply(n, units=units, state=state, attT=attT, v_d=v_d, o_d=o_d, ring_free=ring_free, vd_ok=vd_ok):
            s, qb, h = units[n]
            i = n % 2
            nk = 4 if s == 0 else 2
            a = state[("t", n)]
            j, r0 = h // 2, 64 * (h % 2)
            b2 = take()
            for c in range(nk):
                tb = c + (0 if s == 0 else 2)
                p = mm(b2[r0:r0 + 64, 0:128], v_d[:, tb, 64 * h:64 * h + 64],
                       attT[i][:, 128 * c:128 * c + 128], c == 0, c == nk - 1, a, vd_ok, *b2.free)
            ring_free[("attT", i)] = p
            state[("o", n)] = b2, p

        def keep_o(n, units=units, state=state, o_d=o_d):
            s, qb, h = units[n]
            b2, p = state[("o", n)]
            j, r0 = h // 2, 64 * (h % 2)
            t = D(partial(nc.vector.tensor_copy, o_d[r0:r0 + 64, j, 256 * s + 128 * qb:256 * s + 128 * qb + 128],
                          b2[r0:r0 + 64, 0:128]), p)
            give(b2, t)

        for n in range(2):
            scores(n)
            softmax(n)
            normal(n)
        for n in range(len(units)):
            turn(n)
            if n + 2 < len(units):
                scores(n + 2)
                softmax(n + 2)
            for _ in range(math.ceil(len(fill) / (len(units) - n))):
                fill.pop(0)()
            background(math.ceil((len(adaq) - LEFT - 3) / (len(units) - n)), LEFT + 3)
            if n + 2 < len(units):
                normal(n + 2)
            if n:
                keep_o(n - 1)
            apply(n)
        keep_o(len(units) - 1)
        drain(LEFT + 3)
        for j in range(2):
            background()
            r = stats(lambda i, j=j: o_d[:, j, 0:T], 1, 0, T, par("blk64"), 64.0, D.last)
            t = D(partial(nc.vector.scalar_tensor_tensor, out=MIX[:, 6 + j, 0:T], in0=o_d[:, j, 0:T], scalar=sg,
                                                        in1=RSTD[:, 0:T], op0=ALU.mult, op1=ALU.mult), r, d_sg)
        v4 = lambda t: t.rearrange("p (k t) -> p k t", k=4)
        fence()
        temps.close()
        drain(LEFT)
        mods(f"n2g{l}", 4, 1)
        low_on_pool[0] = 0
        d_mix = D.last
        mixp = []
        Mh2, Ml2 = (v4(sb(f"l{l}m{z}", 2048, F32R, phase)[:, :]) for z in "hl")
        Mh1, Ml1 = (v4(t[:, :]) for t in (HXh, HXl))
        for k in range(8):
            h_, l_ = (Mh1, Ml1) if k < 4 else (Mh2, Ml2)
            m_ = split_to(h_[:, k % 4, 0:T], l_[:, k % 4, 0:T], MIX[:, k, 0:T], D.last if k == 0 else d_mix, A.last
                          if k == 0 else None, P.last if k == 0 else None)
            mixp.append((h_[:, k % 4, 0:T], l_[:, k % 4, 0:T], m_))
        wo, rhs, mm_ = ins[f"wout{l}"], lambda k: mixp[k][0:2], [z[2] for z in mixp]
        first = project2([wo[0], wo[1]], rhs, T, mm_)
        for i in range(8):
            b, p = first[i] if i < 2 else project(wo[i], rhs, T, mm_)
            x_ready = residual(b, i, 2, streams, p)

        fence()
        hm = modulated(1, 3, streams, x_ready)
        if l == DEPTH - 1:
            consts_free.append((P.last, D.last, A.last))
        phase.close()
        phase = ExitStack()
        ar = scratch(phase, f"l{l}f")
        MIDh, MIDl = (ar(4096, F32R).rearrange("p (m t) -> p m t", m=8) for _ in range(2))
        OC = [ar(512) for _ in range(3)]
        oc_free = [None] * 3
        wup = ins[f"wup{l}"]

        nxt = ["wada1", "wada2"][l]
        still_to_do = len(adaq)
        ready = [None, ["c1", "c2"][l]]
        adaq += [ada_step(ins[nxt], i, ready, ["bada1", "bada2"][l], (cur[0] + 1) % 2) for i in range(48)]

        mid_free = None
        for third in range(3):
            ms = range(8 * third, min(8 * third + 8, 22))
            mid = []
            for m in ms:
                if m == 0:
                    (ba, pa), (bb, pb) = project2([wup[0], wup[22]], hk(T), T, hm)
                    background(still_to_do)
                    ada_columns()
                else:
                    ba, pa = project(wup[m], hk(T), T, hm)
                o = OC[m % 3][:, 0:T]
                wc = lambda c: par(f"fconv{l}", 3 * m + c, 3 * m + c + 1)
                a = A(partial(nc.scalar.activation, o, ba[:, 0:T], ACT.Copy, scale=wc(1)), pa, oc_free[m % 3])
                t = conv_taps(o, ba[:, 0:T], wc, len(streams), None, a, pa)
                give(ba, a, t)
                a = A(partial(nc.scalar.activation, o, o, ACT.Silu), t)
                if m:
                    bb, pb = project(wup[22 + m], hk(T), T, hm)
                t = D(partial(nc.vector.tensor_tensor, o, o, bb[:, 0:T], ALU.mult), a, pb)
                give(bb, t)
                h_, l_ = MIDh[:, m % 8, 0:T], MIDl[:, m % 8, 0:T]
                t = split_to(h_, l_, o, t, mid_free)
                oc_free[m % 3] = t
                mid.append((h_, l_, t))
            for m in range(8):
                b = take()
                w = load(ins[f"wdn{l}"][8 * third + m, :, 0:128 * len(ms)], 128 * len(ms))
                wh, wl = (v.rearrange("p (k m) -> p k m", m=128) for v in (w.hi, w.lo))
                for k in range(len(ms)):
                    p = mm3(b[:, 0:T], (wh[:, k, :], wl[:, k, :]), mid[k][0:2], k == 0, k == len(ms) - 1,
                            w.split, mid[k][2], *b.free)
                w.done = p
                x_ready = residual(b, m, 5, streams, p)
                background(1, 32)
            mid_free = P.last
        drain(32)
        fence()
        phase.close()
        cur[0] = (cur[0] + 1) % 2
    mods("n1g2", 1, 0)

    r = stats(lambda i: X[:, i, 0:256], 8, 0, 256, ones, 1024.0, x_ready)
    for k in range(8):
        t = D(partial(nc.vector.scalar_tensor_tensor, out=X[:, k, 0:256], in0=X[:, k, 0:256],
                                                    scalar=par("finalg", k, k + 1), in1=RSTD[:, 0:256],
                                                    op0=ALU.mult, op1=ALU.mult), r)
    x_ready = t

    fence()
    for lane in (P, A, D):
        lane.wait((s_c2, 16), (s_c, 16))
    merge = ExitStack()
    m_T, a_T = (v.rearrange("p (j t) -> p j t", j=4) for v in (XX[:, 0:1024], XX[:, 1024:2048]))
    ar = scratch(merge, "m")
    q_a = ar(1024).rearrange("p (j t) -> p j t", j=4)
    k_a = ar(512)
    v_t = ar(512).rearrange("p (b c) -> p b c", b=4)
    q_m = ar(1024).rearrange("p (j t) -> p j t", j=4)
    k_m = ar(2048).rearrange("p (j t) -> p j t", j=4)
    v_m = ar(2048).rearrange("p (b c) -> p b c", b=4)
    o_g = ar(1024).rearrange("p (j t) -> p j t", j=4)
    prob = [ar(512) for _ in range(3)]
    RB = [ar(512) for _ in range(2)]
    DDa = ar(768)
    DD = [DDa[:, 256 * i:256 * i + 256] for i in range(3)]
    PP = [ar(1024) for _ in range(2)]
    attT = [v[:, 0:512] for v in PP]
    rt = [SQ[2][:, 256 * i:256 * i + 256] for i in range(2)]
    hs = ar(256)
    tmp = [ar(256) for _ in range(2)]
    keep = [ar(512) for _ in range(2)]
    st = ar(64)
    cT = ar(32)

    hm = modulated(0, 0, [0, 1], x_ready, left=LEFT)
    low_on_pool[0] = 2
    w2 = ins["win2"]

    first = project2([w2[16], w2[17]], hk(256), 256, hm)

    w = load(ins["wg2"], 128)
    wvh, wvl = (v.rearrange("p (k m) -> p k m", k=8) for v in (w.hi, w.lo))
    ONE = DDa[0:4, 0:512]
    D(partial(nc.vector.memset, ONE, 1.0))
    spare = [v[:, i:i + 1, :].rearrange("p k t -> p (k t)") for v in (v_m, k_m) for i in range(4)]
    bias = lambda g: par("gbias", g, g + 1)[0:4, :]
    gate_rows = []

    def seq(v, half, d):
        s = v[:, 256:512] if half == 0 else v[:, 0:256]
        return s[:, ::-1] if d else s

    for g in range(4):
        b = take()
        for k in range(8):
            c = slice(4 * g, 4 * g + 4)
            p = mm3(b[0:4, :], (wvh[:, k, c], wvl[:, k, c]), (Hh[:, k, :], Hl[:, k, :]), k == 0, k == 7,
                    w.split, hm[k], *b.free)
        gate_rows.append((b, p))
    w.done = P.last
    for g in range(4):
        b, p = gate_rows[g]
        d = g // 2
        v = keep[d][0:4, :] if g % 2 else spare[4 * d][0:4, :]
        for half in range(2):
            t = D(partial(nc.vector.tensor_scalar, v[:, 256 * half:256 * half + 256], seq(b[0:4, :], half, d),
                          bias(g), None, ALU.add), p)
        give(b, t)
    dirs = [None, None]
    steps = []

    def recurrence(d):
        gi, t1_, t2_, c_n = (spare[4 * d + i][0:4, :] for i in range(4))
        gf = keep[d][0:4, :]
        mk = {}

        def one():
            a = A(partial(nc.scalar.activation, t1_, gf, ACT.Abs), mk["start"])
            mk["a"] = A(partial(nc.scalar.activation, t1_, t1_, ACT.Exp, scale=-1.0), a)

        def two():
            t = D(partial(nc.vector.tensor_scalar, t1_, t1_, 1.0, None, ALU.add), mk["a"])
            mk["a"] = A(partial(nc.scalar.activation, t1_, t1_, ACT.Ln), t)

        def three():
            t = D(partial(nc.vector.tensor_scalar, gf, gf, 0.0, None, ALU.min), mk["a"])
            t = D(partial(nc.vector.tensor_tensor, gf, gf, t1_, ALU.subtract), t)
            t = D(partial(nc.vector.tensor_tensor_scan, t2_, ONE, gf, 0.0, ALU.mult, ALU.add), t)
            t = D(partial(nc.vector.tensor_tensor, gi, gi, t2_, ALU.subtract), t)
            t = D(partial(nc.vector.tensor_tensor_scan, t1_, gi, gi, 0.0, ALU.max, ALU.max), t)
            mk["t"] = D(partial(nc.vector.tensor_tensor, t2_, t2_, t1_, ALU.add), t)

        def four_():
            mseg, eseg, t = t1_[:, 256:512], t2_[:, 256:512], mk["t"]
            D(partial(nc.vector.tensor_scalar, gf[:, 0:256], mseg[:, ::-1] if d else mseg, -1.0, None, ALU.mult), t)
            mk["a"] = A(partial(nc.scalar.activation, gf[:, 256:512], eseg[:, ::-1] if d else eseg, ACT.Exp,
                                scale=-1.0), t)
            D(partial(nc.vector.tensor_copy, c_n[:, 256:512], gi[:, 255::-1] if d else gi[:, 0:256]), t)
            mk["t"] = D(partial(nc.vector.tensor_copy, c_n[:, 0:256],
                                gi[:, 256:512][:, ::-1] if d else gi[:, 256:512]), t)

        def five():
            b = take()
            for tb in range(4):
                p = P(partial(nc.tensor.transpose, b[:, 4 * tb:4 * tb + 4], c_n[:, 128 * tb:128 * tb + 128],
                              eye[0:4, 0:4]), mk["t"], *b.free)
            t = D(partial(nc.vector.tensor_copy, cT[:, 16 * d:16 * d + 16], b[:, 0:16]), p)
            give(b, t)
            dirs[d] = (gf, mk["a"], t)

        mk["start"] = t
        return [one, two, three, four_, five]

    for x in zip(recurrence(0), recurrence(1)):
        steps.append(x)

    def head_norm_rope(dst, n, b, p, g, i):
        c = A(partial(nc.scalar.activation, dst[:, 0:n], b[:, 0:n], ACT.Copy), p)
        give(b, c)
        r = stats(lambda _: dst[:, 0:n], 1, 0, n, par("blk64"), 64.0, c)
        t = D(partial(nc.vector.scalar_tensor_tensor, out=dst[:, 0:n], in0=dst[:, 0:n], scalar=g, in1=RSTD[:, 0:n],
                                               op0=ALU.mult, op1=ALU.mult), r)

        def rest():
            b2 = take()
            p2 = mm(b2[:, 0:256], cst("perm2"), dst[:, 0:256], True, True, t, *b2.free)
            u = D(partial(nc.vector.tensor_tensor, rt[i], b2[:, 0:256], cst("sin2"), ALU.mult), p2, D.last,
                  sq_free[2])
            give(b2, u)
            u = D(partial(nc.vector.tensor_tensor, dst[:, 0:256], dst[:, 0:256], cst("cos2"), ALU.mult), u)
            sq_busy[2] = D(partial(nc.vector.tensor_tensor, dst[:, 0:256], dst[:, 0:256], rt[i], ALU.add), u)
            return sq_busy[2]
        return rest

    pend = []
    rests = []
    for c in range(4):
        b, p = first[c] if c < 2 else project(w2[16 + c], hk(256), 256, hm)
        pend.append((q_a[:, c, :], 256, b, p, par("qg")))
        if len(pend) > 1:
            rests.append(head_norm_rope(*pend.pop(0), c % 2))
        if len(rests) > 1:
            rests.pop(0)()
    b, p = project(w2[20], hk(512), 512, hm)
    pend.append((k_a, 512, b, p, par("kg")))
    rests.append(head_norm_rope(*pend.pop(0), 0))
    rests.pop(0)()
    rests.append(head_norm_rope(*pend.pop(0), 1))
    end = rows(w2[21], 4, hm, v_t, A, acopy_)
    rests.pop(0)()
    background(1, LEFT)
    vt_ok = end()
    qa_ok = ka_ok = rests.pop(0)()

    fill = []

    def proj_m(dst, tile, T, fn, key):
        def go():
            b, p = project(w2[tile], hk(T), T, hm)
            t = fn(dst, b[:, 0:T], p)
            give(b, t)
            marks[key] = t
        return go

    marks = {}

    def dcopy(dst, src, p):
        return D(partial(nc.vector.tensor_copy, dst, src), p)

    def acopy(dst, src, p):
        return A(partial(nc.scalar.activation, dst, src, ACT.Copy), p)

    for c in range(4):
        fill.append(proj_m(q_m[:, c, :], c, 256, dcopy, ("q", c)))
    for c in range(4):
        fill.append(proj_m(o_g[:, c, :], 12 + c, 256, acopy, ("o", c)))
    for c in range(4):
        fill.append(proj_m(k_m[:, c, :], 4 + c, 512, dcopy, ("k", c)))

    ends = []

    def rows_v(c):
        def go():
            end = rows(w2[8 + c], 4, hm, v_m[:, :, 128 * c:128 * c + 128], D, dcopy_)
            if ends:
                marks[("v", c - 1)] = ends.pop()()
            ends.append(end)
        return go

    for c in range(4):
        fill.append(rows_v(c))

    SC2 = 64 ** -0.5
    units = [(c, kv, qb) for c in range(4) for kv in range(2) for qb in range(2)]
    state = {}
    ring_free = {}
    sinkb = par("sink")

    def scores2(n):
        c, kv, qb = units[n]
        r = 64 * kv
        b = take()
        p = P(partial(nc.tensor.matmul, b[:, :], q_a[r:r + 64, c, 128 * qb:128 * qb + 128], k_a[r:r + 64, :],
                                 start=True, stop=True, tile_position=(r, 0)), qa_ok, ka_ok, *b.free)
        edge = b[:, 128:256] if qb == 0 else b[:, 0:128]
        t = D(partial(nc.vector.tensor_tensor, edge, edge, cst("win", 128 * qb, 128 * qb + 128), ALU.add), p)
        i = n % 3
        x0 = 8 * i
        mx, sm_, es = (st[:, x0 + z:x0 + z + 1] for z in range(3))
        h = c + 4 * kv
        sk = sinkb[:, h:h + 1]
        t = D(partial(nc.vector.tensor_reduce, mx, b[:, :], AX_X, ALU.max), t, ring_free.get(("st", i)))
        t = D(partial(nc.vector.scalar_tensor_tensor, out=mx, in0=mx, scalar=SC2, in1=sk, op0=ALU.mult, op1=ALU.max), t)
        t = D(partial(nc.vector.tensor_scalar, mx, mx, -1.0, None, ALU.mult), t)
        pr = prob[i]
        A(partial(nc.scalar.activation, pr, b[:, :], ACT.Exp, bias=mx, scale=SC2, accum_out=sm_), t,
          ring_free.get(("prob", i)))
        a = A(partial(nc.scalar.activation, es, sk, ACT.Exp, bias=mx), t)
        give(b, a)
        state[("e", n)] = a

    def normal2(n):
        i = n % 3
        sm_, es, rc = (st[:, 8 * i + z:8 * i + z + 1] for z in (1, 2, 3))
        pr = prob[i]
        t = D(partial(nc.vector.tensor_tensor, rc, sm_, es, ALU.add), state[("e", n)])
        t = D(partial(nc.vector.reciprocal, rc, rc), t)
        t = D(partial(nc.vector.tensor_scalar, pr, pr, rc, None, ALU.mult), t)
        ring_free[("st", i)] = t
        state[n] = t

    def turn2(n):
        c, kv, qb = units[n]
        b = take()
        i = n % 3
        for kc in range(4):
            p = P(partial(nc.tensor.transpose, b[:, 128 * kc:128 * kc + 128],
                                               prob[i][:, 128 * kc:128 * kc + 128], eye), state[n], *b.free)
        ring_free[("prob", i)] = p
        at = attT[n % 2]
        a = A(partial(nc.scalar.activation, at, b[:, :], ACT.Copy), p, ring_free.get(("attT", n % 2)))
        give(b, a)
        state[("t", n)] = a

    def apply2(n):
        c, kv, qb = units[n]
        at, a = attT[n % 2], state[("t", n)]
        b2 = take()
        r = 64 * kv
        for kc in range(4):
            p = mm(b2[r:r + 64, 0:128], v_t[:, kc, 64 * kv:64 * kv + 64], at[:, 128 * kc:128 * kc + 128],
                   kc == 0, kc == 3, a, vt_ok, *b2.free)
        ring_free[("attT", n % 2)] = p
        state[("o", n)] = b2, p

    def keep_a(n):
        c, kv, qb = units[n]
        r = 64 * kv
        b2, p = state[("o", n)]
        t = D(partial(nc.vector.tensor_copy, a_T[r:r + 64, c, 128 * qb:128 * qb + 128], b2[r:r + 64, 0:128]), p)
        give(b2, t)

    for n in range(2):
        scores2(n)
        normal2(n)
    for n in range(16):
        turn2(n)
        if n + 2 < 16:
            scores2(n + 2)
        if steps:
            for x in steps.pop(0):
                x()
        fill.pop(0)()
        background(1, LEFT)
        if n + 2 < 16:
            normal2(n + 2)
        if n:
            keep_a(n - 1)
        apply2(n)
    keep_a(15)
    marks[("v", 3)] = ends.pop()()
    for c in range(4):
        og_ok = A(partial(nc.scalar.activation, o_g[:, c, :], o_g[:, c, :], ACT.Sigmoid), marks[("o", c)])

    SM2 = 128 ** -0.5
    pp_free = [None, None]
    rb_free = [None, None]
    dd_free = [None] * 3

    def lstm_scores(h):
        sbk = [take(), take()]
        for tb in range(4):
            b = sbk[tb // 2]
            p = mm(b[:, 256 * (tb % 2):256 * (tb % 2) + 256], k_m[:, h, 128 * tb:128 * tb + 128], q_m[:, h, :],
                   True, True, marks[("k", h)], marks[("q", h)], *b.free)
        return sbk, p

    sbks = {0: lstm_scores(0)}
    nums = {}

    spread = []

    def row(h, d):
        rw, ra, ct = dirs[d]
        b = take()
        p = mm(b[:, :], cst("sel", 128 * h, 128 * h + 128)[0:4, :], rw, True, True, ra, ct, *b.free)
        a = A(partial(nc.scalar.activation, RB[d], b[:, :], ACT.Copy), p, rb_free[d])
        give(b, a)
        spread.append(a)

    def seen(d, tb):
        if tb >= 2:
            return 0, 256, None
        if tb == d:
            return 0, 256, 128 * tb
        return 128 * tb, 128 * tb + 128, 128 * tb

    def weigh(h, d):
        rw, ra, ct = dirs[d]
        sbk, ps_ = sbks[h]
        rb, a = RB[d], spread.pop(0)
        pp = PP[d]
        if d == 0 and h < 3:
            sbks[h + 1] = lstm_scores(h + 1)
        for tb in range(4):
            n = 8 * h + 4 * d + tb
            dd = DD[n % 3]
            cc = cT[:, 16 * d + 4 * tb + h:16 * d + 4 * tb + h + 1]
            lo, hi, _ = seen(d, tb)
            t = D(partial(nc.vector.tensor_scalar, dd[:, lo:hi], rb[:, lo:hi], cc, 0.0, ALU.add, ALU.min), a, ct,
                  dd_free[n % 3])
            exps.append((n, tb, A(partial(nc.scalar.activation, dd[:, lo:hi], dd[:, lo:hi], ACT.Exp), t)))
            if len(exps) > 1:
                t = times(h, d, pp, sbk, ps_, *exps.pop(0))
        t = times(h, d, pp, sbk, ps_, *exps.pop(0))
        if d == 1:
            for b_ in sbk:
                give(b_, t)
        return t

    exps = []

    def times(h, d, pp, sbk, ps_, n, tb, ax):
        dd = DD[n % 3]
        lo, hi, cut = seen(d, tb)
        o = pp[:, 256 * tb + lo:256 * tb + hi]
        s = sbk[tb // 2][:, 256 * (tb % 2) + lo:256 * (tb % 2) + hi]
        t = D(partial(nc.vector.scalar_tensor_tensor, out=o, in0=s, scalar=SM2, in1=dd[:, lo:hi], op0=ALU.mult,
                      op1=ALU.mult), ax, ps_, pp_free[d])
        dd_free[n % 3] = t
        if cut is not None:
            o = pp[:, 256 * tb + cut:256 * tb + cut + 128]
            mk = cst("cb" if d else "cf", 256 * tb + cut, 256 * tb + cut + 128)
            t = D(partial(nc.vector.tensor_tensor, o, o, mk, ALU.mult), t)
        return t

    def sums(h, d, t):
        b = take()
        for which, c0 in (("num", 0), ("den", 256)):
            for i, tb in enumerate((2, 3, 0, 1)):
                lo, hi, _ = seen(d, tb)
                lhs = v_m[:, tb, 128 * h:128 * h + 128] if which == "num" else ones
                p = mm(b[:, c0 + lo:c0 + hi], lhs, PP[d][:, 256 * tb + lo:256 * tb + hi], i == 0, i == 3, t,
                       marks[("v", h)], *b.free, skip=True)
        pp_free[d] = p
        nums[(h, d)] = b, p, A(partial(nc.scalar.activation, tmp[d], b[:, 256:512], ACT.Abs), p, tmp_free[d])

    tmp_free = [None, None]

    def divide(h, d):
        b, p, ab_ = nums[(h, d)]
        tm = tmp[d]
        t = D(partial(nc.vector.tensor_tensor, tm, tm, RB[d][:, 256:512], ALU.max), ab_)
        rb_free[d] = t
        t = D(partial(nc.vector.reciprocal, tm, tm), t)
        o = hs if d else m_T[:, h, :]
        t = D(partial(nc.vector.tensor_tensor, o, tm, b[:, 0:256], ALU.mult), t)
        tmp_free[d] = t
        give(b, t)
        if d:
            t = D(partial(nc.vector.tensor_tensor, m_T[:, h, :], m_T[:, h, :], hs, ALU.add), t)
        return t

    before = None
    row(0, 0)
    for h in range(4):
        for d in range(2):
            t = weigh(h, d)
            if before:
                divide(*before)
            if (h, d) != (3, 1):
                row(h + d, 1 - d)
            background(math.ceil((len(adaq) - LEFT) / (8 - 2 * h - d)), LEFT)
            sums(h, d, t)
            before = (h, d)
    t = divide(*before)
    low_on_pool[0] = 0
    first = project2([w2[22], w2[30]], hk(256), 256, hm)
    for z in range(2):
        r = stats(lambda _: m_T[:, 2 * z:2 * z + 2, :].rearrange("p j t -> p (j t)"), 1, 0, 512, ones, 128.0, t)
        for h in (2 * z, 2 * z + 1):
            m = m_T[:, h, :]
            u = D(partial(nc.vector.scalar_tensor_tensor, out=m, in0=m, scalar=par("mng", h, h + 1),
                          in1=RSTD[:, 256 * (h % 2):256 * (h % 2) + 256], op0=ALU.mult, op1=ALU.mult), r)
            D(partial(nc.vector.tensor_tensor, m, m, o_g[:, h, :], ALU.mult), u, og_ok)

    fence()
    merge.close()
    merge = ExitStack()
    ar = scratch(merge, "n")
    MG = ar(2048).rearrange("p (k t) -> p k t", k=8)
    gsb = [ar(256) for _ in range(4)]
    BRh, BRl, MGh, MGl = (ar(2048, F32R).rearrange("p (k t) -> p k t", k=8) for _ in range(4))
    br = []
    for k in range(8):
        src = m_T[:, k, :] if k < 4 else a_T[:, k - 4, :]
        br.append(split_to(BRh[:, k, :], BRl[:, k, :], src))
    g_free = [None] * 4
    mg = []
    for m in range(8):
        j = m % 2
        sg_ = []
        for z in range(2):
            b, p = first[z] if m == 0 else project(w2[22 + 8 * z + m], hk(256), 256, hm)
            gg = gsb[2 * j + z]
            a = A(partial(nc.scalar.activation, gg, b[:, 0:256], ACT.Sigmoid), p, g_free[2 * j + z])
            give(b, a)
            sg_.append((gg, a))
        w = load(ins["wbr2"][m])
        wh, wl = (v.rearrange("p (k m) -> p k m", k=8) for v in (w.hi, w.lo))
        b = take()
        for k in range(8):
            p = mm3(b[:, 256 * (k // 4):256 * (k // 4) + 256], (wh[:, k, :], wl[:, k, :]),
                    (BRh[:, k, :], BRl[:, k, :]), k % 4 == 0, k % 4 == 3, w.split, br[k], *b.free)
        w.done = p
        o = MG[:, m, :]
        t1_ = D(partial(nc.vector.tensor_tensor, o, sg_[0][0], b[:, 0:256], ALU.mult), p, sg_[0][1])
        t2_ = D(partial(nc.vector.tensor_tensor, sg_[1][0], sg_[1][0], b[:, 256:512], ALU.mult), sg_[1][1])
        give(b, t2_)
        t = D(partial(nc.vector.tensor_tensor, o, o, sg_[1][0], ALU.add), t1_, t2_)
        g_free[2 * j] = g_free[2 * j + 1] = t
        mg.append(split_to(MGh[:, m, :], MGl[:, m, :], o, t))
    for i in range(8):
        b, p = project(ins["wout2"][i], lambda k: (MGh[:, k, :], MGl[:, k, :]), 256, mg)
        x_ready = residual(b, i, 2, [0], p)

    HX = [t[:, :].rearrange("p (k t) -> p k t", k=8) for t in (HXh, HXl)]
    XP = XX[:, :].rearrange("p (k t) -> p k t", k=8)
    drain(LEFT)
    mods("n2g2", 4, 1)
    hm = modulated(1, 3, [0], x_ready, HX)
    wq, rhs = ins["wq2"], lambda k: (HX[0][:, k, :], HX[1][:, k, :])
    first = project2([wq[0], wq[1]], rhs, 256, hm)
    D(partial(nc.vector.tensor_copy, XP, X[:, :, 0:256]))
    fence()
    merge.close()
    early.close()
    late = ExitStack()
    GT = sb("G", 32768, at=late)
    WP = [[sb(f"W{z}{i}", 256, F32R, late)[:, :] for z in "hl"] for i in range(3)]
    TT = [sb(f"T{i}", 256, F32, late)[:, :] for i in range(3)]
    GG = GT[:, :].rearrange("p (a t) -> p a t", a=128)
    at = [64 * 256]

    def ar(n):
        at[0] += n
        assert at[0] <= 32768
        return GT[:, at[0] - n:at[0]]

    q_p = ar(4096).rearrange("p (j t) -> p j t", j=16)
    Sb = [ar(2048) for _ in range(2)]
    S2 = ar(2048)
    W1, W2 = ar(2048), ar(2048)
    top = ar(256).rearrange("p (j k) -> p j k", k=16)
    tid = ar(256).rearrange("p (j k) -> p j k", k=16)
    tidf = ar(256)
    ctop = ar(128)
    cpos = ar(128)
    ca, cb_ = ar(128), ar(128)
    gsm = ar(128)
    gs = ar(16)
    idA, idB = ar(128), ar(128)
    drain()
    for c in range(16):
        b, p = first[c] if c < 2 else project(wq[c], rhs, 256, hm)
        a = A(partial(nc.scalar.activation, q_p[:, c, :], b[:, 0:256], ACT.Copy), p)
        give(b, a)
    for half in range(2):
        wk = load(ins["keys2"][half], TILE, False)
        for tb in range(2):
            for q4 in (2 * half, 2 * half + 1):
                b = take()
                for z in range(4):
                    c = 4 * q4 + z
                    p = mm(b[:, 128 * z:128 * z + 128], q_p[:, c, 128 * tb:128 * tb + 128],
                           wk.raw[:, 128 * (c % 8):128 * (c % 8) + 128], True, True, a, wk.ready, *b.free)
                sv = Sb[tb][:, 512 * q4:512 * q4 + 512]
                ac = A(partial(nc.scalar.activation, sv, b[:, :], ACT.Copy), p)
                give(b, ac)
        wk.done = wk.freed = p
    iAT, iBT, gT = TT
    NEG = -3.0e38
    ab = [take() for _ in range(3)]
    picked = [None]

    def up(a_):
        w = load(ins["ut2"][a_])
        wh, wl = (v.rearrange("p (k m) -> p k m", k=8) for v in (w.hi, w.lo))
        b = ab[a_ % 3]
        for k in range(8):
            p = mm3(b[:, 0:256], (wh[:, k, :], wl[:, k, :]), (HX[0][:, k, :], HX[1][:, k, :]), k == 0, k == 7,
                    w.split, *b.free)
        w.done = p
        t = A(partial(nc.scalar.activation, GG[:, a_, :], b[:, 0:256], ACT.Gelu_apprx_tanh), p, picked[0])
        b.release(t)

    s_done = ac
    low_on_pool[0] = 1

    def pick(tb):
        S = Sb[tb]
        free_s = s_done
        t = None
        for c in range(16):
            sv = S[:, 128 * c:128 * c + 128]
            s2 = S2[:, 128 * c:128 * c + 128]
            v0, v1 = top[:, c, 0:8], top[:, c, 8:16]
            i0, i1 = tid[:, c, 0:8].bitcast(U32), tid[:, c, 8:16].bitcast(U32)
            t = D(partial(nc.vector.max, v0, sv), free_s)
            D(partial(nc.vector.max_index, i0, v0, sv), t)
            t = D(partial(nc.vector.match_replace, s2, v0, sv, NEG), t)
            t = D(partial(nc.vector.max, v1, s2), t)
            t = D(partial(nc.vector.max_index, i1, v1, s2), t)
        ti = tid.rearrange("p j k -> p (j k)").bitcast(U32)
        t_ids = D(partial(nc.vector.tensor_copy, tidf, ti), t)
        for h in range(8):
            o = W1[:, 256 * h:256 * h + 256].rearrange("p (a b) -> p a b", b=16)
            s1b = top[:, 2 * h, :].rearrange("p (a o) -> p a o", o=1).to_broadcast([128, 16, 16])
            s2b = top[:, 2 * h + 1, :].rearrange("p (o b) -> p o b", o=1).to_broadcast([128, 16, 16])
            t = D(partial(nc.vector.tensor_tensor, o, s1b, s2b, ALU.add), t)
            sv, s2 = W1[:, 256 * h:256 * h + 256], W2[:, 256 * h:256 * h + 256]
            v0, v1 = ctop[:, 16 * h:16 * h + 8], ctop[:, 16 * h + 8:16 * h + 16]
            i0, i1 = (cpos[:, 16 * h + 8 * z:16 * h + 8 * z + 8].bitcast(U32) for z in range(2))
            t = D(partial(nc.vector.max, v0, sv), t)
            D(partial(nc.vector.max_index, i0, v0, sv), t)
            t = D(partial(nc.vector.match_replace, s2, v0, sv, NEG), t)
            t = D(partial(nc.vector.max, v1, s2), t)
            t = D(partial(nc.vector.max_index, i1, v1, s2), t)
        c3 = ctop.rearrange("p (h k) -> p h k", k=16)
        g3 = gsm.rearrange("p (h k) -> p h k", k=16)
        tg = D(partial(nc.vector.tensor_tensor, g3, c3, c3[:, :, 0:1].to_broadcast([128, 8, 16]), ALU.subtract), t)
        ag = A(partial(nc.scalar.activation, gsm, gsm, ACT.Exp), tg)
        cp = cpos.bitcast(U32)
        cau, cbu = ca.bitcast(U32), cb_.bitcast(U32)
        t = D(partial(nc.vector.tensor_scalar, cau, cp, 4, None, ALU.logical_shift_right), t)
        t1_ = D(partial(nc.vector.tensor_scalar, cbu, cp, 15, None, ALU.bitwise_and), t)
        fa, fb = W2[:, 0:128], W2[:, 128:256]
        t = D(partial(nc.vector.tensor_copy, fa, cau), t1_)
        t = D(partial(nc.vector.tensor_copy, fb, cbu), t)
        for z, f, idx in ((0, fa, idA), (1, fb, idB)):
            e3 = W1.rearrange("p (a j) -> p a j", j=16)
            e4 = W1.rearrange("p (h k j) -> p h k j", k=16, j=16)
            fo = f.rearrange("p (a o) -> p a o", o=1).to_broadcast([128, 128, 16])
            io = iota[:, 0:16].rearrange("p (o j) -> p o j", o=1).to_broadcast([128, 128, 16])
            t = D(partial(nc.vector.tensor_tensor, e3, fo, io, ALU.is_equal), t, t_ids)
            src = tidf.rearrange("p (h z j) -> p h z j", z=2, j=16)[:, :, z:z + 1, :].to_broadcast([128, 8, 16, 16])
            t = D(partial(nc.vector.tensor_tensor, e4, e4, src, ALU.mult), t)
            t = D(partial(nc.vector.tensor_reduce, idx, e3, AX_X, ALU.add), t)
        tg = D(partial(nc.vector.tensor_reduce, gs[:, 0:8], g3, AX_X, ALU.add), ag)
        tg = D(partial(nc.vector.reciprocal, gs[:, 8:16], gs[:, 0:8]), tg)
        tg = D(partial(nc.vector.tensor_tensor, g3, g3, gs[:, 8:16].rearrange("p (h o) -> p h o", o=1)
                                         .to_broadcast([128, 8, 16]), ALU.mult), tg)
        b = take()
        for z, v in enumerate((idA, idB, gsm)):
            p = P(partial(nc.tensor.transpose, b[:, 128 * z:128 * z + 128], v, eye), t, tg, *b.free)
        for z, v in enumerate((iAT, iBT, gT)):
            o = v[:, 128 * tb:128 * tb + 128]
            t = D(partial(nc.vector.tensor_copy, o, b[:, 128 * z:128 * z + 128]), p)
        give(b, t)

    for a_ in range(32):
        up(a_)
    pick(0)
    for a_ in range(32, 64):
        up(a_)
    pick(1)
    picked[0] = D.last
    for a_ in range(64, 128):
        if a_ == 128 - AHEAD:
            low_on_pool[0] = 0
        up(a_)
    acts_done = A.last
    for b in ab:
        give(b, *b.free)

    n_before_lent = [len(asked)]
    fence()
    oh = [(RAW[:, 1024 * i:1024 * i + 512], RAW[:, 1024 * i + 512:1024 * i + 1024]) for i in range(4)]
    oh_free = [None] * 4
    gq = []

    def onto(q, b, p):
        dst = GG[:, :, 4 * q:4 * q + 4].rearrange("p a t -> p t a")
        t = D(partial(nc.vector.tensor_tensor, dst, dst, b[:, :].rearrange("p (t a) -> p t a", t=4), ALU.mult),
              p, acts_done)
        give(b, t)

    for q in range(64):
        b = take()
        oa, ob = oh[q % 4]
        for y in range(3):
            tk = 4 * q + y
            aa = A(partial(nc.scalar.activation, oa[:, 128 * y:128 * y + 128], iota, ACT.Abs, scale=-1.0,
                           bias=iAT[:, tk:tk + 1]), oh_free[q % 4])
        aa = A(partial(nc.scalar.activation, oa[:, 0:384], oa[:, 0:384], ACT.Relu, scale=-1.0,
                       bias=ones[:, 0:1]), aa)
        tk = 4 * q + 3
        G(partial(nc.gpsimd.tensor_scalar, oa[:, 384:512], iota, iAT[:, tk:tk + 1], None, ALU.is_equal),
          oh_free[q % 4])
        ga = G(partial(nc.gpsimd.tensor_scalar, ob[:, 384:512], iota, iBT[:, tk:tk + 1], gT[:, tk:tk + 1],
                       ALU.is_equal, ALU.mult), oh_free[q % 4])
        for y in range(3):
            tk = 4 * q + y
            t = D(partial(nc.vector.tensor_scalar, ob[:, 128 * y:128 * y + 128], iota, iBT[:, tk:tk + 1],
                          gT[:, tk:tk + 1], ALU.is_equal, ALU.mult), oh_free[q % 4])
        for y in range(4):
            c = slice(128 * y, 128 * y + 128)
            p = mm(b[:, c], ob[:, c], oa[:, c], True, True, t, ga, aa, *b.free)
        oh_free[q % 4] = p
        gq.append((q, b, p))
        if q:
            onto(*gq.pop(0))
    onto(*gq.pop(0))
    lent = [P.last, D.last, G.last, A.last]
    yb = [take() for _ in range(4)]
    act_free = [None] * 3
    wact = {}

    def part(a_):
        wact[a_] = split_to(WP[a_ % 3][0], WP[a_ % 3][1], GG[:, a_, :], lent[1], act_free[a_ % 3])

    def down(a_):
        w = load(ins["v2"][a_])
        for m in range(8):
            b = yb[m // 2]
            c = slice(128 * m, 128 * m + 128)
            mm3(b[:, 256 * (m % 2):256 * (m % 2) + 256], (w.hi[:, c], w.lo[:, c]), WP[a_ % 3],
                a_ == 0 and m % 2 == 0, a_ == 127, w.split, wact[a_], *b.free, skip=True, inc=m == 7)
        w.done = P.last
        act_free[a_ % 3] = P.last

    part(0)
    for a_ in range(128):
        if a_ < 127:
            part(a_ + 1)
        down(a_)
    pl = P.last
    outs = [GT[:, 1024 * i:1024 * i + 1024] for i in range(2)]
    for m in range(8):
        i = yb[m // 2][:, 256 * (m % 2):256 * (m % 2) + 256]
        o = XP[:, m, :]
        t = D(partial(nc.vector.scalar_tensor_tensor, out=o, in0=i, scalar=adac(5, m, 0), in1=o,
                                                              op0=ALU.mult, op1=ALU.add), pl)
    out_marks = []
    for tb in range(2):
        for half in range(2):
            b = take()
            for z in range(4):
                m = 4 * half + z
                p = P(partial(nc.tensor.transpose, b[:, 128 * z:128 * z + 128],
                                                                 XP[:, m, 128 * tb:128 * tb + 128], eye),
                      t, *b.free)
            o = outs[tb][:, 512 * half:512 * half + 512]
            a = A(partial(nc.scalar.activation, o, b[:, :], ACT.Copy), p)
            give(b, a)
        out_marks.append(a)

    late.close()
    if not order:
        return asked

    block = ctx.enter_context(nc.Block())

    @block.sync
    def _(e):
        e.dma_start(PT[:, :], ins["par"]).then_inc(s_in, 16)
        first_up = n_before_lent[0]
        todo = [(x2_free, X[:, :, 256:512], ins["ctx2t"].rearrange("p (k t) -> p k t", k=8), s_c2),
                (consts_free[0], CT[:, 0:NCS2], ins["cs2"], s_c)]
        todo.sort(key=lambda x: x[0][0][1])
        for i, t in enumerate(tiles):
            if i == 3:
                e.dma_start(XT[:, :], ins["xt"]).then_inc(s_x, 16)
            if i == 18:
                e.dma_start(CT[:, :], ins["cst"]).then_inc(s_k, 16)
            if i >= NRAW:
                last = tiles[i - NRAW]
                frees = [last.freed]
                while todo and tiles[i - 1].done and (tiles[i - NRAW].done[1] > todo[0][0][0][1]):
                    for m in todo[0][0]:
                        e.wait_ge(m[0], m[1])
                    e.dma_start(todo[0][1], todo[0][2]).then_inc(todo[0][3], 16)
                    todo.pop(0)
                if first_up + AHEAD <= i < first_up + AHEAD + NRAW:
                    frees += lent
                for m in frees:
                    e.wait_ge(m[0], m[1])
            e.dma_start(t.raw, t.src).then_inc(s_ring[i % NRAW], 16)
        assert not todo
        for tb in range(2):
            e.wait_ge(out_marks[tb][0], out_marks[tb][1])
            e.dma_start(out[0, 128 * tb:128 * tb + 128, :], outs[tb]).then_inc(s_out, 16)
        e.wait_ge(s_out, 32)

    @block.tensor
    def _(e):
        P.play(e)

    @block.vector
    def _(e):
        D.play(e)

    @block.scalar
    def _(e):
        A.play(e)

    @block.gpsimd
    def _(e):
        G.play(e)


def _cols(v):
    return np.ascontiguousarray(v.reshape(-1, 128).T)


def _tiles(w, cols=128):
    k, n = w.shape
    return np.ascontiguousarray(w.reshape(k // 128, 128, n // cols, cols).transpose(2, 1, 0, 3)
                                .reshape(n // cols, 128, (k // 128) * cols))


def _constants():
    c, c2 = np.zeros((128, NCST), np.float32), np.zeros((128, NCS2), np.float32)

    def put(name, v):
        at, n = (CST if name in CST else CS2)[name]
        (c if name in CST else c2)[:v.shape[0], at:at + n] = v.reshape(v.shape[0], n)

    p = np.arange(128)
    t = np.arange(256)
    row, col = (t // 64).astype(np.float32), (t % 64).astype(np.float32)
    d = p % 32
    j = d % 16
    perm = np.zeros((128, 128), np.float32)
    perm[np.where(j < 8, p + 8, p - 8), p] = np.where(j < 8, -1.0, 1.0)
    put("perm1", perm)
    inv = (np.float32(10000.0) ** (-np.arange(0, 16, 2, dtype=np.float32) / np.float32(16))).astype(np.float32)
    ang = np.where((d // 16 == 0)[:, None], row[None, :], col[None, :]) * inv[j % 8][:, None]
    put("cos1", np.cos(ang.astype(np.float32)))
    put("sin1", np.sin(ang.astype(np.float32)))
    d = p % 64
    perm = np.zeros((128, 128), np.float32)
    perm[np.where(d < 32, p + 32, p - 32), p] = np.where(d < 32, -1.0, 1.0)
    put("perm2", perm)
    inv = (np.float32(10000.0) ** (-np.arange(16, dtype=np.float32) / np.float32(16))).astype(np.float32)
    i = d % 32
    ang = np.where((i < 16)[:, None], row[None, :], col[None, :]) * inv[i % 16][:, None]
    put("cos2", np.cos(ang.astype(np.float32)))
    put("sin2", np.sin(ang.astype(np.float32)))
    n = np.arange(256)
    th = 2 * np.pi * ((n[:, None] * n[None, :]) % 256) / 256
    cs = np.concatenate([np.cos(th), np.sin(th)], axis=1) / 16
    put("dftn", cs.reshape(2, 128, 512).transpose(1, 0, 2).reshape(128, 1024).astype(np.float32))
    n = np.arange(64)
    th = 2 * np.pi * ((n[:, None] * n[None, :]) % 64) / 64
    z = np.zeros((128, 128))
    z[:64, :64] = z[64:, 64:] = np.cos(th) / 8
    put("cd", z.astype(np.float32))
    z = np.zeros((128, 128))
    z[:64, :64] = z[64:, 64:] = -np.sin(th) / 8
    put("sd", z.astype(np.float32))
    s = 128 * np.arange(2)[None, :, None] + p[:, None, None]
    put("cf", (t[None, None, :] >= s).astype(np.float32).reshape(128, 512))
    put("cb", (t[None, None, :] <= s).astype(np.float32).reshape(128, 512))
    q, k = p[:, None], p[None, :]
    win = np.concatenate([np.where(k + 128 - q <= 128, 0.0, -1e30), np.where(q + 128 - k <= 128, 0.0, -1e30)], axis=1)
    put("win", win.astype(np.float32))
    sel = np.zeros((4, 4, 128), np.float32)
    for r in range(4):
        sel[r, r, :] = 1.0
    put("sel", sel.reshape(4, 512))
    return c, c2


def kernel(**inputs):
    import concourse.bacc as _bacc
    from concourse.bass_utils import run_bass_kernel_spmd as _run

    v = {k: np.asarray(a) for k, a in inputs.items()}
    pa = np.zeros((128, NPAR), np.float32)

    def put(name, a):
        at, n = PAR[name]
        pa[:a.shape[0], at:at + n] = a.reshape(a.shape[0], n)

    put("eye", np.eye(128, dtype=np.float32))
    put("ones", np.ones((128, 128), np.float32))
    p_ = np.arange(128)
    put("blk64", (p_[:, None] // 64 == p_[None, :] // 64).astype(np.float32))
    put("sum2", np.array([[1, 0], [1, 0], [0, 1], [0, 1]], np.float32))
    put("iota", np.tile(np.arange(128, dtype=np.float32), (128, 1)))
    put("c1", np.stack([_cols(v["c"][0]), _cols(v["c_ctx"])], axis=2))
    put("c2", np.stack([_cols(v["c_2"][0]), _cols(v["c_ctx_2"])], axis=2))
    put("finalg", _cols(v["final_g"]))
    for l in range(DEPTH):
        put(f"bada{l}", _cols(v["b_ada"][l]))
        put(f"n1g{l}", _cols(v["norm1_g"][l]))
        put(f"n2g{l}", _cols(v["norm2_g"][l]))
        put(f"sconv{l}", v["sconv_w"][l].reshape(3, 2, 128).transpose(2, 1, 0))
        put(f"subln{l}", np.concatenate([v["subln_g"][l]] * 2)[:, None])
        put(f"fconv{l}", v["ffn_conv_w"][l].reshape(3, 22, 128).transpose(2, 1, 0))
        put(f"lam{l}", np.stack([v[n][l] for n in ("lambda_q1", "lambda_q2", "lambda_k1", "lambda_k2")], axis=1))
    put("bada2", _cols(v["b_ada_2"][0]))
    put("n1g2", _cols(v["norm_mix_g_2"][0]))
    put("n2g2", _cols(v["norm_ffn_g_2"][0]))
    put("gbias", v["b_mgates_2"][0].reshape(4, 4).T)
    put("mng", _cols(v["mlstm_norm_g_2"][0]))
    put("qg", np.concatenate([v["attn_q_norm_g_2"][0]] * 2)[:, None])
    put("kg", np.concatenate([v["attn_k_norm_g_2"][0]] * 2)[:, None])
    put("sink", np.tile(v["attn_sink_2"][0], (128, 1)))

    def toks(a):
        return a.reshape(256, 8, 128).transpose(2, 1, 0)

    c1, c2 = _constants()
    at, n = CST["ws"]
    c1[:, at:at + n] = v["gmlp_ws"].transpose(3, 0, 1, 2).reshape(128, 1024)
    at, n = CST["bs"]
    c1[:, at:at + n] = np.repeat(v["gmlp_bs"].reshape(2, 2, 2, 1, 128), 64, axis=3).reshape(2, 2, 128, 128)\
        .transpose(2, 0, 1, 3).reshape(128, 512)
    arr = {"par": pa, "cst": c1, "cs2": c2}
    arr["xt"] = np.concatenate([toks(v["x"][0]), toks(v["ctx"][0])], axis=2).reshape(128, 4096)
    arr["ctx2t"] = toks(v["ctx_2"][0]).reshape(128, 2048)
    for l in range(DEPTH):
        arr[f"wada{l}"] = _tiles(v["w_ada"][l])
        arr[f"win{l}"] = _tiles(v["w_in"][l])
        arr[f"wout{l}"] = _tiles(v["w_out"][l])
        arr[f"wup{l}"] = _tiles(v["ffn_w_up"][l])
        wd = np.zeros((3072, 1024), np.float32)
        wd[:2816] = v["ffn_w_down"][l]
        arr[f"wdn{l}"] = wd.reshape(3, 8, 128, 8, 128).transpose(0, 3, 2, 1, 4).reshape(24, 128, 1024)
    arr["wada2"] = _tiles(v["w_ada_2"][0])
    w = v["w_in_2"][0]
    qo = np.concatenate([np.arange(64 * h, 64 * h + 64) for c in range(4) for h in (c, c + 4)])
    arr["win2"] = _tiles(np.concatenate([w[:, 0:2048], w[:, 2064:2576][:, qo], w[:, 2576:]], axis=1))
    arr["wg2"] = w[:, 2048:2064].reshape(8, 128, 16).transpose(1, 0, 2).reshape(128, 128)
    arr["wbr2"] = _tiles(np.concatenate([v["w_branch_m_2"][0], v["w_branch_a_2"][0][qo]], axis=0))
    arr["wout2"] = _tiles(v["w_out_2"][0])
    arr["wq2"] = _tiles(v["peer_w_query_2"][0])
    arr["keys2"] = v["peer_sub_keys_2"][0].reshape(2, 8, 128, 128).transpose(0, 3, 1, 2).reshape(2, 128, 1024)
    arr["ut2"] = np.ascontiguousarray(v["peer_u_2"][0].reshape(128, 128, 8, 128).transpose(0, 3, 2, 1)
                                      .reshape(128, 128, 1024))
    arr["v2"] = np.ascontiguousarray(v["peer_v_2"][0].reshape(128, 128, 1024))

    nc = _bacc.Bacc("TRN2", target_bir_lowering=False, num_devices=1)
    feeds, args = {}, {}
    for name, a in arr.items():
        a = np.ascontiguousarray(a)
        feeds[f"in_{name}"] = a
        args[name] = nc.dram_tensor(f"in_{name}", a.shape, mybir.dt.from_np(a.dtype), kind="ExternalInput").ap()
    out = nc.dram_tensor("out_0", (1, 256, 1024), F32, kind="ExternalOutput").ap()
    build(nc, args, out)
    r = _run(nc, [feeds], core_ids=[0])
    return r.results[0]["out_0"]
```
